# Optimizing a Trainium2 kernel written in Bass

```python
import math
import jax, jax.numpy as jnp
from jax import lax
import numpy as np

D_MODEL = 1024
BATCH = 1
SEQ = 1024
DEPTH = 1
DEC_BATCH = 1
DEC_SEQ = 64
PAST_LEN = 256

CHUNK = 64
MIX_WIDTH = D_MODEL
S5_WIDTH = MIX_WIDTH // 2
S5_GROUP = 16
S5_GROUPS = S5_WIDTH // S5_GROUP
S5_STATE = 64
GDN_WIDTH = MIX_WIDTH - S5_WIDTH
GDN_HEAD_DIM = 128
GDN_HEADS = GDN_WIDTH // GDN_HEAD_DIM
CONV_WIDTH = 4
CONV_CH = 3 * GDN_WIDTH
D_FF = -(-8 * D_MODEL // (3 * 256)) * 256
OFF_Q = S5_WIDTH
OFF_K = OFF_Q + GDN_WIDTH
OFF_V = OFF_K + GDN_WIDTH
OFF_Z = OFF_V + GDN_WIDTH
OFF_B = OFF_Z + GDN_WIDTH
OFF_A = OFF_B + GDN_HEADS
IN_COLS = OFF_A + GDN_HEADS
SPLITS = (OFF_Q, OFF_K, OFF_V, OFF_Z, OFF_B, OFF_A)
ALPHA = (2 * DEPTH) ** 0.25
BETA_INIT = (8 * DEPTH) ** -0.25
LN_EPS = 1e-5
RMS_EPS = 1e-6

kernel_name = 'hymba_s5_gdn_deepnorm_adaln_stream_step'

F32 = jnp.float32

def layer_norm(x, g=None, b=None):
    xf = x.astype(F32)
    mu = jnp.mean(xf, -1, keepdims=True)
    var = jnp.mean(jnp.square(xf - mu), -1, keepdims=True)
    y = (xf - mu) * lax.rsqrt(var + LN_EPS)
    if g is not None:
        y = y * g.astype(F32) + b.astype(F32)
    return y.astype(x.dtype)

def l2norm(t):
    return t * lax.rsqrt(jnp.sum(t * t, -1, keepdims=True) + RMS_EPS)

def causal_conv(x, buf, w):
    L = x.shape[1]
    xp = jnp.concatenate([buf.astype(x.dtype), x], axis=1)
    y = sum(xp[:, j:j + L] * w[j] for j in range(CONV_WIDTH))
    return y, xp[:, -(CONV_WIDTH - 1):]

def s5_mixer(u, h0_re, h0_im, a_re, a_im, log_dt, b_re, b_im, c_re, c_im, d_skip, w_glu):
    Bsz, L, _ = u.shape
    uf = u.astype(F32).reshape(Bsz, L, S5_GROUPS, S5_GROUP)
    a_re = a_re.astype(F32)
    a_im = a_im.astype(F32)
    dt = jnp.exp(log_dt.astype(F32))[:, None]
    mag = jnp.exp(a_re * dt)
    ab_re, ab_im = mag * jnp.cos(a_im * dt), mag * jnp.sin(a_im * dt)
    den = a_re * a_re + a_im * a_im
    num_re, num_im = ab_re - 1.0, ab_im
    f_re = (num_re * a_re + num_im * a_im) / den
    f_im = (num_im * a_re - num_re * a_im) / den
    bu_re = jnp.einsum('blgj,gpj->blgp', uf, b_re.astype(F32))
    bu_im = jnp.einsum('blgj,gpj->blgp', uf, b_im.astype(F32))
    x_re = f_re * bu_re - f_im * bu_im
    x_im = f_re * bu_im + f_im * bu_re
    h0_re = h0_re.astype(F32)
    h0_im = h0_im.astype(F32)
    x_re = x_re.at[:, 0].add(ab_re * h0_re - ab_im * h0_im)
    x_im = x_im.at[:, 0].add(ab_re * h0_im + ab_im * h0_re)
    A_re = jnp.broadcast_to(ab_re, x_re.shape)
    A_im = jnp.broadcast_to(ab_im, x_re.shape)

    def combine(e1, e2):
        a1r, a1i, b1r, b1i = e1
        a2r, a2i, b2r, b2i = e2
        return (a1r * a2r - a1i * a2i,
                a1r * a2i + a1i * a2r,
                a2r * b1r - a2i * b1i + b2r,
                a2r * b1i + a2i * b1r + b2i)

    _, _, h_re, h_im = lax.associative_scan(combine, (A_re, A_im, x_re, x_im), axis=1)
    y = (jnp.einsum('blgp,gjp->blgj', h_re, c_re.astype(F32))
         - jnp.einsum('blgp,gjp->blgj', h_im, c_im.astype(F32))
         + d_skip.astype(F32).reshape(S5_GROUPS, S5_GROUP) * uf)
    y = jax.nn.gelu(y.reshape(Bsz, L, S5_WIDTH))
    za, zb = jnp.split(y @ w_glu.astype(F32), 2, axis=-1)
    return za * jax.nn.sigmoid(zb), h_re[:, -1], h_im[:, -1]

def chunk_gated_delta(q, k, v, g, beta, s0):
    Bsz, H, L, Dh = q.shape
    C = min(CHUNK, L)
    N = L // C
    q, k, v = (t.reshape(Bsz, H, N, C, Dh) for t in (q, k, v))
    g, beta = (t.reshape(Bsz, H, N, C) for t in (g, beta))
    decay = jnp.cumsum(g, axis=-1)
    causal = jnp.tril(jnp.ones((C, C), bool))
    strict = jnp.tril(jnp.ones((C, C), bool), -1)
    diff = decay[..., :, None] - decay[..., None, :]
    dmask = jnp.exp(jnp.where(causal, diff, -jnp.inf))
    k_beta = k * beta[..., None]
    v_beta = v * beta[..., None]
    A = jnp.where(strict, jnp.einsum('bhnid,bhnjd->bhnij', k_beta, k) * dmask, 0.0)
    eye = jnp.eye(C, dtype=F32)
    T = lax.linalg.triangular_solve(eye + A, jnp.broadcast_to(eye, A.shape),
                                    left_side=True, lower=True)
    u = T @ v_beta
    w = T @ (k_beta * jnp.exp(decay)[..., None])
    qk = jnp.einsum('bhnid,bhnjd->bhnij', q, k) * dmask
    q_dec = q * jnp.exp(decay)[..., None]
    k_dec = k * jnp.exp(decay[..., -1:] - decay)[..., None]
    g_last = jnp.exp(decay[..., -1])

    def step(S, inp):
        u_n, w_n, qk_n, qd_n, kd_n, gl_n = inp
        v_new = u_n - w_n @ S
        o_n = qd_n @ S + qk_n @ v_new
        S = S * gl_n[..., None, None] + jnp.einsum('bhck,bhcv->bhkv', kd_n, v_new)
        return S, o_n

    xs = tuple(jnp.moveaxis(t, 2, 0) for t in (u, w, qk, q_dec, k_dec, g_last))
    S, o = lax.scan(step, s0, xs)
    return jnp.moveaxis(o, 0, 2).reshape(Bsz, H, L, Dh), S

def gdn_mixer(q, k, v, z, b_raw, a_raw, s0, conv_buf, conv_w, a_log, dt_bias, norm_g):
    Bsz, L, _ = q.shape
    qkv, new_buf = causal_conv(jnp.concatenate([q, k, v], -1), conv_buf, conv_w)
    qkv = jax.nn.silu(qkv).astype(F32)
    heads = lambda t: t.reshape(Bsz, L, GDN_HEADS, GDN_HEAD_DIM).transpose(0, 2, 1, 3)
    qh, kh, vh = (heads(t) for t in jnp.split(qkv, 3, axis=-1))
    qh = l2norm(qh) * GDN_HEAD_DIM ** -0.5
    kh = l2norm(kh)
    beta = jax.nn.sigmoid(b_raw.astype(F32)).transpose(0, 2, 1)
    g = -jnp.exp(a_log.astype(F32)) * jax.nn.softplus(a_raw.astype(F32) + dt_bias.astype(F32))
    o, s_new = chunk_gated_delta(qh, kh, vh, g.transpose(0, 2, 1), beta, s0.astype(F32))
    o = o.transpose(0, 2, 1, 3)
    o = o * lax.rsqrt(jnp.mean(o * o, -1, keepdims=True) + RMS_EPS) * norm_g.astype(F32)
    o = o * jax.nn.silu(z.astype(F32)).reshape(Bsz, L, GDN_HEADS, GDN_HEAD_DIM)
    return o.reshape(Bsz, L, GDN_WIDTH), s_new, new_buf

def trunk_layer(x, c, h_re, h_im, s_gdn, conv_buf,
                w_ada, b_ada, w_in, s5_a_re, s5_a_im, s5_log_dt, s5_b_re, s5_b_im,
                s5_c_re, s5_c_im, s5_d, w_s5_glu, gdn_conv_w, gdn_a_log, gdn_dt_bias,
                gdn_norm_g, w_out, ln1_g, ln1_b, w_ffn_up, w_ffn_down, ln2_g, ln2_b):
    mod = (jax.nn.silu(c) @ w_ada + b_ada)[:, None, :]
    sh1, sc1, g1, sh2, sc2, g2 = jnp.split(mod, 6, axis=-1)
    h = layer_norm(x) * (1 + sc1) + sh1
    u, q, k, v, z, b_raw, a_raw = jnp.split(h @ w_in, SPLITS, axis=-1)
    y_a, h_re, h_im = s5_mixer(u, h_re, h_im, s5_a_re, s5_a_im, s5_log_dt, s5_b_re, s5_b_im,
                               s5_c_re, s5_c_im, s5_d, w_s5_glu)
    y_b, s_gdn, conv_buf = gdn_mixer(q, k, v, z, b_raw, a_raw, s_gdn, conv_buf, gdn_conv_w,
                                     gdn_a_log, gdn_dt_bias, gdn_norm_g)
    mix = jnp.concatenate([y_a.astype(x.dtype), y_b.astype(x.dtype)], -1) @ w_out
    x = layer_norm(ALPHA * x + (1 + g1) * mix, ln1_g, ln1_b)
    h = layer_norm(x) * (1 + sc2) + sh2
    gate, up = jnp.split(h @ w_ffn_up, 2, axis=-1)
    ffn = (jax.nn.silu(gate) * up) @ w_ffn_down
    x = layer_norm(ALPHA * x + (1 + g2) * ffn, ln2_g, ln2_b)
    return x, h_re, h_im, s_gdn, conv_buf

def setup_inputs(seed: int = 0) -> dict:
    key = jax.random.key(seed)
    ks = jax.random.split(key, 32)
    nrm = lambda k, shape, s: s * jax.random.normal(k, shape, F32)
    G, P, J, H, Dh = S5_GROUPS, S5_STATE, S5_GROUP, GDN_HEADS, GDN_HEAD_DIM
    n_idx = jnp.arange(P, dtype=F32)
    dt0 = jnp.exp(jax.random.uniform(ks[22], (DEPTH, H), F32, math.log(1e-3), math.log(1e-1)))
    return {
        'x_prompt': nrm(ks[0], (BATCH, SEQ, D_MODEL), 1.0),
        'x_sample': nrm(ks[1], (DEC_BATCH, DEC_SEQ, D_MODEL), 1.0),
        'state_s5_re': nrm(ks[2], (DEPTH, DEC_BATCH, G, P), 0.3),
        'state_s5_im': nrm(ks[3], (DEPTH, DEC_BATCH, G, P), 0.3),
        'state_gdn': nrm(ks[4], (DEPTH, DEC_BATCH, H, Dh, Dh), 0.3),
        'cache_gdn_conv': nrm(ks[5], (DEPTH, DEC_BATCH, CONV_WIDTH - 1, CONV_CH), 1.0),
        'c_prompt': nrm(ks[6], (BATCH, D_MODEL), 1.0),
        'c_sample': nrm(ks[7], (DEC_BATCH, D_MODEL), 1.0),
        'w_ada': nrm(ks[8], (DEPTH, D_MODEL, 6 * D_MODEL), 0.1 * D_MODEL ** -0.5),
        'b_ada': nrm(ks[9], (DEPTH, 6 * D_MODEL), 0.01),
        'w_in': nrm(ks[10], (DEPTH, D_MODEL, IN_COLS), D_MODEL ** -0.5),
        's5_a_re': -0.5 + nrm(ks[11], (DEPTH, G, P), 0.01),
        's5_a_im': jnp.pi * n_idx + nrm(ks[12], (DEPTH, G, P), 0.01),
        's5_log_dt': jax.random.uniform(ks[13], (DEPTH, G), F32, math.log(1e-3), math.log(1e-1)),
        's5_b_re': nrm(ks[14], (DEPTH, G, P, J), (2 * J) ** -0.5),
        's5_b_im': nrm(ks[15], (DEPTH, G, P, J), (2 * J) ** -0.5),
        's5_c_re': nrm(ks[16], (DEPTH, G, J, P), P ** -0.5),
        's5_c_im': nrm(ks[17], (DEPTH, G, J, P), P ** -0.5),
        's5_d': nrm(ks[18], (DEPTH, S5_WIDTH), 1.0),
        'w_s5_glu': nrm(ks[19], (DEPTH, S5_WIDTH, 2 * S5_WIDTH), S5_WIDTH ** -0.5),
        'gdn_conv_w': nrm(ks[20], (DEPTH, CONV_WIDTH, CONV_CH), CONV_WIDTH ** -0.5),
        'gdn_a_log': jnp.log(jax.random.uniform(ks[21], (DEPTH, H), F32, 1.0, 16.0)),
        'gdn_dt_bias': dt0 + jnp.log(-jnp.expm1(-dt0)),
        'gdn_norm_g': 1.0 + nrm(ks[23], (DEPTH, Dh), 0.1),
        'w_out': nrm(ks[24], (DEPTH, MIX_WIDTH, D_MODEL), BETA_INIT * MIX_WIDTH ** -0.5),
        'ln1_g': 1.0 + nrm(ks[25], (DEPTH, D_MODEL), 0.1),
        'ln1_b': nrm(ks[26], (DEPTH, D_MODEL), 0.01),
        'w_ffn_up': nrm(ks[27], (DEPTH, D_MODEL, 2 * D_FF), D_MODEL ** -0.5),
        'w_ffn_down': nrm(ks[28], (DEPTH, D_FF, D_MODEL), BETA_INIT * D_FF ** -0.5),
        'ln2_g': 1.0 + nrm(ks[29], (DEPTH, D_MODEL), 0.1),
        'ln2_b': nrm(ks[30], (DEPTH, D_MODEL), 0.01),
    }

def reference(x_prompt, x_sample, state_s5_re, state_s5_im, state_gdn, cache_gdn_conv,
              c_prompt, c_sample, w_ada, b_ada, w_in, s5_a_re, s5_a_im, s5_log_dt,
              s5_b_re, s5_b_im, s5_c_re, s5_c_im, s5_d, w_s5_glu, gdn_conv_w, gdn_a_log,
              gdn_dt_bias, gdn_norm_g, w_out, ln1_g, ln1_b, w_ffn_up, w_ffn_down, ln2_g, ln2_b):
    bp = x_prompt.shape[0]
    xp, xs = x_prompt, x_sample
    p_re, p_im, p_gdn, p_conv = [], [], [], []
    s_re, s_im, s_gdn, s_conv = [], [], [], []
    for l in range(DEPTH):
        lw = (w_ada[l], b_ada[l], w_in[l], s5_a_re[l], s5_a_im[l], s5_log_dt[l], s5_b_re[l],
              s5_b_im[l], s5_c_re[l], s5_c_im[l], s5_d[l], w_s5_glu[l], gdn_conv_w[l],
              gdn_a_log[l], gdn_dt_bias[l], gdn_norm_g[l], w_out[l], ln1_g[l], ln1_b[l],
              w_ffn_up[l], w_ffn_down[l], ln2_g[l], ln2_b[l])
        xp, hr, hi, sg, cb = trunk_layer(
            xp, c_prompt,
            jnp.zeros((bp, S5_GROUPS, S5_STATE), F32),
            jnp.zeros((bp, S5_GROUPS, S5_STATE), F32),
            jnp.zeros((bp, GDN_HEADS, GDN_HEAD_DIM, GDN_HEAD_DIM), F32),
            jnp.zeros((bp, CONV_WIDTH - 1, CONV_CH), x_prompt.dtype),
            *lw)
        p_re.append(hr); p_im.append(hi); p_gdn.append(sg); p_conv.append(cb)
        xs, hr, hi, sg, cb = trunk_layer(
            xs, c_sample, state_s5_re[l], state_s5_im[l], state_gdn[l], cache_gdn_conv[l], *lw)
        s_re.append(hr); s_im.append(hi); s_gdn.append(sg); s_conv.append(cb)
    return (xp, xs,
            jnp.stack(p_re), jnp.stack(p_im), jnp.stack(p_gdn), jnp.stack(p_conv),
            jnp.stack(s_re), jnp.stack(s_im), jnp.stack(s_gdn), jnp.stack(s_conv))


_drawn_inputs = setup_inputs


def setup_inputs(seed=0):
    import zlib

    import numpy as np

    out = dict(_drawn_inputs(seed))
    spreads = {}
    factors = {'s5_a_re': 53.815, 'ln1_b': 5.393, 'ln2_b': 5.561, 's5_c_re': 2.693, 's5_c_im': 2.695}
    for name, (base, spread) in spreads.items():
        noise = np.random.default_rng([zlib.crc32(name.encode()), seed]).standard_normal(out[name].shape)
        drawn = base * np.exp(spread * noise) if base else spread * noise
        out[name] = __import__('jax').numpy.asarray(drawn.astype(out[name].dtype))
    for name, factor in factors.items():
        out[name] = (out[name] * factor).astype(out[name].dtype)
    return out
```

```python
import concourse.bass as bass
from concourse import mybir
from contextlib import ExitStack

F32 = mybir.dt.float32
F32R = mybir.dt.float32r
ALU = mybir.AluOpType
ACT = mybir.ActivationFunctionType

P = 128
D_MODEL, SEQ, DEC_SEQ = 1024, 1024, 64
TOK = SEQ + DEC_SEQ
KD = D_MODEL // P
TILES = -(-TOK // P)
PTILES = SEQ // P
S5_G, S5_J, S5_P = 32, 16, 64
STEP = P // S5_J
NCH = SEQ // STEP
SCH = DEC_SEQ // STEP
W5 = 1 + NCH + 1 + SCH
SAMP5 = 1 + NCH
GB = P // S5_J
NB5 = S5_G // GB
HEADS, HD = 4, 128
CONVW = 4
GAP = CONVW - 1
ROWW = SEQ + GAP + P
SAMP_COL = SEQ + GAP
RAWW = GAP + SEQ + GAP + DEC_SEQ
D_FF = 2816
FB = D_FF // P
CH = [(0, 384), (384, 384), (768, 320)]
ADA_N = 512
ALPHA = 2 ** 0.25
LN_EPS, RMS_EPS = 1e-5, 1e-6
OFF_Z = 2048
OFF_BA = 2560
LEVELS = (2, 4, 8, 16, 32, 64)
LV = len(LEVELS)
TWO_PI = 6.283185307179586
ROUND = 12582912.0


SIGNALS = [
    "a_mm", "acc_in", "ada_mm", "bc", "bl_evac", "bt_T", "bt_ready", "c_silu", "ca_ready", "cas_ready", "cleared",
    "conv", "f_add", "f_bn", "f_mv", "f_n", "f_sil", "f_tmp", "f_xg", "g1_row", "g2_row", "g_A", "g_AT", "g_ATs",
    "g_E", "g_EA", "g_EB", "g_KK", "g_L", "g_P", "g_Pb", "g_QK", "g_QKp", "g_R", "g_S", "g_T", "g_U", "g_V", "g_Vb",
    "g_X", "g_X0", "g_XX", "g_Xm", "g_col", "g_dd", "g_init", "g_kS", "g_kv", "g_kv8", "g_mix", "g_mm", "g_oT",
    "g_ob", "g_pool", "g_qd", "g_red", "g_row", "g_sc", "g_sc2", "g_sq", "gate_T", "gate_act", "gate_d", "gate_dve",
    "gate_exp", "gate_g", "gate_ln", "gate_sum", "gate_x", "gates", "glu_mix", "glu_sig", "h2_scale", "h_hi",
    "h_lo", "h_mod", "halfpi", "hist", "in_evac", "k_evac", "ln1_rows", "ln2_rows", "ln_bn", "ln_mv", "ln_r",
    "ln_rs", "masks", "mm", "mod_T", "mod_cols", "mod_ready", "mod_row", "mt", "out", "ph_ready", "pool_step",
    "row_silu", "s5_abs", "s5_arg", "s5_d", "s5_den", "s5_exp_dt", "s5_g", "s5_gelu", "s5_h", "s5_rden", "s5_rot",
    "s5_trig", "s5_x", "s5_x1", "s5_y", "s_state", "small", "state_out", "tail", "tap", "tap0", "u_stored", "ud",
    "w_hi", "w_lo", "wtap", "x_T", "y_hi", "y_lo", "y_mm", "y_out", "y_stored", "z_mm", "z_read",
]
SIGNALS_OF_SLOTS = {"ada": 2, "adb": 2, "mod_st": 2, "raw": 2, "row_stored": 2,
                    "stg": 2, "x": 2, "x1_st": 2, "x_norm": 2, "xt": 2, "y": 4}

COUNTED_ON = {
    "o_T": ("g_T", TILES), "wo_mm": ("g_row", TILES), "f_dn": ("g_kv", TILES * HEADS),
    "ms_hi": ("g_sq", 2 * TILES), "o_n1": ("g_kv8", 2 * TILES), "o_n2": ("g_E", 3 * TILES), "h2_mod": ("g_ATs", TILES),
    "f_hi": ("g_Vb", TILES * HEADS),
    "ms_lo": ("g_red", 2 * TILES), "o_tmp": ("g_dd", TILES), "o_r": ("g_mm", 2 * TILES), "o_bn": ("g_A", TILES * HEADS),
    "o_mv": ("g_QK", TILES), "o_xg": ("g_qd", TILES), "h2_hi": ("g_Xm", 2 * TILES), "h2_lo": ("g_X0", 2 * TILES),
    "f_mul": ("g_R", TILES * HEADS), "f_lo": ("g_ob", TILES),
    "o_rs": ("g_col", TILES), "o_p": ("g_pool", 10 * TILES), "x1_ready": ("g_U", TILES), "f_rs": ("g_EA", TILES),
    "f_p": ("g_EB", TILES), "y_ready": ("g_sc2", TILES), "o_g1": ("g_sc", TILES), "f_g2": ("g_L", LV * TILES),
}


def bc(ap, axis, n):
    a = ap.unsqueeze(axis)
    shape = list(a.shape)
    shape[axis] = n
    return a.to_broadcast(shape)


def stream_step(nc, I, O, DR):
    ctx = ExitStack()
    with ctx:
        on = {name: ctx.enter_context(nc.semaphore(name)) for name in SIGNALS}
        for name, slots in SIGNALS_OF_SLOTS.items():
            on[name] = [ctx.enter_context(nc.semaphore(f"{name}{n}")) for n in range(slots)]
        for name, (earlier, _) in COUNTED_ON.items():
            on[name] = on[earlier]

        def at(name, shape, off, dt=F32):
            n = 4
            for d in shape[1:]:
                n *= d
            t = nc.alloc_sbuf_tensor_at(name, shape, dt, offset=off)
            return t, off + (n + 31) // 32 * 32

        base = -(-nc.sbuf_base // 32) * 32 if isinstance(nc.sbuf_base, int) else 1024
        off = base
        LIMIT = nc.sbuf_usable_end if isinstance(nc.sbuf_usable_end, int) else 212000

        def seq(start, *items):
            o, out = start, []
            for it in items:
                name, shape = it[0], it[1]
                t, o = at(name, shape, o, it[2] if len(it) > 2 else F32)
                out.append(t)
            assert o <= LIMIT, (items[0][0], o, LIMIT)
            return out, o

        (ident, triu, ones, lower, mask1, maskT, swapm, cT, csil, modc, onep,
         s5p, trig, sgn, mhalf, dcol_b, dcol, rad8, h0c, hout,
         tilecol, convw, cache, rawtail, normg, balog, gcol, stat, rstd), tables_at = seq(
            off,
            ("ident", [P, P]), ("triu", [P, P]), ("ones", [P, P]), ("lower", [P, P]), ("mask1", [P, P]),
            ("maskT", [P, 7, P]), ("swapm", [P, P]),
            ("cT", [P, KD, 2]), ("csil", [P, KD, 2]), ("modc", [P, 12, 4, 2]), ("onep", [P, 2, KD, 2]),
            ("s5p", [P, 3, S5_G]), ("trig", [P, 16, S5_G]),
            ("sgn", [P, 2]), ("mhalf", [P, 8]), ("dcol_b", [P, GB]), ("dcol", [P, S5_G]), ("rad8", [P, S5_G]),
            ("h0c", [P, S5_G]), ("hout", [P, S5_G, 2]),
            ("tilecol", [P, 2, 10, HEADS]), ("convw", [P, 12, CONVW]), ("cache", [P, 12, GAP]), ("rawtail", [P, 12, 2, GAP]),
            ("normg", [P, 1]), ("balog", [P, 2, HEADS]), ("gcol", [P, 10, TILES, HEADS]),
            ("stat", [P, 2, 16]), ("rstd", [P, 2, 2]))
        (pw_r, pw_i, rev_r, rev_i, en1, en2, coef), tables_end = seq(
            tables_at, ("pw_r", [P, S5_G, 9]), ("pw_i", [P, S5_G, 9]), ("rev_r", [P, S5_G, 8]), ("rev_i", [P, S5_G, 8]),
            ("en1", [P, S5_G, 8]), ("en2", [P, S5_G, 8]), ("coef", [P, 4, S5_G, 9]))
        off = tables_end
        R1 = off
        (hT_hi, hT_lo), R2 = seq(R1, ("hT_hi", [P, KD, TOK], F32R), ("hT_lo", [P, KD, TOK], F32R))
        (wraw, whi, wlo), R3 = seq(R2, ("wraw", [P, 2, 1024]), ("whi", [P, 2, 1024], F32R), ("wlo", [P, 2, 1024], F32R))
        (rawrow, convrow, urow, wtap, Ud, CA, CAs, BT, Bl, Bls, Mt, Ksb, phC, phS, rho, X, G, cG, sG,
         bc12, ptmp), endA = seq(
            R3, ("rawrow", [P, RAWW]), ("convrow", [P, 2, ROWW]), ("urow", [P, STEP, W5]), ("wtap", [P, 2, CONVW]),
            ("Ud", [P, GB, W5]), ("CA", [P, GB, 9, S5_J]), ("CAs", [P, GB, STEP, S5_J]), ("BT", [P, GB, STEP, S5_J]),
            ("Bl", [P, GB, P]), ("Bls", [P, GB, P]), ("Mt", [P, GB, P]), ("Ksb", [S5_J, GB, P]),
            ("phC", [P, GB, W5]), ("phS", [P, GB, W5]), ("rho", [P, GB, W5]), ("X", [P, GB, W5]),
            ("G", [P, GB, W5]), ("cG", [P, GB, W5]), ("sG", [P, GB, W5]),
            ("bc12", [P, 4, GB, S5_J]), ("ptmp", [P, GB * 9 * S5_J]))
        (bas,), _ = seq(endA, ("bas", [8, TILES * P]))
        (yraw, y_hi, y_lo, sgb), endG = seq(R3, ("yraw", [P, 4, STEP * W5]), ("y_hi", [P, 4, STEP * W5], F32R),
                                            ("y_lo", [P, 4, STEP * W5], F32R), ("sgb", [P, STEP * W5]))
        (wada2, bada2), _ = seq(endG, ("wada2", [P, 2, KD, ADA_N]), ("bada2", [2, ADA_N]))
        (stg, Lneg, modrow2), _ = seq(R1, ("stg", [P, 2, 16, P]), ("Lneg", [P, 6, HEADS, P]), ("modrow2", [2, 2, ADA_N]))
        hp = [P, HEADS, P]
        (gU, dd, EA, EB, Am, AT, QK, erow, qd, kdec, vp, Pb, Rb, Vb, ob, sq, Sst, Xb, sc), endD = seq(
            R3, ("gU", hp), ("dd", hp), ("EA", hp), ("EB", hp), ("Am", hp), ("AT", hp), ("QK", hp), ("erow", hp),
            ("qd", hp), ("kdec", hp), ("vp", hp), ("Pb", hp), ("Rb", hp), ("Vb", hp), ("ob", hp),
            ("sq", [P, 2 * HEADS, P]), ("Sst", [P, 2, HEADS, P]), ("Xb", [P, HEADS, 2, P]), ("sc", [P, 12, HEADS]))
        assert endD <= endG
        mixT, _ = at("mixT", [P, KD, TOK], R1 + (R2 - R1) // 2)
        (xin, xnorm, hpre, wada, bada, modrow), _ = seq(
            R3, ("xin", [P, 2, D_MODEL]), ("xnorm", [P, 2, D_MODEL]), ("hpre", [P, 2, KD, P]),
            ("wada", [P, 2, KD, ADA_N]), ("bada", [2, 2, ADA_N]), ("modrow", [2, 2, ADA_N]))
        (wo_hi, wo_lo, xt, xn2, hp2, otmp, g1r), _ = seq(
            R3, ("wo_hi", [P, KD, D_MODEL], F32R), ("wo_lo", [P, KD, D_MODEL], F32R), ("xt", [P, 2, D_MODEL]),
            ("xn2", [P, 2, D_MODEL]), ("hp2", [P, KD, P]), ("otmp", [P, D_MODEL]), ("g1r", [P, D_MODEL]))
        (ln1r,), rows_end = seq(tables_at, ("ln1r", [P, 2, D_MODEL]))
        (g2r,), _ = seq(tables_at, ("g2r", [P, 2, D_MODEL]))
        assert rows_end <= tables_end
        (acc, hid_hi, hid_lo, wd_hi, wd_lo, sil, dtmp), _ = seq(
            R3, ("acc", [P, TILES, D_MODEL]), ("hid_hi", [P, 2, TOK], F32R), ("hid_lo", [P, 2, TOK], F32R),
            ("wd_hi", [P, 2, D_MODEL], F32R), ("wd_lo", [P, 2, D_MODEL], F32R), ("sil", [P, TOK]), ("dtmp", [P, D_MODEL]))
        (ln2r,), _ = seq(R1, ("ln2r", [P, 2, D_MODEL]))
        ps = [ctx.enter_context(nc.psum_tensor(f"bank{n}", [P, 512], F32)) for n in range(8)]

        def count(value):
            return max(0, value) if isinstance(value, int) else value

        def since(name, value):
            return COUNTED_ON[name][1] + count(value)

        def alone(e, value):
            if not isinstance(value, int):
                value = e.to_reg(value)
                e.wait_ge(on["small"], 16 * len(SMALL))
            return value

        class Steps:

            def __init__(self, e, done, base=0):
                self.e, self.done, self.base, self.n = e, done, base, 0

            def __call__(self, ins):
                ins.then_inc(self.done, 1)
                self.n += 1
                self.e.wait_ge(self.done, alone(self.e, self.base + self.n))

        def split_hi(e, slot, loaded, width=1024):
            e.wait_ge(on["raw"][slot], count(loaded))
            nc.scalar.activation(whi[:, slot, 0:width], wraw[:, slot, 0:width], ACT.Copy).then_inc(on["w_hi"], 1)

        def split_lo(e, slot, hi_at, width=1024):
            e.wait_ge(on["w_hi"], count(hi_at))
            nc.vector.tensor_tensor(wlo[:, slot, 0:width], wraw[:, slot, 0:width],
                                         whi[:, slot, 0:width].bitcast(F32), ALU.subtract).then_inc(on["w_lo"], 1)

        def proj_block(e, slot, split_at, banks, bank_free, a_hi, a_lo, kt=KD, chunks=CH):
            e.wait_ge(on["w_lo"], count(split_at))
            for c, (c0, cw) in enumerate(chunks):
                bank_free(c)
                for k in range(kt):
                    for n, (w, a) in enumerate(((whi, a_hi), (whi, a_lo), (wlo, a_hi))):
                        last = nc.tensor.matmul(ps[banks[c]][:, 0:cw], w[:, slot, k * P:(k + 1) * P],
                                                a[:, k, c0:c0 + cw], start=(k == 0 and n == 0),
                                                stop=(k == kt - 1 and n == 2))
                last.then_inc(on["mm"], 1)

        NU, NMAIN = NB5, 4 * NB5
        win = I["w_in"].rearrange("(k p) n -> p k n", p=P)
        wad = I["w_ada"].rearrange("(k p) n -> p k n", p=P)
        SMALL = [(cT, "cT"), (s5p, "s5p"), (dcol, "s5d"), (h0c, "s5h0"), (convw, "convw"), (cache, "cache"),
                 (balog, "balog"), (normg, "normg")]
        ROUNDS5 = [(0, 3), (3, 3), (6, 2)]

        def loads_before(sp):
            for t, name in SMALL:
                sp.dma_start(t[:], I[name]).then_inc(on["small"], 16)
            for c in range(2):
                sp.dma_start(wada[:, c, :, :], wad[:, :, c * ADA_N:(c + 1) * ADA_N]).then_inc(on["ada"][c], 16)
                sp.dma_start(bada[:, c, :], I["b_ada"][:, c * ADA_N:(c + 1) * ADA_N]).then_inc(on["ada"][c], 16)
            for s in range(2):
                sp.dma_start(xin[:, s, :], I["x_prompt"][s * P:(s + 1) * P, :]).then_inc(on["x"][s], 16)
            for c in range(2, 4):
                sp.wait_ge(on["ada_mm"], count(c - 1))
                sp.dma_start(wada[:, c % 2, :, :], wad[:, :, c * ADA_N:(c + 1) * ADA_N]).then_inc(on["ada"][c % 2], 16)
                sp.wait_ge(on["mod_row"], count(c - 1))
                sp.dma_start(bada[:, c % 2, :], I["b_ada"][:, c * ADA_N:(c + 1) * ADA_N]).then_inc(on["ada"][c % 2], 16)
            with sp.Fori(1, PTILES // 2) as i:
                for s in range(2):
                    sp.wait_ge(on["x_norm"][s], count(i))
                    sp.dma_start(xin[:, s, :], I["x_prompt"][bass.ds(i * 2 * P + s * P, P), :]).then_inc(on["x"][s], 16)
            sp.wait_ge(on["x_norm"][0], PTILES // 2)
            sp.dma_start(xin[0:DEC_SEQ, 0, :], I["x_sample"]).then_inc(on["x"][0], 16)

        def loads_projection(sp):
            for n in range(NU):
                if n >= 2:
                    sp.wait_ge(on["w_lo"], count(n - 1))
                sp.dma_start(wraw[:, n % 2, :].rearrange("p (k n) -> p k n", k=KD), win[:, :, n * P:(n + 1) * P]).then_inc(on["raw"][n % 2], 16)
            with sp.Fori(0, NB5) as b:
                for j in range(4):
                    sp.wait_ge(on["w_lo"], count(b * 4 + (NU + j - 1)))
                    sp.dma_start(wraw[:, j % 2, :].rearrange("p (k n) -> p k n", k=KD), win[:, :, bass.ds(b * P + (j + 1) * 512, P)]).then_inc(on["raw"][j % 2], 16)
                    if j == 0:
                        sp.wait_ge(on["u_stored"], NU * 16)
                        sp.wait_ge(on["y_mm"], count(b))
                        sp.wait_ge(on["s5_y"], count(b * 3))
                        for s in range(STEP):
                            sp.dma_start(Ud[s * S5_J:(s + 1) * S5_J, :, :], DR["u"][bass.ds(b * GB, GB), :, s, :].rearrange("g j n -> j g n")).then_inc(on["ud"], 16)
                    if j == 3:
                        sp.wait_ge(on["k_evac"], count(b * 2 + 2))
                        for s in range(STEP):
                            sp.dma_start(Mt[s * S5_J:(s + 1) * S5_J, :, s * S5_J:P], Ksb[:, :, 0:P - s * S5_J]).then_inc(on["mt"], 16)
            sp.wait_ge(on["w_lo"], NU + NMAIN - 1)
            sp.dma_start(wraw[:, 0, :].rearrange("p (k n) -> p k n", k=KD), win[:, :, OFF_BA + 8 - P:OFF_BA + 8]).then_inc(on["raw"][0], 16)

        def masks(pool):
            g = Steps(pool, on["pool_step"])
            for t in (ident, lower, mask1, swapm):
                g(pool.memset(t[:], 0.0))
            g(pool.memset(triu[:], 1.0))
            g(pool.memset(ones[:], 1.0))
            g(pool.memset(lower[:], 1.0))
            g(pool.memset(maskT[:], 0.0))
            g(pool.memset(sgn[:], 1.0))
            g(pool.memset(mhalf[:], -0.5))
            g(pool.memset(sgn[0:S5_P, 0:1], -1.0))
            sel = lambda ap, pat, op, fill, base, cm: g(pool.affine_select(
                out=ap, in_=ap, compare_op=op, fill=fill, base=base, pattern=pat, channel_multiplier=cm))
            sel(ident[:], [[-1, P]], ALU.not_equal, 1.0, 0, 1)
            sel(triu[:], [[1, P]], ALU.is_ge, 0.0, 0, -1)
            sel(lower[:], [[-1, P]], ALU.is_gt, 0.0, 0, 1)
            sel(swapm[:], [[-1, P]], ALU.not_equal, -1.0, -S5_P, 1)
            sel(swapm[:], [[-1, P]], ALU.not_equal, 1.0, S5_P, 1)
            for n, b in enumerate((1,) + LEVELS):
                v = maskT[:, n, :].rearrange("p (m h c) -> p m h c", h=2, c=b)[:, :, 1, :]
                g(pool.memset(v, -1.0))
                sel(v, [[-2 * b, P // (2 * b)], [0, b]], ALU.is_ge, 0.0, 0, 1)
                sel(v, [[2 * b, P // (2 * b)], [0, b]], ALU.is_ge, 0.0, b - 1, -1)
            v = mask1[:].rearrange("p (m h) -> p m h", h=2)[:, :, 0]
            g(pool.memset(v, -1.0))
            sel(v, [[-2, P // 2]], ALU.is_equal, 0.0, -1, 1)
            pool.memset(trig[:, 13, :], TWO_PI / 4).then_inc(on["halfpi"], 1)
            pool.memset(sgn[:, 1:2], 1.0).then_inc(on["masks"], 1)
            return g.n

        def s5_tables(pool, n0):
            g = Steps(pool, on["pool_step"], n0)
            tt = lambda o, a, b, op: g(pool.tensor_tensor(o, a, b, op))
            ts = lambda o, a, s1, s2, op0, op1=None: g(pool.tensor_scalar(o, a, s1, s2, op0, op1) if op1 is not None
                                                       else pool.tensor_scalar(o, a, s1, None, op0))
            T = lambda n: trig[:, n, :]
            are, aim, ldt = (s5p[:, n, :] for n in range(3))
            DT, EXA, TH, KK, MAG, COS, SIN, A1, A2, DEN, FR, FI = range(12)

            def cmul(o_r, o_i, x_r, x_i, y_r, y_i, t1, t2):
                tt(t1, x_r, y_r, ALU.mult)
                tt(t2, x_i, y_i, ALU.mult)
                tt(t1, t1, t2, ALU.subtract)
                tt(t2, x_r, y_i, ALU.mult)
                tt(o_i, x_i, y_r, ALU.mult)
                tt(o_i, o_i, t2, ALU.add)
                g(pool.tensor_copy(o_r, t1))

            pool.wait_ge(on["s5_exp_dt"], 1)
            tt(T(EXA), are, T(DT), ALU.mult)
            pool.tensor_copy(T(A1), T(EXA)).then_inc(on["s5_arg"], 1)
            pool.wait_ge(on["s5_arg"], 1)
            tt(T(TH), aim, T(DT), ALU.mult)
            ts(T(KK), T(TH), 1.0 / TWO_PI, ROUND, ALU.mult, ALU.add)
            ts(T(KK), T(KK), ROUND, None, ALU.subtract)
            for part in (6.28125, 0.0019340515136718750, 1.2556659146e-06):
                ts(T(A2), T(KK), part, None, ALU.mult)
                tt(T(TH), T(TH), T(A2), ALU.subtract)
            g(pool.tensor_scalar(T(TH), T(TH), 3.1415925, -3.1415925, ALU.min, ALU.max))
            pool.tensor_copy(T(A2), T(TH)).then_inc(on["s5_arg"], 1)
            pool.wait_ge(on["s5_arg"], 2)
            pool.wait_ge(on["s5_trig"], 3)
            one = lambda ap: g(pool.memset(ap, 1.0))
            one(pw_r[:, :, 0])
            g(pool.memset(pw_i[:, :, 0], 0.0))
            tt(pw_r[:, :, 1], T(MAG), T(COS), ALU.mult)
            tt(pw_i[:, :, 1], T(MAG), T(SIN), ALU.mult)
            ts(T(FR), pw_r[:, :, 1], 1.0, None, ALU.subtract)
            tt(T(A1), are, are, ALU.mult)
            tt(T(A2), aim, aim, ALU.mult)
            tt(T(A1), T(A1), T(A2), ALU.add)
            pool.tensor_copy(T(14), T(A1)).then_inc(on["s5_den"], 1)
            pool.wait_ge(on["s5_den"], 1)
            tt(T(A1), T(FR), are, ALU.mult)
            tt(T(A2), pw_i[:, :, 1], aim, ALU.mult)
            tt(T(A1), T(A1), T(A2), ALU.add)
            tt(T(A2), T(FR), aim, ALU.mult)
            tt(T(FI), pw_i[:, :, 1], are, ALU.mult)
            tt(T(FI), T(FI), T(A2), ALU.subtract)
            pool.wait_ge(on["s5_rden"], 1)
            tt(T(FR), T(A1), T(DEN), ALU.mult)
            tt(T(FI), T(FI), T(DEN), ALU.mult)
            t1, t2 = rev_r, rev_i
            for lo, m, y in ((1, 1, 1), (1, 2, 2), (1, 4, 4)):
                cmul(pw_r[:, :, lo + m:lo + 2 * m], pw_i[:, :, lo + m:lo + 2 * m], pw_r[:, :, lo:lo + m], pw_i[:, :, lo:lo + m],
                     pw_r[:, :, y:y + 1].to_broadcast([P, S5_G, m]), pw_i[:, :, y:y + 1].to_broadcast([P, S5_G, m]),
                     t1[:, :, 0:m], t2[:, :, 0:m])
            ts(coef[:, 1, :, :], pw_i[:], -1.0, None, ALU.mult)
            ts(coef[:, 3, :, :], pw_r[:], -1.0, None, ALU.mult)
            ts(coef[:, 0, :, :], coef[:, 3, :, :], sgn[:, 0:1], None, ALU.mult)
            ts(coef[:, 2, :, :], pw_i[:], sgn[:, 0:1], None, ALU.mult)
            for s in range(STEP):
                g(pool.tensor_copy(rev_r[:, :, s], pw_r[:, :, STEP - 1 - s]))
                g(pool.tensor_copy(rev_i[:, :, s], pw_i[:, :, STEP - 1 - s]))
            fr, fi = bc(T(FR), 2, STEP), bc(T(FI), 2, STEP)
            ptv = ptmp[:, 0:S5_G * STEP].rearrange("p (g s) -> p g s", g=S5_G)
            tt(en1[:], rev_r[:], fr, ALU.mult)
            tt(ptv, rev_i[:], fi, ALU.mult)
            tt(en1[:], en1[:], ptv, ALU.subtract)
            tt(en2[:], rev_r[:], fi, ALU.mult)
            tt(ptv, rev_i[:], fr, ALU.mult)
            tt(en2[:], en2[:], ptv, ALU.add)
            ts(en2[:], en2[:], sgn[:, 0:1], None, ALU.mult)
            for _ in range(3):
                tt(T(A1), T(COS), T(COS), ALU.mult)
                tt(T(A2), T(SIN), T(SIN), ALU.mult)
                tt(T(SIN), T(SIN), T(COS), ALU.mult)
                ts(T(SIN), T(SIN), 2.0, None, ALU.mult)
                tt(T(COS), T(A1), T(A2), ALU.subtract)
                tt(T(MAG), T(MAG), T(MAG), ALU.mult)
            return n0 + g.n, (COS, SIN, MAG)

        def s5_batch_tables(pool, b, n0, per, trigs):
            COS, SIN, MAG = trigs
            g = Steps(pool, on["pool_step"], n0 + b * per)
            tt = lambda o, a, c, op: pool.tensor_tensor(o, a, c, op)
            gs = bass.ds(b * GB, GB)
            pool.dma_start(bc12[:], I["s5bc"][:, :, gs, :]).then_inc(on["bc"], 16)
            pool.wait_ge(on["bc"], alone(pool, count(b * 16 + 16)))

            def combine(out, tmp, m, x, y, c1, c2, name):
                n = out.shape[2]
                g(tt(out, bc(x, 2, n), bc(c1, 3, S5_J), ALU.mult))
                g(tt(tmp, bc(y, 2, n), bc(c2, 3, S5_J), ALU.mult))
                tt(out, out, tmp, ALU.add).then_inc(name, 1)

            B1, B2, C1, C2 = (bc12[:, n, :, :] for n in range(4))
            tmp9 = ptmp[:].rearrange("p (g m j) -> p g m j", g=GB, j=S5_J)
            tmp8 = ptmp[:, 0:GB * STEP * S5_J].rearrange("p (g m j) -> p g m j", g=GB, j=S5_J)
            pool.wait_ge(on["a_mm"], alone(pool, count(b)))
            combine(BT[:], tmp8, STEP, B1, B2, en1[:, gs, :], en2[:, gs, :], on["bt_ready"])
            pool.wait_ge(on["bt_ready"], alone(pool, count(b + 1)))
            pool.wait_ge(on["y_mm"], alone(pool, count(b)))
            combine(CA[:], tmp9, 9, C1, C2, coef[:, 0, gs, :], coef[:, 1, gs, :], on["ca_ready"])
            pool.wait_ge(on["ca_ready"], alone(pool, count(b + 1)))
            g(pool.memset(phC[:, :, 0:1], 1.0))
            g(pool.memset(phS[:, :, 0:1], 0.0))
            g(pool.tensor_copy(phC[:, :, 1], trig[:, COS, gs]))
            g(pool.tensor_copy(phS[:, :, 1], trig[:, SIN, gs]))
            m = 1
            while m < NCH:
                a_r, a_i = phC[:, :, 1:1 + m], phS[:, :, 1:1 + m]
                y_r, y_i = (x[:, :, m:m + 1].to_broadcast([P, GB, m]) for x in (phC, phS))
                o_r, o_i = phC[:, :, 1 + m:1 + 2 * m], phS[:, :, 1 + m:1 + 2 * m]
                t1 = ptmp[:, 0:GB * m].rearrange("p (g m) -> p g m", g=GB)
                t2 = ptmp[:, GB * m:2 * GB * m].rearrange("p (g m) -> p g m", g=GB)
                g(tt(o_r, a_r, y_r, ALU.mult))
                g(tt(t1, a_i, y_i, ALU.mult))
                g(tt(o_r, o_r, t1, ALU.subtract))
                g(tt(o_i, a_r, y_i, ALU.mult))
                g(tt(t1, a_i, y_r, ALU.mult))
                g(tt(o_i, o_i, t1, ALU.add))
                m *= 2
            for x in (phC, phS):
                g(pool.tensor_copy(x[:, :, SAMP5:W5], x[:, :, 0:1 + SCH]))
            g(pool.tensor_copy(rho[:], bc(trig[:, MAG, gs], 2, W5)))
            g(pool.memset(rho[:, :, 0:1], 0.0))
            pool.memset(rho[:, :, SAMP5:SAMP5 + 1], 0.0).then_inc(on["ph_ready"], 1)
            combine(CAs[:], tmp8, STEP, C1, C2, coef[:, 2, gs, 1:9], coef[:, 3, gs, 1:9], on["cas_ready"])
            pool.wait_ge(on["cas_ready"], alone(pool, count(b + 1)))
            return g.n

        def ada_mm(e, c, slot, loaded, freed, bank):
            e.wait_ge(on["ada"][slot], count(loaded))
            for k in range(KD):
                last = nc.tensor.matmul(ps[bank][0:2, :], csil[:, k, :], wada[:, slot, k, :], start=(k == 0), stop=(k == KD - 1))
            last.then_inc(on["ada_mm"], 1)
            e.wait_ge(on["mod_row"], count(freed))
            for q in range(4):
                last = nc.tensor.transpose(ps[7][:, 2 * q:2 * q + 2], modrow[:, slot, q * P:(q + 1) * P], ident[0:2, 0:2])
            last.then_inc(on["mod_T"], 1)

        def ln_transpose(e, s, ready, freed, rows):
            e.wait_ge(on["x_norm"][s], count(ready))
            e.wait_ge(on["h_mod"], count(freed))
            for k in range(KD):
                last = nc.tensor.transpose(ps[2 * s + k // 4][:, (k % 4) * P:(k % 4) * P + rows],
                                           xnorm[0:rows, s, k * P:(k + 1) * P], ident[0:rows, 0:rows])
            last.then_inc(on["x_T"], 1)

        def s5_A(e, b):
            e.wait_ge(on["bt_ready"], count(b + 1))
            e.wait_ge(on["s5_y"], count(b * 3))
            for g in range(GB):
                last = nc.tensor.transpose(ps[3 + g // 4][:, (g % 4) * P:(g % 4 + 1) * P],
                                           BT[:, g, :, :].rearrange("p s j -> p (s j)"), ident[:])
            last.then_inc(on["bt_T"], 1)
            e.wait_ge(on["ca_ready"], count(b + 1))
            for g in range(GB):
                last = nc.tensor.matmul(ps[5 + g // 4][0:S5_J, (g % 4) * P:(g % 4 + 1) * P], BT[:, g, STEP - 1, :],
                                        CA[:, g, 0:STEP, :].rearrange("p t i -> p (t i)"), start=True, stop=True)
            last.then_inc(on["a_mm"], 1)

        def s5_Z(e, b):
            e.wait_ge(on["ud"], count(b * (16 * STEP) + 16 * STEP))
            e.wait_ge(on["bl_evac"], count(b * 2 + 2))
            e.wait_ge(on["k_evac"], count(b * 2 + 2))
            for r, (g0, gn) in enumerate(ROUNDS5):
                if r == 2:
                    e.wait_ge(on["z_read"], count(b * 3 + 1))
                for q in range(gn):
                    for B, bank in ((Bl, 3 + r % 2), (Bls, 5 + r % 2)):
                        last = nc.tensor.matmul(ps[bank][:, q * W5:(q + 1) * W5], B[:, g0 + q, :], Ud[:, g0 + q, :],
                                                start=True, stop=True)
                last.then_inc(on["z_mm"], 1)

        def s5_Y(e, b):
            e.wait_ge(on["cas_ready"], count(b + 1))
            e.wait_ge(on["mt"], count(b * (16 * STEP) + 16 * STEP))
            e.wait_ge(on["s5_rot"], count(b * 2 + 2))
            for r, (g0, gn) in enumerate(ROUNDS5):
                for q in range(gn):
                    g, out = g0 + q, ps[3 + r][:, q * W5:q * W5 + W5 - 1]
                    nc.tensor.matmul(out, CA[:, g, 1:9, :].rearrange("p t i -> p (t i)"), cG[:, g, 0:W5 - 1], start=True, stop=False)
                    nc.tensor.matmul(out, CAs[:, g, :, :].rearrange("p t i -> p (t i)"), sG[:, g, 0:W5 - 1], start=False, stop=False)
                    last = nc.tensor.matmul(out, Mt[:, g, :], Ud[:, g, 1:W5], start=False, stop=True)
                last.then_inc(on["y_out"], 1)
            last = nc.tensor.matmul(ps[6][:, 0:GB], swapm[:], sG[:, :, NCH], start=True, stop=True)
            last = nc.tensor.matmul(ps[6][:, GB:2 * GB], swapm[:], sG[:, :, W5 - 1], start=True, stop=True)
            last.then_inc(on["y_mm"], 1)

        def in_block(e, slot, n):
            def bank_free(c):
                if not isinstance(n, int) or n:
                    e.wait_ge(on["in_evac"], count(n * 3 + (c - 2)))
            proj_block(e, slot, n + 1, (0, 1, 2), bank_free, hT_hi, hT_lo)

        def ln_norm(e, s, ready, used, rows):
            e.wait_ge(on["ln_rs"], count(ready))
            e.wait_ge(on["x_T"], count(used))
            nc.scalar.activation(xnorm[0:rows, s, :], xin[0:rows, s, :], ACT.Identity, bias=rstd[0:rows, s, 1:2],
                                      scale=rstd[0:rows, s, 0:1]).then_inc(on["x_norm"][s], 1)

        def ln_mod(e, s, ready, used, rows, tok, which, sh):
            e.wait_ge(on["x_T"], count(ready))
            e.wait_ge(on["h_lo"], count(used))
            for k in range(KD):
                last = nc.scalar.activation(hpre[:, s, k, 0:rows], ps[2 * s + k // 4][:, (k % 4) * P:(k % 4) * P + rows], ACT.Identity,
                                            scale=onep[:, which, k, tok:tok + 1],
                                            bias=modc[:, sh + k // 4, k % 4, tok:tok + 1])
            last.then_inc(on["h_mod"], 1)

        def evac_chunks(n, put):
            for c, (c0, cw) in enumerate(CH):
                nc.scalar.wait_ge(on["mm"], count(n * 3 + (c + 1)))
                put(c, c0, cw).then_inc(on["in_evac"], 1)

        def s5_evac_A(act, b):
            act.wait_ge(on["bt_T"], count(b + 1))
            act.wait_ge(on["s5_y"], count(b * 3))
            for h in range(2):
                src = ps[3 + h][:].rearrange("p (g c) -> p g c", c=P)
                dst = slice(4 * h, 4 * h + 4)
                act.activation(Bl[:, dst, :], src, ACT.Copy)
                act.activation(Bls[:, dst, 0:S5_P], src[:, :, S5_P:P], ACT.Copy)
                act.activation(Bls[:, dst, S5_P:P], src[:, :, 0:S5_P], ACT.Copy, scale=-1.0).then_inc(on["bl_evac"], 1)
            act.wait_ge(on["a_mm"], count(b + 1))
            act.wait_ge(on["mt"], count(b * (16 * STEP)))
            for h in range(2):
                act.activation(Ksb[:, 4 * h:4 * h + 4, :], ps[5 + h][0:S5_J, :].rearrange("p (g c) -> p g c", c=P), ACT.Copy).then_inc(on["k_evac"], 1)

        def s5_scan(dve, b):
            dve.wait_ge(on["ph_ready"], count(b + 1))
            dve.wait_ge(on["y_stored"], count(b * (STEP * 16)))
            for r, (g0, gn) in enumerate(ROUNDS5):
                dve.wait_ge(on["z_mm"], count(b * 3 + (r + 1)))
                gsl = slice(g0, g0 + gn)
                v = lambda bank: ps[bank][:, 0:gn * W5].rearrange("p (g w) -> p g w", g=gn)
                dve.tensor_tensor(X[:, gsl, :], phC[:, gsl, :], v(3 + r % 2), ALU.mult).then_inc(on["s5_x1"], 1)
                dve.tensor_tensor(cG[:, gsl, :], phS[:, gsl, :], v(5 + r % 2), ALU.mult).then_inc(on["z_read"], 1)
            dve.wait_ge(on["s5_x1"], count(b * 3 + 3))
            dve.wait_ge(on["z_read"], count(b * 3 + 3))
            dve.tensor_tensor(X[:], X[:], cG[:], ALU.add).then_inc(on["s5_x"], 1)
            dve.wait_ge(on["s5_x"], count(b * 2 + 1))
            dve.tensor_copy(X[:, :, SAMP5], h0c[:, bass.ds(b * GB, GB)]).then_inc(on["s5_x"], 1)
            dve.wait_ge(on["s5_x"], count(b * 2 + 2))
            dve.tensor_copy(dcol_b[:], dcol[:, bass.ds(b * GB, GB)]).then_inc(on["s5_d"], 1)
            flat = lambda t: t[:].rearrange("p g w -> p (g w)")
            dve.tensor_tensor_scan(flat(G), flat(rho), flat(X), 0.0, ALU.mult, ALU.add).then_inc(on["s5_g"], 1)
            dve.wait_ge(on["s5_g"], count(b + 1))
            dve.tensor_tensor(cG[:], phC[:], G[:], ALU.mult).then_inc(on["s5_rot"], 1)
            dve.tensor_tensor(sG[:], phS[:], G[:], ALU.mult).then_inc(on["s5_rot"], 1)

        def s5_out(dve, b):
            dve.wait_ge(on["s5_d"], count(b + 1))
            for r, (g0, gn) in enumerate(ROUNDS5):
                dve.wait_ge(on["y_out"], count(b * 3 + (r + 1)))
                dve.wait_ge(on["s5_rot"], count(b * 2 + 2))
                for q in range(gn):
                    g = g0 + q
                    last = dve.scalar_tensor_tensor(out=X[:, g, 0:W5 - 1], in0=Ud[:, g, 1:W5], scalar=dcol_b[:, g:g + 1],
                                                    in1=ps[3 + r][:, q * W5:q * W5 + W5 - 1], op0=ALU.mult, op1=ALU.add)
                last.then_inc(on["s5_y"], 1)
            dve.wait_ge(on["y_mm"], count(b + 1))
            for n, col in enumerate((NCH, W5 - 1)):
                last = dve.tensor_tensor(hout[:, bass.ds(b * GB, GB), n], cG[:, :, col], ps[6][:, n * GB:(n + 1) * GB], ALU.add)
            last.then_inc(on["s5_h"], 1)


        (BETA, GATE, DEC, TOT, NEXP, KDEC, GLAST, T0, T1, T2) = range(10)
        gc = lambda n, t: gcol[:, n, t, :] if isinstance(t, int) else gcol[:, n, bass.ds(t, 1), :].rearrange("p a h -> p (a h)")
        R_BA = NU + NMAIN
        R_GLU = R_BA + 1
        MM_BA, MM_GLU = 3 * R_BA, 3 * R_GLU

        def gates_pe(pe):
            pe.wait_ge(on["w_lo"], R_BA + 1)
            for c, (c0, cw) in enumerate(CH):
                pe.wait_ge(on["in_evac"], count(MM_BA - 3 + c + 1))
                for k in range(KD):
                    for n, (w, a) in enumerate(((whi, hT_hi), (whi, hT_lo), (wlo, hT_hi))):
                        last = pe.matmul(ps[c][0:8, 0:cw], w[:, 0, (k + 1) * P - 8:(k + 1) * P], a[:, k, c0:c0 + cw],
                                         start=(k == 0 and n == 0), stop=(k == KD - 1 and n == 2))
                last.then_inc(on["mm"], 1)
            pe.wait_ge(on["in_evac"], MM_BA + 3)
            for t in range(TILES):
                last = pe.transpose(ps[7][:, 8 * t:8 * t + 8], bas[:, t * P:(t + 1) * P], ident[0:8, 0:8])
            last.then_inc(on["gate_T"], 1)
            pe.wait_ge(on["gate_g"], 1)
            flat = gcol[:, GATE, :, :].rearrange("p t h -> p (t h)")
            pe.matmul(ps[6][:, 0:TILES * HEADS], triu[:], flat, start=True, stop=True)
            pe.matmul(ps[6][:, 64:64 + TILES * HEADS], ones[:], flat, start=True, stop=True).then_inc(on["gate_sum"], 1)

        def gates_act(act):
            for c, (c0, cw) in enumerate(CH):
                act.wait_ge(on["mm"], count(MM_BA + c + 1))
                act.activation(bas[:, c0:c0 + cw], ps[c][0:8, 0:cw], ACT.Copy).then_inc(on["in_evac"], 1)
            g = Steps(act, on["gate_act"])
            act.wait_ge(on["gate_x"], 1)
            raw = ps[7][:, 0:8 * TILES].rearrange("p (t c) -> p t c", c=8)
            g(act.activation(gcol[:, BETA, :, :], raw[:, :, 0:HEADS], ACT.Sigmoid))
            g(act.activation(gcol[:, T1, :, :], gcol[:, T0, :, :], ACT.Abs))
            g(act.activation(gcol[:, T1, :, :], gcol[:, T1, :, :], ACT.Exp, scale=-1.0))
            g(act.activation(gcol[:, T1, :, :], gcol[:, T1, :, :], ACT.Ln, bias=1.0))
            g(act.activation(balog[:, 0, :], balog[:, 0, :], ACT.Exp))
            act.activation(gcol[:, T2, :, :], gcol[:, T0, :, :], ACT.Relu).then_inc(on["gate_ln"], 1)
            act.wait_ge(on["gate_sum"], 1)
            act.wait_ge(on["gate_d"], 2)
            g(act.activation(gcol[:, NEXP, :, :], gcol[:, DEC, :, :], ACT.Exp))
            g(act.activation(gcol[:, GLAST, :, :], gcol[:, TOT, :, :], ACT.Exp))
            act.wait_ge(on["gate_d"], 3)
            act.activation(gcol[:, KDEC, :, :], gcol[:, T0, :, :], ACT.Exp).then_inc(on["gate_exp"], 1)

        def gates_dve(dve):
            dve.wait_ge(on["gate_T"], 1)
            raw = ps[7][:, 0:8 * TILES].rearrange("p (t c) -> p t c", c=8)
            dve.tensor_tensor(gcol[:, T0, :, :], raw[:, :, HEADS:8], bc(balog[:, 1, :], 1, TILES), ALU.add).then_inc(on["gate_x"], 1)
            dve.wait_ge(on["gate_ln"], 1)
            dve.wait_ge(on["gate_act"], 5)
            g = Steps(dve, on["gate_dve"])
            g(dve.tensor_tensor(gcol[:, T1, :, :], gcol[:, T1, :, :], gcol[:, T2, :, :], ALU.add))
            g(dve.tensor_tensor(gcol[:, T1, :, :], gcol[:, T1, :, :], bc(balog[:, 0, :], 1, TILES), ALU.mult))
            g(dve.tensor_scalar(gcol[:, GATE, :, :], gcol[:, T1, :, :], -1.0, None, ALU.mult))
            dve.memset(gcol[DEC_SEQ:P, GATE, TILES - 1, :], 0.0).then_inc(on["gate_g"], 1)
            dve.wait_ge(on["gate_sum"], 1)
            n = TILES * HEADS
            v = lambda a: a.rearrange("p (t h) -> p t h", h=HEADS)
            dve.tensor_copy(gcol[:, DEC, :, :], v(ps[6][:, 0:n])).then_inc(on["gate_d"], 1)
            dve.tensor_copy(gcol[:, TOT, :, :], v(ps[6][:, 64:64 + n])).then_inc(on["gate_d"], 1)
            dve.wait_ge(on["gate_d"], 2)
            dve.tensor_tensor(gcol[:, T0, :, :], gcol[:, TOT, :, :], gcol[:, DEC, :, :], ALU.subtract).then_inc(on["gate_d"], 1)
            dve.wait_ge(on["gate_exp"], 1)
            dve.wait_ge(on["gate_act"], 7)
            dve.tensor_scalar(gcol[:, NEXP, :, :], gcol[:, NEXP, :, :], -1.0, None, ALU.mult).then_inc(on["gates"], 1)

        TCH = [(0, 3), (3, 3), (6, 2)]
        YCH = [(t0 * W5, tn * W5) for t0, tn in TCH]

        def glu_pe(pe):
            pe.wait_ge(on["gate_d"], 2)
            pe.wait_ge(on["y_lo"], 4)
            with pe.Fori(0, 4) as f:
                proj_block(pe, 1, f * 2 + (R_GLU + 1), (3, 4, 5), lambda c: pe.wait_ge(on["glu_sig"], count(f * 3)), y_hi, y_lo, 4, YCH)
                proj_block(pe, 0, f * 2 + (R_GLU + 2), (0, 1, 2), lambda c: pe.wait_ge(on["glu_mix"], count(f * 3)), y_hi, y_lo, 4, YCH)

        def glu_act(act):
            for k in range(4):
                act.wait_ge(on["y"][k], 16)
                act.activation(y_hi[:, k, :], yraw[:, k, :], ACT.Copy).then_inc(on["y_hi"], 1)
            act.wait_ge(on["mm"], MM_BA)
            split_hi(act, 1, 16 * (R_GLU // 2 + 1), 512)
            def pair(f, more):
                act.wait_ge(on["mm"], count(f * 6 + MM_GLU))
                split_hi(act, 0, f * 16 + 16 * ((R_GLU + 1) // 2 + 1), 512)
                act.wait_ge(on["glu_mix"], count(f * 3))
                for c, (c0, cw) in enumerate(YCH):
                    act.wait_ge(on["mm"], count(f * 6 + (MM_GLU + c + 1)))
                    act.activation(sgb[:, c0:c0 + cw], ps[3 + c][:, 0:cw], ACT.Sigmoid).then_inc(on["glu_sig"], 1)
                act.wait_ge(on["mm"], count(f * 6 + (MM_GLU + 3)))
                if more:
                    split_hi(act, 1, f * 16 + 16 * ((R_GLU + 2) // 2 + 1), 512)

            with act.Fori(0, 3) as f:
                pair(f, True)
            pair(3, False)

        def glu_dve(dve):
            for k in range(4):
                dve.wait_ge(on["y_hi"], count(k + 1))
                dve.tensor_tensor(y_lo[:, k, :], yraw[:, k, :], y_hi[:, k, :].bitcast(F32), ALU.subtract).then_inc(on["y_lo"], 1)
            split_lo(dve, 1, R_GLU + 1, 512)
            def pair(f, more):
                split_lo(dve, 0, f * 2 + (R_GLU + 2), 512)
                if more:
                    split_lo(dve, 1, f * 2 + (R_GLU + 3), 512)
                for c, (t0, tn) in enumerate(TCH):
                    dve.wait_ge(on["mm"], count(f * 6 + (MM_GLU + 3 + c + 1)))
                    dve.wait_ge(on["glu_sig"], count(f * 3 + (c + 1)))
                    a = ps[c][:, 0:tn * W5].rearrange("p (t w) -> p t w", w=W5)
                    b = sgb[:, t0 * W5:(t0 + tn) * W5].rearrange("p (t w) -> p t w", w=W5)
                    for w0, wn, first in ((0, NCH, 0), (SAMP5, SCH, SEQ)):
                        out = mixT[:, bass.ds(f, 1), first:first + wn * STEP].rearrange("p a (n t) -> p (a t) n", t=STEP)[:, t0:t0 + tn, :]
                        last = dve.tensor_tensor(out, a[:, :, w0:w0 + wn], b[:, :, w0:w0 + wn], ALU.mult)
                    last.then_inc(on["glu_mix"], 1)

            with dve.Fori(0, 3) as f:
                pair(f, True)
            pair(3, False)

        RQ, RK, DD, C1, C2, SSO, RS = 0, 1, 2, 3, 4, 5, 6
        f4 = lambda ap: ap.rearrange("p h c -> p (h c)")
        h4 = lambda bank: ps[bank][:].rearrange("p (h c) -> p h c", c=P)
        hb = lambda h, part: ps[h][:, part * P:(part + 1) * P]
        q_, k_, v_, z_ = 0, HEADS, 2 * HEADS, 3 * HEADS

        def gdn_pe(pe, t, s, loaded, st, ada, mod_at):
            pe.wait_ge(on["stg"][s], count(loaded))
            pe.wait_ge(on["g_mix"], count(t))
            pe.wait_ge(on["g_S"], count(t * HEADS))
            pe.wait_ge(on["mod_cols"], count(mod_at))
            for part, bank in ((q_, 4), (k_, 5), (v_, 6)):
                for h in range(HEADS):
                    last = pe.transpose(h4(bank)[:, h, :], stg[:, s, part + h, :], ident[:])
            last.then_inc(on["g_T"], 1)
            pe.wait_ge(on["g_U"], count(t + 1))
            pe.matmul(ps[7][:], ones[:], f4(gU[:]), start=True, stop=True).then_inc(on["g_row"], 1)
            for h in range(HEADS):
                pe.matmul(hb(h, 0), stg[:, s, k_ + h, :], stg[:, s, k_ + h, :], start=True, stop=True).then_inc(on["g_KK"], 1)
            pe.wait_ge(on["g_sq"], count(t * 2 + 1))
            for h in range(HEADS):
                last = pe.matmul(h4(4)[:, h, :], stg[:, s, k_ + h, :], stg[:, s, q_ + h, :], start=True, stop=True)
            last.then_inc(on["g_QKp"], 1)
            pe.wait_ge(on["g_kv8"], count(t * 2 + 1))
            for h in range(HEADS):
                pe.wait_ge(on["g_A"], count(t * HEADS + (h + 1)))
                last = pe.transpose(h4(5)[:, h, :], Am[:, h, :], ident[:])
            last.then_inc(on["g_AT"], 1)
            pe.wait_ge(on["g_X0"], count(t * 2 + 2))
            for l in range(LV):
                pe.wait_ge(on["g_L"], count(t * LV + (l + 1)))
                for h in range(HEADS):
                    if l:
                        pe.wait_ge(on["g_X"], count(t * (HEADS * LV) + ((l - 1) * HEADS + h + 1)))
                    pe.matmul(hb(h, 0), Lneg[:, l, h, :], Xb[:, h, 0, :], start=True, stop=True).then_inc(on["g_P"], 1)
                for h in range(HEADS):
                    pe.wait_ge(on["g_Pb"], count(t * (HEADS * LV) + (l * HEADS + h + 1)))
                    if l < LV - 1:
                        pe.matmul(hb(h, 1), Xb[:, h, 1, :], Pb[:, h, :], start=True, stop=True)
                    pe.matmul(hb(h, 2), Pb[:, h, :], Xb[:, h, 1, :], start=True, stop=True).then_inc(on["g_XX"], 1)
            pe.wait_ge(on["g_QK"], count(t + 1))
            pe.wait_ge(on["g_qd"], count(t + 1))
            for h in range(HEADS):
                pe.wait_ge(on["g_X"], count(t * (HEADS * LV) + ((LV - 1) * HEADS + h + 1)))
                pe.matmul(hb(h, 0), stg[:, s, k_ + h, :], Sst[:, st, h, :], start=True, stop=True).then_inc(on["g_kS"], 1)
            for h in range(HEADS):
                pe.wait_ge(on["g_R"], count(t * HEADS + (h + 1)))
                pe.matmul(hb(h, 3), Xb[:, h, 1, :], Rb[:, h, :], start=True, stop=True).then_inc(on["g_V"], 1)
            pe.wait_ge(on["g_ATs"], count(t + 1))
            pe.wait_ge(on["g_kv8"], count(t * 2 + 2))
            for h in range(HEADS):
                pe.wait_ge(on["g_Vb"], count(t * HEADS + (h + 1)))
                pe.matmul(h4(4)[:, h, :], qd[:, h, :], Sst[:, st, h, :], start=True, stop=False)
                pe.matmul(h4(4)[:, h, :], QK[:, h, :], Vb[:, h, :], start=False, stop=True)
                pe.matmul(hb(h, 0), kdec[:, h, :], Vb[:, h, :], start=True, stop=True).then_inc(on["g_kv"], 1)
            if ada is not None:
                pe.wait_ge(on["g_E"], count(t * 3 + 1))
                ada_chunk_pe(pe, ada[1], s)
            pe.wait_ge(on["g_ob"], count(t + 1))
            for h in range(HEADS):
                last = pe.transpose(h4(6)[:, h, :], ob[:, h, :], ident[:])
            last.then_inc(on["g_oT"], 1)
            if ada is not None:
                pe.wait_ge(on["mod_row"], alone(pe, count(ada[0] + 1)))
                for q in range(4):
                    last = pe.transpose(ps[5][:, 2 * q:2 * q + 2], modrow2[:, s, q * P:(q + 1) * P], ident[0:2, 0:2])
                last.then_inc(on["mod_T"], 1)

        def ada_chunk_pe(pe, loaded, s):
            pe.wait_ge(on["adb"][s], count(loaded))
            for k in range(KD):
                last = pe.matmul(ps[7][0:2, :], csil[:, k, :], wada2[:, s, k, :], start=(k == 0), stop=(k == KD - 1))
            last.then_inc(on["ada_mm"], 1)

        def gdn_act(act, t, s, ada):
            act.wait_ge(on["g_T"], count(t + 1))
            act.wait_ge(on["g_red"], count(t * 2))
            act.activation(sq[:, 0:HEADS, :], h4(4), ACT.Square)
            act.activation(sq[:, HEADS:, :], h4(5), ACT.Square).then_inc(on["g_sq"], 1)
            act.wait_ge(on["g_col"], count(t + 1))
            for h in range(HEADS):
                last = act.activation(kdec[:, h, :], h4(5)[:, h, :], ACT.Copy, scale=tilecol[:, s, KDEC, h:h + 1])
            last.then_inc(on["g_kv8"], 1)
            act.wait_ge(on["g_dd"], count(t + 1))
            act.activation(f4(erow[:]), ps[7][:], ACT.Exp).then_inc(on["g_E"], 1)
            act.wait_ge(on["g_mm"], count(t * 2 + 2))
            act.activation(EA[:], EA[:], ACT.Exp, scale=-1.0).then_inc(on["g_E"], 1)
            act.activation(EB[:], EB[:], ACT.Exp).then_inc(on["g_E"], 1)
            act.wait_ge(on["g_sc"], count(t + 1))
            for h in range(HEADS):
                last = act.activation(vp[:, h, :], h4(6)[:, h, :], ACT.Copy, scale=sc[:, C1, h:h + 1])
            last.then_inc(on["g_kv8"], 1)
            act.wait_ge(on["g_AT"], count(t + 1))
            act.activation(AT[:], h4(5), ACT.Copy).then_inc(on["g_ATs"], 1)
            for l in range(LV):
                for h in range(HEADS):
                    act.wait_ge(on["g_P"], count(t * (HEADS * LV) + (l * HEADS + h + 1)))
                    act.activation(Pb[:, h, :], hb(h, 0), ACT.Copy).then_inc(on["g_Pb"], 1)
            for h in range(HEADS):
                act.wait_ge(on["g_V"], count(t * HEADS + (h + 1)))
                act.activation(Vb[:, h, :], hb(h, 3), ACT.Copy).then_inc(on["g_Vb"], 1)
            act.wait_ge(on["g_kv"], count(t * HEADS + HEADS))
            act.activation(sq[:, 0:HEADS, :], h4(4), ACT.Square).then_inc(on["g_sq"], 1)
            if ada is not None:
                act.wait_ge(on["mod_row"], count(ada[0] + 1))
                act.dma_start(DR["mod"][:, bass.ds(ada[0] * ADA_N, ADA_N)], modrow2[:, s, :]).then_inc(on["mod_st"][s], 16)

        def gdn_pool(pool, t, s):
            pool.wait_ge(on["g_mix"], alone(pool, count(t)))
            pool.tensor_copy(tilecol[:, s, :, :], gcol[:, :, bass.ds(t, 1), :].rearrange("p n a h -> p n (a h)")).then_inc(on["g_col"], 1)
            pool.wait_ge(on["g_col"], alone(pool, count(t + 1)))
            pool.tensor_tensor(gU[:], bc(triu[:], 1, HEADS), bc(tilecol[:, s, GATE, :], 2, P), ALU.mult).then_inc(on["g_U"], 1)
            g = Steps(pool, on["g_pool"], t * 10)
            pool.wait_ge(on["g_red"], alone(pool, count(t * 2 + 1)))
            g(pool.tensor_scalar(sc[:, 0:2, :], sc[:, 7:9, :], RMS_EPS, None, ALU.add))
            g(pool.tensor_tensor(sc[:, 0:2, :], sc[:, 0:2, :], mhalf[:].rearrange("p (a b) -> p a b", a=2), ALU.pow))
            g(pool.tensor_tensor(sc[:, C1, :], sc[:, RK, :], tilecol[:, s, BETA, :], ALU.mult))
            g(pool.tensor_tensor(sc[:, DD, :], sc[:, C1, :], sc[:, RK, :], ALU.mult))
            g(pool.tensor_tensor(sc[:, C2, :], sc[:, DD, :], tilecol[:, s, NEXP, :], ALU.mult))
            g(pool.tensor_scalar(sc[:, RQ, :], sc[:, RQ, :], HD ** -0.5, None, ALU.mult))
            pool.tensor_tensor(sc[:, 9, :], sc[:, RQ, :], sc[:, RQ, :], ALU.mult).then_inc(on["g_sc"], 1)
            pool.wait_ge(on["g_E"], alone(pool, count(t * 3 + 3)))
            pool.tensor_tensor(EA[:], EA[:], bc(lower[:], 1, HEADS), ALU.mult).then_inc(on["g_EA"], 1)
            pool.tensor_tensor(EB[:], EB[:], bc(triu[:], 1, HEADS), ALU.mult).then_inc(on["g_EB"], 1)
            pool.wait_ge(on["g_ATs"], alone(pool, count(t + 1)))
            for l in range(LV):
                pool.tensor_tensor(Lneg[:, l, :, :], AT[:], bc(maskT[:, l + 1, :], 1, HEADS), ALU.mult).then_inc(on["g_L"], 1)
            pool.wait_ge(on["g_red"], alone(pool, count(t * 2 + 2)))
            pool.wait_ge(on["g_sc"], alone(pool, count(t + 1)))
            g(pool.tensor_tensor(sc[:, RS, :], sc[:, SSO, :], sc[:, 9, :], ALU.mult))
            g(pool.tensor_scalar(sc[:, RS, :], sc[:, RS, :], 1.0 / HD, RMS_EPS, ALU.mult, ALU.add))
            g(pool.tensor_tensor(sc[:, RS, :], sc[:, RS, :], mhalf[:, 0:HEADS], ALU.pow))
            g(pool.tensor_tensor(sc[:, RS, :], sc[:, RS, :], sc[:, RQ, :], ALU.mult))
            assert g.n == 10
            pool.tensor_copy(sc[:, 10, :], sc[:, RS, :]).then_inc(on["g_sc2"], 1)

        def gdn_dve(dve, t, s, st, first, n, ada):
            dve.wait_ge(on["g_sq"], count(t * 2 + 1))
            dve.wait_ge(on["g_sc2"], count(t))
            dve.tensor_reduce(sc[:, 7:9, :].rearrange("p a h -> p (a h)"), sq[:], mybir.AxisListType.X, ALU.add).then_inc(on["g_red"], 1)
            dve.wait_ge(on["g_row"], count(t + 1))
            dve.wait_ge(on["g_col"], count(t + 1))
            dve.tensor_tensor(dd[:], h4(7), bc(tilecol[:, s, DEC, :], 2, P), ALU.subtract).then_inc(on["g_dd"], 1)
            dve.wait_ge(on["g_dd"], count(t + 1))
            dve.tensor_scalar(EA[:], dd[:], 0.0, None, ALU.max).then_inc(on["g_mm"], 1)
            dve.tensor_scalar(EB[:], dd[:], 0.0, None, ALU.min).then_inc(on["g_mm"], 1)
            dve.wait_ge(on["g_sc"], count(t + 1))
            dve.wait_ge(on["g_EA"], count(t + 1))
            for h in range(HEADS):
                dve.wait_ge(on["g_KK"], count(t * HEADS + (h + 1)))
                dve.scalar_tensor_tensor(out=Am[:, h, :], in0=hb(h, 0), scalar=sc[:, DD, h:h + 1], in1=EA[:, h, :],
                                              op0=ALU.mult, op1=ALU.mult).then_inc(on["g_A"], 1)
            dve.wait_ge(on["g_EB"], count(t + 1))
            dve.wait_ge(on["g_QKp"], count(t + 1))
            dve.tensor_tensor(QK[:], h4(4), EB[:], ALU.mult).then_inc(on["g_QK"], 1)
            dve.tensor_tensor(qd[:], stg[:, s, 0:HEADS, :], erow[:], ALU.mult).then_inc(on["g_qd"], 1)
            dve.wait_ge(on["g_A"], count(t * HEADS + HEADS))
            dve.wait_ge(on["g_V"], count(t * HEADS))
            dve.tensor_tensor(Xb[:, :, 0, :], Am[:], bc(mask1[:], 1, HEADS), ALU.mult).then_inc(on["g_Xm"], 1)
            dve.wait_ge(on["g_Xm"], count(t * 2 + 1))
            dve.tensor_tensor(Xb[:, :, 0, :], Xb[:, :, 0, :], bc(ident[:], 1, HEADS), ALU.add).then_inc(on["g_X0"], 1)
            dve.wait_ge(on["g_ATs"], count(t + 1))
            dve.tensor_tensor(Xb[:, :, 1, :], AT[:], bc(maskT[:, 0, :], 1, HEADS), ALU.mult).then_inc(on["g_Xm"], 1)
            dve.wait_ge(on["g_Xm"], count(t * 2 + 2))
            dve.tensor_tensor(Xb[:, :, 1, :], Xb[:, :, 1, :], bc(ident[:], 1, HEADS), ALU.add).then_inc(on["g_X0"], 1)
            dve.wait_ge(on["g_X0"], count(t * 2 + 2))
            for l in range(LV):
                for h in range(HEADS):
                    dve.wait_ge(on["g_XX"], count(t * (HEADS * LV) + (l * HEADS + h + 1)))
                    dve.wait_ge(on["g_X"], count(t * (HEADS * LV) + max(0, l - 1) * HEADS + (h + 1 if l else 0)))
                    lo = 0 if l < LV - 1 else 1
                    src = ps[h][:, P:3 * P].rearrange("p (x c) -> p x c", x=2)
                    dve.tensor_tensor(Xb[:, h, lo:2, :], Xb[:, h, lo:2, :], src[:, lo:2, :], ALU.add).then_inc(on["g_X"], 1)
            dve.wait_ge(on["g_kv8"], count(t * 2 + 2))
            for h in range(HEADS):
                dve.wait_ge(on["g_kS"], count(t * HEADS + (h + 1)))
                dve.scalar_tensor_tensor(out=Rb[:, h, :], in0=hb(h, 0), scalar=sc[:, C2, h:h + 1], in1=vp[:, h, :],
                                              op0=ALU.mult, op1=ALU.add).then_inc(on["g_R"], 1)
            for h in range(HEADS):
                dve.wait_ge(on["g_kv"], count(t * HEADS + (h + 1)))
                dve.wait_ge(on["g_S"], count(t * HEADS))
                dve.scalar_tensor_tensor(out=Sst[:, st, h, :], in0=Sst[:, st, h, :], scalar=tilecol[:, s, GLAST, h:h + 1],
                                              in1=hb(h, 0), op0=ALU.mult, op1=ALU.add).then_inc(on["g_S"], 1)
            dve.wait_ge(on["g_sq"], count(t * 2 + 2))
            dve.tensor_reduce(sc[:, SSO, :], sq[:, 0:HEADS, :], mybir.AxisListType.X, ALU.add).then_inc(on["g_red"], 1)
            dve.wait_ge(on["g_sc2"], count(t + 1))
            dve.wait_ge(on["g_oT"], count(t))
            dve.tensor_tensor(ob[:], h4(4), bc(sc[:, 10, :], 2, P), ALU.mult).then_inc(on["g_ob"], 1)
            if ada is not None:
                dve.wait_ge(on["adb"][s], count(ada[1]))
                dve.wait_ge(on["ada_mm"], count(ada[0] + 1))
                dve.wait_ge(on["mod_st"][s], count(ada[2]))
                dve.tensor_tensor(modrow2[:, s, :], ps[7][0:2, :], bada2[:], ALU.add).then_inc(on["mod_row"], 1)
            dve.wait_ge(on["g_oT"], count(t + 1))
            out = mixT[:, HEADS:, first] if not isinstance(first, int) else mixT[:, HEADS:, first:first + n]
            dve.scalar_tensor_tensor(out=out, in0=h4(6)[:, :, 0:n], scalar=normg[:, 0:1], in1=stg[:, s, z_:, 0:n],
                                          op0=ALU.mult, op1=ALU.mult).then_inc(on["g_mix"], 1)
            if ada is not None:
                dve.wait_ge(on["mod_T"], count(ada[0] + 1))
                dve.tensor_copy(modc[:, bass.ds(ada[0], 1), :, :].rearrange("p c q t -> p (c q) t"),
                                     ps[5][:, 0:8].rearrange("p (q t) -> p q t", t=2)).then_inc(on["mod_cols"], 1)

        R_WO = R_GLU + 8
        R_FF = R_WO + KD
        MM_FF = MM_GLU + 3 * 8
        G1_AT, G2_AT = 2 * D_MODEL, 5 * D_MODEL

        def wo_steps(eng, step):
            step(0, 0)
            step(1, 1)
            with eng.Fori(0, 2) as i:
                for s in range(2):
                    step(i * 2 + (2 + s), s)
            for t in range(6, TILES):
                step(t, t % 2)

        def tile_rows(t):
            return DEC_SEQ if isinstance(t, int) and t == PTILES else P

        def tile_cols(t):
            return bass.ds(t * P, P) if not isinstance(t, int) else slice(t * P, t * P + tile_rows(t))

        def wo_pe(pe):
            pe.wait_ge(on["g_mix"], TILES)

            def transposes(u, s):
                n = tile_rows(u)
                pe.wait_ge(on["o_n2"], since("o_n2", u + 1))
                pe.wait_ge(on["h2_mod"], since("h2_mod", u))
                for k in range(KD):
                    last = pe.transpose(ps[4 + k // 4][:, (k % 4) * P:(k % 4) * P + n], xn2[0:n, s, k * P:(k + 1) * P], ident[0:n, 0:n])
                last.then_inc(on["o_T"], 1)

            def step(t, s):
                n = tile_rows(t)
                pe.wait_ge(on["ms_lo"], since("ms_lo", t + 1))
                pe.wait_ge(on["o_tmp"], since("o_tmp", t * 2 - 2))
                for k in range(KD):
                    pe.wait_ge(on["w_lo"], count(R_WO + k + 1))
                    for h in range(2):
                        cols = slice(h * 512, (h + 1) * 512)
                        for m, (a, w) in enumerate(((whi, wo_hi), (whi, wo_lo), (wlo, wo_hi))):
                            last = pe.matmul(ps[2 * s + h][0:n, :], a[:, s, k * P:k * P + n], w[:, k, cols],
                                             start=(k == 0 and m == 0), stop=(k == KD - 1 and m == 2))
                last.then_inc(on["wo_mm"], 1)
                if not (isinstance(t, int) and t < 2):
                    transposes(t - 2, s)

            wo_steps(pe, step)
            transposes(PTILES - 1, 1)
            transposes(PTILES, 0)

        def tile_hi(act, t, s):
            n = tile_rows(t)
            act.wait_ge(on["wo_mm"], since("wo_mm", t - 1))
            act.activation(whi[:, s, :].rearrange("p (k c) -> p k c", c=P)[:, :, 0:n], mixT[:, :, tile_cols(t)], ACT.Copy).then_inc(on["ms_hi"], 1)

        def tile_lo(dve, t, s):
            n = tile_rows(t)
            v = lambda x: x[:, s, :].rearrange("p (k c) -> p k c", c=P)[:, :, 0:n]
            dve.wait_ge(on["ms_hi"], since("ms_hi", t + 1))
            dve.tensor_tensor(v(wlo), mixT[:, :, tile_cols(t)], v(whi).bitcast(F32), ALU.subtract).then_inc(on["ms_lo"], 1)

        def normalise(act, out, in_, n, rs, name):
            act.activation(out, in_, ACT.Identity, bias=rstd[0:n, rs, 1:2], scale=rstd[0:n, rs, 0:1]).then_inc(name, 1)

        def wo_act(act):
            act.wait_ge(on["g_mix"], TILES)
            for t in range(2):
                tile_hi(act, t, t)
            for k in range(KD):
                r = R_WO + k
                act.wait_ge(on["raw"][r % 2], count(16 * (r // 2 + 1)))
                act.activation(wo_hi[:, k, :], wraw[:, r % 2, :], ACT.Copy).then_inc(on["w_hi"], 1)

            def modulate(u):
                n, tok = tile_rows(u), 0 if tile_rows(u) == P else 1
                act.wait_ge(on["h2_lo"], since("h2_lo", u))
                act.wait_ge(on["h2_scale"], 1)
                act.wait_ge(on["o_T"], since("o_T", u + 1))
                for k in range(KD):
                    last = act.activation(hp2[:, k, 0:n], ps[4 + k // 4][:, (k % 4) * P:(k % 4) * P + n], ACT.Identity,
                                          scale=onep[:, 1, k, tok:tok + 1], bias=modc[:, 6 + k // 4, k % 4, tok:tok + 1])
                last.then_inc(on["h2_mod"], 1)

            def step(t, s):
                n = tile_rows(t)
                if not (isinstance(t, int) and t < 2):
                    modulate(t - 2)
                if not (isinstance(t, int) and t > PTILES - 2):
                    tile_hi(act, t + 2, s)
                act.wait_ge(on["o_rs"], since("o_rs", t * 2 + 1))
                act.wait_ge(on["o_bn"], since("o_bn", t * 4 + 2))
                normalise(act, xt[0:n, s, :], xt[0:n, s, :], n, 0, on["o_n1"])
                act.wait_ge(on["o_rs"], since("o_rs", t * 2 + 2))
                act.wait_ge(on["x1_ready"], since("x1_ready", t + 1))
                act.wait_ge(on["o_T"], since("o_T", t - 1))
                normalise(act, xn2[0:n, s, :], xt[0:n, s, :], n, 1, on["o_n2"])

            wo_steps(act, step)
            modulate(PTILES - 1)
            modulate(PTILES)

        def wo_dve(dve):
            dve.wait_ge(on["mod_cols"], 12)
            dve.tensor_scalar(onep[:, 1, :, :], modc[:, 8:10, :, :].rearrange("p a q t -> p (a q) t"), 1.0, None, ALU.add).then_inc(on["h2_scale"], 1)
            for t in range(2):
                tile_lo(dve, t, t)
            dve.wait_ge(on["mod_st"][0], 64)
            dve.wait_ge(on["mod_st"][1], 64)
            dve.wait_ge(on["state_out"], 32)
            for k in range(KD):
                dve.wait_ge(on["w_hi"], count(R_WO + k + 1))
                dve.tensor_tensor(wo_lo[:, k, :], wraw[:, (R_WO + k) % 2, :], wo_hi[:, k, :].bitcast(F32), ALU.subtract).then_inc(on["w_lo"], 1)

            def stats(x, n, slot, bn, name):
                for h in range(2):
                    dve.bn_stats(stat[0:n, slot, 6 * h:6 * h + 6], x[:, h * 512:(h + 1) * 512]).then_inc(on["o_bn"], 1)
                dve.wait_ge(on["o_bn"], alone(dve, since("o_bn", bn)))
                dve.bn_aggr(stat[0:n, slot, 12:14], stat[0:n, slot, 0:12]).then_inc(name, 1)

            def split_h2(u):
                n = tile_rows(u)
                dve.wait_ge(on["h2_mod"], since("h2_mod", u + 1))
                dve.tensor_copy(hT_hi[:, :, tile_cols(u)], hp2[:, :, 0:n]).then_inc(on["h2_hi"], 1)
                dve.wait_ge(on["h2_hi"], since("h2_hi", u + 1))
                dve.tensor_tensor(hT_lo[:, :, tile_cols(u)], hp2[:, :, 0:n], hT_hi[:, :, tile_cols(u)].bitcast(F32), ALU.subtract).then_inc(on["h2_lo"], 1)

            def step(t, s):
                n = tile_rows(t)
                dve.wait_ge(on["wo_mm"], since("wo_mm", t + 1))
                dve.wait_ge(on["o_g1"], since("o_g1", 2 if n < P else 1))
                dve.wait_ge(on["o_r"], since("o_r", t))
                for h in range(2):
                    dve.tensor_tensor(otmp[0:n, h * 512:(h + 1) * 512], ps[2 * s + h][0:n, :], g1r[0:n, h * 512:(h + 1) * 512], ALU.mult).then_inc(on["o_tmp"], 1)
                dve.wait_ge(on["o_tmp"], since("o_tmp", t * 2 + 2))
                dve.wait_ge(on["xt"][s], count((t - s) * 8 + 16))
                dve.scalar_tensor_tensor(out=xt[0:n, s, :], in0=xt[0:n, s, :], scalar=ALPHA, in1=otmp[0:n, :],
                                              op0=ALU.mult, op1=ALU.add).then_inc(on["o_r"], 1)
                dve.wait_ge(on["o_r"], since("o_r", t + 1))
                stats(xt[0:n, s, :], n, 0, t * 4 + 2, on["o_mv"])
                if not (isinstance(t, int) and t < 2):
                    split_h2(t - 2)
                dve.wait_ge(on["o_n1"], since("o_n1", t + 1))
                dve.wait_ge(on["ln1_rows"], 32)
                dve.tensor_tensor(xt[0:n, s, :], xt[0:n, s, :], ln1r[0:n, 0, :], ALU.mult).then_inc(on["o_xg"], 1)
                if not (isinstance(t, int) and t > PTILES - 2):
                    tile_lo(dve, t + 2, s)
                dve.wait_ge(on["x1_ready"], since("x1_ready", t + 1))
                stats(xt[0:n, s, :], n, 1, t * 4 + 4, on["o_mv"])

            wo_steps(dve, step)
            split_h2(PTILES - 1)
            split_h2(PTILES)

        def rstd_steps(pool, g, n, slot, eps, name):
            g(pool.tensor_scalar(rstd[0:n, slot, 0:1], stat[0:n, slot, 13:14], eps, None, ALU.add))
            g(pool.tensor_tensor(rstd[0:n, slot, 0:1], rstd[0:n, slot, 0:1], mhalf[0:n, 0:1], ALU.pow))
            pool.tensor_scalar(rstd[0:n, slot, 1:2], stat[0:n, slot, 12:13], rstd[0:n, slot, 0:1], -1.0, ALU.mult, ALU.mult).then_inc(name, 1)

        def wo_pool(pool):
            pool.wait_ge(on["g1_row"], 16)
            pool.tensor_scalar(g1r[:], g1r[:], 1.0, None, ALU.add).then_inc(on["o_g1"], 1)

            def step(t, s):
                n = tile_rows(t)
                g = Steps(pool, on["o_p"], since("o_p", t * 4))
                pool.wait_ge(on["o_mv"], alone(pool, since("o_mv", t * 2 + 1)))
                pool.wait_ge(on["o_n1"], alone(pool, since("o_n1", t)))
                rstd_steps(pool, g, n, 0, LN_EPS, on["o_rs"])
                pool.wait_ge(on["o_xg"], alone(pool, since("o_xg", t + 1)))
                pool.tensor_tensor(xt[0:n, s, :], xt[0:n, s, :], ln1r[0:n, 1, :], ALU.add).then_inc(on["x1_ready"], 1)
                pool.wait_ge(on["o_mv"], alone(pool, since("o_mv", t * 2 + 2)))
                pool.wait_ge(on["o_n2"], alone(pool, since("o_n2", t)))
                rstd_steps(pool, g, n, 1, LN_EPS, on["o_rs"])
                if isinstance(t, int) and t == PTILES - 1:
                    pool.wait_ge(on["g1_row"], 32)
                    pool.tensor_scalar(g1r[0:DEC_SEQ, :], g1r[0:DEC_SEQ, :], 1.0, None, ALU.add).then_inc(on["o_g1"], 1)

            wo_steps(pool, step)

        def mod_row_of(stream, at_col, n):
            return DR["mod"][stream:stream + 1, at_col:at_col + D_MODEL].to_broadcast([n, D_MODEL])

        def wo_loads(sp):
            sp.wait_ge(on["mod_cols"], 12)
            sp.wait_ge(on["g_mix"], TILES)
            sp.wait_ge(on["mod_st"][0], 16)
            sp.wait_ge(on["mod_st"][1], 16)
            sp.dma_start(g1r[:], mod_row_of(0, G1_AT, P)).then_inc(on["g1_row"], 16)
            for s in range(2):
                sp.dma_start(xt[:, s, :], I["x_prompt"][s * P:(s + 1) * P, :]).then_inc(on["xt"][s], 16)
            for n in range(2):
                sp.dma_start(ln1r[:, n, :], I["ln_rows"][n:n + 1, :].to_broadcast([P, D_MODEL])).then_inc(on["ln1_rows"], 16)
            for k in range(2, KD):
                sp.wait_ge(on["w_lo"], count(R_WO + k - 1))
                sp.dma_start(wraw[:, (R_WO + k) % 2, :], I["w_out"][k * P:(k + 1) * P, :]).then_inc(on["raw"][(R_WO + k) % 2], 16)
            for q in range(2):
                up_load(sp, 0, q)

            def step(t, s):
                n = tile_rows(t)
                sp.wait_ge(on["x1_ready"], since("x1_ready", t + 1))
                sp.dma_start(DR["x1"][tile_cols(t), :], xt[0:n, s, :]).then_inc(on["x1_st"][s], 16)
                sp.wait_ge(on["o_n2"], since("o_n2", t + 1))
                sp.wait_ge(on["x1_st"][s], count((t - s) * 8 + 16))
                if isinstance(t, int) and t >= PTILES - 2:
                    if t == PTILES - 2:
                        sp.dma_start(xt[0:DEC_SEQ, 0, :], I["x_sample"]).then_inc(on["xt"][0], 16)
                    elif t == PTILES - 1:
                        sp.wait_ge(on["o_tmp"], since("o_tmp", 2 * PTILES))
                        sp.dma_start(g1r[0:DEC_SEQ, :], mod_row_of(1, G1_AT, DEC_SEQ)).then_inc(on["g1_row"], 16)
                else:
                    nxt = bass.ds(t * P + 2 * P, P) if not isinstance(t, int) else slice((t + 2) * P, (t + 3) * P)
                    sp.dma_start(xt[:, s, :], I["x_prompt"][nxt, :]).then_inc(on["xt"][s], 16)

            wo_steps(sp, step)

        FI = FB // 2
        wup = I["w_up"].rearrange("(k p) n -> p k n", p=P)
        slot_of = lambda j: (R_FF + j) % 2
        loaded = lambda i, j: i * 48 + 16 * ((R_FF + j) // 2 + 1)

        def up_load(sp, i, j):
            sl = slot_of(j)
            sp.wait_ge(on["w_lo"], alone(sp, count(i * 6 + (R_FF + j - 1))))
            if j < 4:
                col = i * 2 * P + ((j // 2) * P + (j % 2) * D_FF)
                cols = slice(col, col + P) if isinstance(col, int) else bass.ds(col, P)
                sp.dma_start(wraw[:, sl, :].rearrange("p (k n) -> p k n", k=KD), wup[:, :, cols]).then_inc(on["raw"][sl], 16)
            else:
                row = i * 2 * P + (j - 4) * P
                rows = slice(row, row + P) if isinstance(row, int) else bass.ds(row, P)
                sp.dma_start(wraw[:, sl, :], I["w_down"][rows, :]).then_inc(on["raw"][sl], 16)

        def ffn_loads(sp):
            sp.wait_ge(on["wo_mm"], since("wo_mm", TILES))
            for j in range(2, 6):
                up_load(sp, 0, j)
            sp.wait_ge(on["x1_st"][0], 16 * (PTILES // 2 + 1))
            sp.wait_ge(on["x1_st"][1], 16 * (PTILES // 2))
            sp.wait_ge(on["x1_ready"], since("x1_ready", TILES))
            sp.wait_ge(on["mod_st"][0], 64)
            sp.wait_ge(on["mod_st"][1], 64)
            sp.dma_start(acc[:, 0:PTILES, :], DR["x1"][0:SEQ, :].rearrange("(t p) n -> p t n", p=P)).then_inc(on["acc_in"], 16)
            sp.dma_start(acc[0:DEC_SEQ, PTILES, :], DR["x1"][SEQ:TOK, :]).then_inc(on["acc_in"], 16)
            sp.dma_start(g2r[:, 0, :], mod_row_of(0, G2_AT, P)).then_inc(on["g2_row"], 16)
            sp.dma_start(g2r[0:DEC_SEQ, 1, :], mod_row_of(1, G2_AT, DEC_SEQ)).then_inc(on["g2_row"], 16)
            with sp.Fori(1, FI) as i:
                for j in range(6):
                    up_load(sp, i, j)
            sp.wait_ge(on["mm"], MM_FF + 12 * FI)
            for n in range(2):
                sp.dma_start(ln2r[:, n, :], I["ln_rows"][2 + n:3 + n, :].to_broadcast([P, D_MODEL])).then_inc(on["ln2_rows"], 16)
            with sp.Fori(0, PTILES) as t:
                sp.wait_ge(on["y_ready"], since("y_ready", t + 1))
                sp.dma_start(O["y_prompt"][bass.ds(t * P, P), :], acc[:, bass.ds(t, 1), :].rearrange("p a n -> p (a n)")).then_inc(on["out"], 16)
            sp.wait_ge(on["y_ready"], since("y_ready", TILES))
            sp.dma_start(O["y_sample"], acc[0:DEC_SEQ, PTILES, :]).then_inc(on["out"], 16)

        def ffn_pool(pool):
            pool.wait_ge(on["g2_row"], 32)
            pool.tensor_scalar(g2r[:, 0, :], g2r[:, 0, :], 1.0, 1.0 / ALPHA, ALU.add, ALU.mult).then_inc(on["f_g2"], 1)
            pool.tensor_scalar(g2r[0:DEC_SEQ, 1, :], g2r[0:DEC_SEQ, 1, :], 1.0, 1.0 / ALPHA, ALU.add, ALU.mult).then_inc(on["f_g2"], 1)
            pool.wait_ge(on["ln2_rows"], 32)

            def step(t, s, n):
                a = acc_tile(t, n)
                g = Steps(pool, on["f_p"], since("f_p", t * 2))
                pool.wait_ge(on["f_mv"], alone(pool, count(t + 1)))
                pool.wait_ge(on["f_n"], alone(pool, count(t - 1 if isinstance(t, int) else t)))
                rstd_steps(pool, g, n, s, LN_EPS / ALPHA ** 2, on["f_rs"])
                pool.wait_ge(on["f_xg"], alone(pool, count(t + 1)))
                pool.tensor_tensor(a, a, ln2r[0:n, 1, :], ALU.add).then_inc(on["y_ready"], 1)

            final_steps(pool, step)

        def acc_tile(t, n):
            return acc[0:n, t, :] if isinstance(t, int) else acc[0:n, bass.ds(t, 1), :].rearrange("p a n -> p (a n)")

        def final_steps(eng, step):
            with eng.Fori(0, PTILES // 2) as i:
                for s in range(2):
                    step(i * 2 + s, s, P)
            step(PTILES, 0, DEC_SEQ)

        def ffn_down_pe(pe, i):
            pe.wait_ge(on["w_lo"], count(i * 6 + R_FF))
            pe.wait_ge(on["f_lo"], since("f_lo", i * 6))
            for t in range(TILES):
                n = tile_rows(t)
                cols = slice(t * P, t * P + n)
                for h in range(2):
                    pe.wait_ge(on["f_tmp"], count(i * 2 * TILES + (t * 2 + h - 2 * TILES - (1 if t + h else 0))))
                    for b in range(2):
                        for m, (a, w) in enumerate(((hid_hi, wd_hi), (hid_hi, wd_lo), (hid_lo, wd_hi))):
                            last = pe.matmul(ps[6 + h][0:n, :], a[:, b, cols], w[:, b, h * 512:(h + 1) * 512],
                                             start=(b == 0 and m == 0), stop=(b == 1 and m == 2))
                    last.then_inc(on["f_dn"], 1)

        def ffn_pe(pe):
            def block(i, j, first=False):
                def bank_free(c):
                    if first:
                        pe.wait_ge(on["o_tmp"], since("o_tmp", 2 * TILES))
                        pe.wait_ge(on["h2_lo"], since("h2_lo", min(TILES, 3 * (c + 1))))
                    if j % 2 == 0:
                        pe.wait_ge(on["f_sil"], count(i * 6 + (3 * (j // 2) + c - 2)))
                    else:
                        pe.wait_ge(on["f_mul"], since("f_mul", i * 6 + (3 * (j // 2) + c - 2)))
                proj_block(pe, slot_of(j), i * 6 + (R_FF + j + 1), (0, 1, 2) if j % 2 == 0 else (3, 4, 5),
                           bank_free, hT_hi, hT_lo)

            for j in range(4):
                if j == 1:
                    pe.wait_ge(on["h2_mod"], since("h2_mod", TILES))
                block(0, j, j == 0)
            with pe.Fori(1, FI) as i:
                block(i, 0)
                ffn_down_pe(pe, i)
                for j in range(1, 4):
                    block(i, j)
            ffn_down_pe(pe, FI)

        def ffn_act(act):
            def hi(i, j):
                act.wait_ge(on["mm"], count(i * 12 + (MM_FF + 3 * (j - 1))))
                split_hi(act, slot_of(j), loaded(i, j))

            def silu(i, b):
                for c, (c0, cw) in enumerate(CH):
                    act.wait_ge(on["f_lo"], since("f_lo", i * 6 + (3 * b - 3 + c + 1)))
                    act.wait_ge(on["mm"], count(i * 12 + (MM_FF + 6 * b + c + 1)))
                    act.activation(sil[:, c0:c0 + cw], ps[c][:, 0:cw], ACT.Silu).then_inc(on["f_sil"], 1)

            def hidden_hi(i, b):
                act.wait_ge(on["f_dn"], since("f_dn", i * 2 * TILES))
                for c, (c0, cw) in enumerate(CH):
                    act.wait_ge(on["f_mul"], since("f_mul", i * 6 + (3 * b + c + 1)))
                    act.activation(hid_hi[:, b, c0:c0 + cw], sil[:, c0:c0 + cw], ACT.Copy).then_inc(on["f_hi"], 1)

            def turn(i, more):
                hi(i, 1)
                silu(i, 0)
                hi(i, 2)
                hidden_hi(i, 0)
                hi(i, 3)
                silu(i, 1)
                for b in range(2):
                    sl = slot_of(4 + b)
                    act.wait_ge(on["raw"][sl], count(loaded(i, 4 + b)))
                    act.wait_ge(on["f_dn"], since("f_dn", i * 2 * TILES))
                    act.activation(wd_hi[:, b, :], wraw[:, sl, :], ACT.Copy).then_inc(on["w_hi"], 1)
                if more:
                    hi(i + 1, 0)
                hidden_hi(i, 1)

            act.wait_ge(on["wo_mm"], since("wo_mm", TILES - 1))
            hi(0, 0)
            act.wait_ge(on["wo_mm"], since("wo_mm", TILES))
            turn(0, True)
            with act.Fori(1, FI - 1) as i:
                turn(i, True)
            turn(FI - 1, False)

            def step(t, s, n):
                act.wait_ge(on["f_rs"], since("f_rs", t + 1))
                a = acc_tile(t, n)
                normalise(act, a, a, n, s, on["f_n"])

            final_steps(act, step)

        def ffn_dve(dve):
            def lo(i, j):
                split_lo(dve, slot_of(j), i * 6 + (R_FF + j + 1))

            def down_tile(i, t):
                n = tile_rows(t)
                row = g2r[0:n, 1 if n < P else 0, :]
                for h in range(2):
                    cols, k = slice(h * 512, (h + 1) * 512), t * 2 + h - 2 * TILES
                    dve.wait_ge(on["f_dn"], since("f_dn", i * 2 * TILES + (k + 1)))
                    dve.wait_ge(on["f_add"], count(i * 2 * TILES + (k - (1 if t + h else 0))))
                    dve.tensor_tensor(dtmp[0:n, cols], ps[6 + h][0:n, :], row[:, cols], ALU.mult).then_inc(on["f_tmp"], 1)
                for h in range(2):
                    cols, k = slice(h * 512, (h + 1) * 512), t * 2 + h - 2 * TILES
                    dve.wait_ge(on["f_tmp"], count(i * 2 * TILES + (k + 1)))
                    dve.tensor_tensor(acc[0:n, t, cols], acc[0:n, t, cols], dtmp[0:n, cols], ALU.add).then_inc(on["f_add"], 1)

            def multiply(i, b):
                for c, (c0, cw) in enumerate(CH):
                    dve.wait_ge(on["f_sil"], count(i * 6 + (3 * b + c + 1)))
                    dve.wait_ge(on["mm"], count(i * 12 + (MM_FF + 6 * b + 3 + c + 1)))
                    dve.tensor_tensor(sil[:, c0:c0 + cw], sil[:, c0:c0 + cw], ps[3 + c][:, 0:cw], ALU.mult).then_inc(on["f_mul"], 1)

            def hidden_lo(i, b):
                for c, (c0, cw) in enumerate(CH):
                    dve.wait_ge(on["f_hi"], since("f_hi", i * 6 + (3 * b + c + 1)))
                    dve.tensor_tensor(hid_lo[:, b, c0:c0 + cw], sil[:, c0:c0 + cw], hid_hi[:, b, c0:c0 + cw].bitcast(F32),
                                           ALU.subtract).then_inc(on["f_lo"], 1)

            def turn(i, down, more):
                lo(i, 1)
                if down:
                    for t in range(TILES):
                        down_tile(i, t)
                lo(i, 2)
                multiply(i, 0)
                hidden_lo(i, 0)
                lo(i, 3)
                for b in range(2):
                    dve.wait_ge(on["w_hi"], count(i * 6 + (R_FF + 5 + b)))
                    dve.tensor_tensor(wd_lo[:, b, :], wraw[:, slot_of(4 + b), :], wd_hi[:, b, :].bitcast(F32), ALU.subtract).then_inc(on["w_lo"], 1)
                if more:
                    lo(i + 1, 0)
                multiply(i, 1)
                hidden_lo(i, 1)

            lo(0, 0)
            turn(0, False, True)
            dve.wait_ge(on["acc_in"], 32)
            dve.wait_ge(on["f_g2"], since("f_g2", 2))
            with dve.Fori(1, FI - 1) as i:
                turn(i, True, True)
            turn(FI - 1, True, False)
            for t in range(TILES + 1):
                if t < TILES:
                    n, s = tile_rows(t), t % 2
                    down_tile(FI, t)
                    dve.wait_ge(on["f_add"], count(2 * TILES * (FI - 1) + 2 * t + 2))
                    dve.wait_ge(on["f_rs"], since("f_rs", t - 1))
                    for h in range(2):
                        dve.bn_stats(stat[0:n, s, 6 * h:6 * h + 6], acc[0:n, t, h * 512:(h + 1) * 512]).then_inc(on["f_bn"], 1)
                    dve.wait_ge(on["f_bn"], count(t * 2 + 2))
                    dve.bn_aggr(stat[0:n, s, 12:14], stat[0:n, s, 0:12]).then_inc(on["f_mv"], 1)
                if t:
                    u = t - 1
                    n = tile_rows(u)
                    dve.wait_ge(on["ln2_rows"], 32)
                    dve.wait_ge(on["f_n"], count(u + 1))
                    dve.tensor_tensor(acc[0:n, u, :], acc[0:n, u, :], ln2r[0:n, 0, :], ALU.mult).then_inc(on["f_xg"], 1)

        block = ctx.enter_context(nc.Block())

        @block.sync
        def _(sp):
            loads_before(sp)
            loads_projection(sp)
            wglu = I["w_glu"].rearrange("(k p) n -> p k n", p=P)

            def glu_piece(slot, col, free):
                sp.wait_ge(on["w_lo"], alone(sp, count(free)))
                sp.dma_start(wraw[:, slot, 0:512].rearrange("p (k n) -> p k n", k=4), wglu[:, :, col]).then_inc(on["raw"][slot], 16)

            glu_piece(1, slice(512, 640), R_GLU - 1)
            sp.wait_ge(on["y_stored"], NB5 * STEP * 16)
            sp.wait_ge(on["row_stored"][0], 2 * NB5 * 16)
            sp.wait_ge(on["row_stored"][1], 2 * NB5 * 16)
            sp.wait_ge(on["s5_h"], NB5)
            for k in range(4):
                sp.dma_start(yraw[:, k, :].rearrange("p (t w) -> p t w", t=STEP), DR["y"][k * GB:(k + 1) * GB].rearrange("g i t w -> (g i) t w")).then_inc(on["y"][k], 16)
            glu_piece(0, slice(0, P), R_GLU)
            with sp.Fori(1, 4) as f:
                glu_piece(1, bass.ds(f * P + 512, P), f * 2 + (R_GLU - 1))
                glu_piece(0, bass.ds(f * P, P), f * 2 + R_GLU)
            sp.wait_ge(on["gate_T"], 1)
            rows = DR["rows"].rearrange("a p w -> p a w")

            def ada_load(c, s):
                sp.wait_ge(on["ada_mm"], count(c - 1))
                sp.dma_start(wada2[:, s, :, :], wad[:, :, bass.ds(c * ADA_N, ADA_N)]).then_inc(on["adb"][s], 16)
                sp.wait_ge(on["mod_row"], count(c))
                sp.dma_start(bada2[:], I["b_ada"][:, bass.ds(c * ADA_N, ADA_N)]).then_inc(on["adb"][s], 16)

            for s in range(2):
                sp.dma_start(stg[:, s, :, :], rows[:, :, s * P:(s + 1) * P]).then_inc(on["stg"][s], 16)
                ada_load(4 + s, s)
            for k in range(2):
                sp.wait_ge(on["w_lo"], count(R_WO + k - 1))
                sp.dma_start(wraw[:, (R_WO + k) % 2, :], I["w_out"][k * P:(k + 1) * P, :]).then_inc(on["raw"][(R_WO + k) % 2], 16)
            sp.wait_ge(on["glu_mix"], 12)
            sp.dma_start(Sst[:, 1, :, :], I["state_gdn"].rearrange("h k v -> k h v")).then_inc(on["s_state"], 16)
            with sp.Fori(1, PTILES // 2) as i:
                for s in range(2):
                    sp.wait_ge(on["g_mix"], count(i * 2 + (s - 1)))
                    sp.dma_start(stg[:, s, :, :], rows[:, :, bass.ds(i * 2 * P + s * P, P)]).then_inc(on["stg"][s], 16)
                    ada_load(i * 2 + (4 + s), s)
            sp.wait_ge(on["g_mix"], PTILES - 1)
            sp.dma_start(stg[:, 0, :, :], rows[:, :, SAMP_COL:SAMP_COL + P]).then_inc(on["stg"][0], 16)
            sp.wait_ge(on["g_S"], PTILES * HEADS)
            sp.dma_start(O["gdn_states"][0].rearrange("h k v -> k h v"), Sst[:, 0, :, :]).then_inc(on["state_out"], 16)
            sp.wait_ge(on["g_S"], TILES * HEADS)
            sp.dma_start(O["gdn_states"][1].rearrange("h k v -> k h v"), Sst[:, 1, :, :]).then_inc(on["state_out"], 16)
            sp.dma_start(O["s5_states"], hout[:]).then_inc(on["out"], 16)
            sp.dma_start(O["conv_tails"], rawtail[:]).then_inc(on["out"], 16)
            wo_loads(sp)
            ffn_loads(sp)
            sp.wait_ge(on["out"], 16 * (2 + TILES))

        @block.gpsimd
        def _(pool):
            n0 = masks(pool)
            pool.wait_ge(on["small"], 16 * len(SMALL))
            pool.wait_ge(on["halfpi"], 1)
            n0, trigs = s5_tables(pool, n0)

            def reciprocal_std(s, rows, tile, used):
                pool.wait_ge(on["ln_mv"], alone(pool, count(tile + 1)))
                pool.wait_ge(on["x_norm"][s], alone(pool, count(used)))
                pool.tensor_scalar(rstd[0:rows, s, 0:1], stat[0:rows, s, 13:14], LN_EPS, None, ALU.add).then_inc(on["ln_r"], 1)
                pool.wait_ge(on["ln_r"], alone(pool, count(tile * 2 + 1)))
                pool.tensor_tensor(rstd[0:rows, s, 0:1], rstd[0:rows, s, 0:1], mhalf[0:rows, 0:1], ALU.pow).then_inc(on["ln_r"], 1)
                pool.wait_ge(on["ln_r"], alone(pool, count(tile * 2 + 2)))
                pool.tensor_scalar(rstd[0:rows, s, 1:2], stat[0:rows, s, 12:13], rstd[0:rows, s, 0:1], -1.0,
                                        ALU.mult, ALU.mult).then_inc(on["ln_rs"], 1)

            with pool.Fori(0, PTILES // 2) as i:
                for s in range(2):
                    reciprocal_std(s, P, i * 2 + s, i)
            reciprocal_std(0, DEC_SEQ, PTILES, PTILES // 2)
            pool.wait_ge(on["h_lo"], TILES)
            pool.wait_ge(on["mod_cols"], 4)
            for t in (urow, convrow, Mt, bas):
                pool.memset(t[:], 0.0).then_inc(on["cleared"], 1)
            pool.memset(rawrow[:, 0:GAP], 0.0).then_inc(on["cleared"], 1)
            with pool.Fori(0, NB5) as b:
                n = s5_batch_tables(pool, b, n0, 56, trigs)
                assert n == 56, n
            pool.wait_ge(on["glu_mix"], 12)
            pool.wait_ge(on["gates"], 1)
            pool.memset(Sst[:, 0, :, :], 0.0).then_inc(on["g_init"], 1)
            with pool.Fori(0, PTILES // 2) as i:
                for s in range(2):
                    gdn_pool(pool, i * 2 + s, s)
            gdn_pool(pool, PTILES, 0)
            wo_pool(pool)
            ffn_pool(pool)

        @block.tensor
        def _(pe):
            pe.wait_ge(on["masks"], 1)
            pe.wait_ge(on["c_silu"], 1)
            for c in range(4):
                if c:
                    pe.wait_ge(on["mod_cols"], count(c))
                ada_mm(pe, c, c % 2, 32 * (c // 2 + 1), c + 1, 4 + c % 2)
            with pe.Fori(0, PTILES // 2) as i:
                for s in range(2):
                    ln_transpose(pe, s, i + 1, i * 2, P)
            ln_transpose(pe, 0, PTILES // 2 + 1, PTILES - 1, DEC_SEQ)
            pe.wait_ge(on["h_lo"], TILES)
            for n in range(NU):
                in_block(pe, n % 2, n)
            with pe.Fori(0, NB5) as b:
                for j in range(4):
                    in_block(pe, j % 2, b * 4 + (NU + j))
                    if j == 1:
                        s5_A(pe, b)
                    if j == 2:
                        s5_Z(pe, b)
                    if j == 3:
                        s5_Y(pe, b)
            gates_pe(pe)
            glu_pe(pe)
            pe.wait_ge(on["g_init"], 1)
            with pe.Fori(0, PTILES // 2) as i:
                for s in range(2):
                    gdn_pe(pe, i * 2 + s, s, i * 16 + 16, 0, (i * 2 + (4 + s), i * 32 + 32, i * 16), i * 2 + (4 + s))
            pe.wait_ge(on["s_state"], 16)
            gdn_pe(pe, PTILES, 0, 16 * (PTILES // 2 + 1), 1, None, 12)
            wo_pe(pe)
            ffn_pe(pe)

        @block.scalar
        def _(act):
            act.wait_ge(on["small"], 16 * len(SMALL))
            act.activation(csil[:], cT[:], ACT.Silu).then_inc(on["c_silu"], 1)
            act.activation(trig[:, 0, :], s5p[:, 2, :], ACT.Exp).then_inc(on["s5_exp_dt"], 1)
            act.wait_ge(on["s5_arg"], 1)
            act.activation(trig[:, 4, :], trig[:, 1, :], ACT.Exp).then_inc(on["s5_trig"], 1)
            act.wait_ge(on["s5_arg"], 2)
            act.activation(trig[:, 6, :], trig[:, 2, :], ACT.Sin).then_inc(on["s5_trig"], 1)
            act.activation(trig[:, 12, :], trig[:, 2, :], ACT.Abs).then_inc(on["s5_abs"], 1)
            act.wait_ge(on["s5_abs"], 1)
            act.activation(trig[:, 5, :], trig[:, 12, :], ACT.Sin, scale=-1.0, bias=trig[:, 13, 0:1]).then_inc(on["s5_trig"], 1)
            with act.Fori(0, PTILES // 2) as i:
                for s in range(2):
                    ln_norm(act, s, i * 2 + (s + 1), i * 2, P)
                    act.wait_ge(on["mod_ready"], 1)
                    ln_mod(act, s, i * 2 + (s + 1), i * 2, P, 0, 0, 0)
            ln_norm(act, 0, TILES, PTILES - 1, DEC_SEQ)
            ln_mod(act, 0, TILES, PTILES - 1, DEC_SEQ, 1, 0, 0)
            act.wait_ge(on["h_lo"], TILES)
            act.wait_ge(on["cleared"], 5)
            split_hi(act, 0, 16)

            def put_u(c, c0, cw):
                p0 = min(cw, SEQ - c0)
                ins = act.activation(urow[:, :, 1 + c0 // STEP:1 + (c0 + p0) // STEP].rearrange("p s n -> p n s"),
                                     ps[c][:, 0:p0].rearrange("p (n s) -> p n s", s=STEP), ACT.Copy)
                if p0 < cw:
                    ins = act.activation(urow[:, :, SAMP5 + 1:W5].rearrange("p s n -> p n s"),
                                         ps[c][:, p0:cw].rearrange("p (n s) -> p n s", s=STEP), ACT.Copy)
                return ins

            def put_row(row, first, func):
                def put(c, c0, cw):
                    p0 = min(cw, SEQ - c0)
                    ins = act.activation(row[:, first + c0:first + c0 + p0], ps[c][:, 0:p0], func)
                    if p0 < cw:
                        ins = act.activation(row[:, first + SAMP_COL:first + SAMP_COL + DEC_SEQ], ps[c][:, p0:cw], func)
                    return ins
                return put

            for n in range(NU):
                if n:
                    act.wait_ge(on["mm"], count(3 * n))
                split_hi(act, (n + 1) % 2, 16 * ((n + 1) // 2 + 1))
                if n:
                    act.wait_ge(on["u_stored"], count(16 * n))
                evac_chunks(n, put_u)
                act.wait_ge(on["in_evac"], count(3 * n + 3))
                act.dma_start(DR["u"][n * GB:(n + 1) * GB].rearrange("g j s w -> (g j) s w"), urow[:]).then_inc(on["u_stored"], 16)
            live = SEQ + GAP + DEC_SEQ
            with act.Fori(0, NB5) as b:
                for j in range(4):
                    n, sl = b * 4 + (NU + j), j % 2
                    act.wait_ge(on["mm"], count(n * 3))
                    split_hi(act, (j + 1) % 2, b * 32 + 16 * ((NU + j + 1) // 2 + 1))
                    if j == 2:
                        s5_evac_A(act, b)
                    if j < 3:
                        act.wait_ge(on["conv"], count(b * 3 + j))
                        act.activation(rawrow[:, GAP + SEQ:SAMP_COL + GAP], cache[:, bass.ds(b + 4 * j, 1), :].rearrange("p a c -> p (a c)"),
                                            ACT.Copy).then_inc(on["hist"], 1)
                        evac_chunks(n, put_row(rawrow, GAP, ACT.Copy))
                        act.wait_ge(on["hist"], count(b * 3 + (j + 1)))
                        act.wait_ge(on["in_evac"], count(n * 3 + 3))
                        act.wait_ge(on["wtap"], count(b * 3 + (j + 1)))
                        act.wait_ge(on["row_stored"][sl], count(b * 32 + 16 * (j // 2)))
                        act.activation(convrow[:, sl, 0:live], rawrow[:, 0:live], ACT.Copy, scale=wtap[:, sl, 0:1]).then_inc(on["tap0"], 1)
                        act.wait_ge(on["conv"], count(b * 3 + (j + 1)))
                        act.activation(convrow[:, sl, 0:live], convrow[:, sl, 0:live], ACT.Silu).then_inc(on["row_silu"], 1)
                        act.wait_ge(on["row_silu"], count(b * 3 + (j + 1)))
                    else:
                        act.wait_ge(on["row_stored"][sl], count(b * 32 + 16))
                        evac_chunks(n, put_row(convrow[:, sl, :], 0, ACT.Silu))
                        act.wait_ge(on["in_evac"], count(n * 3 + 3))
                    act.dma_start(DR["rows"][bass.ds(b + 4 * j, 1)].rearrange("a p w -> (a p) w"), convrow[:, sl, :]).then_inc(on["row_stored"][sl], 16)
                act.wait_ge(on["s5_y"], count(b * 3 + 3))
                act.activation(G[:], X[:], ACT.Gelu_apprx_tanh).then_inc(on["s5_gelu"], 1)
                act.wait_ge(on["s5_gelu"], count(b + 1))
                for t in range(STEP):
                    act.dma_start(DR["y"][bass.ds(b * GB, GB), :, t, :].rearrange("g i w -> i g w"), G[t * S5_J:(t + 1) * S5_J, :, :]).then_inc(on["y_stored"], 16)
            gates_act(act)
            glu_act(act)
            act.wait_ge(on["glu_mix"], 12)
            act.wait_ge(on["gates"], 1)
            with act.Fori(0, PTILES // 2) as i:
                for s in range(2):
                    gdn_act(act, i * 2 + s, s, (i * 2 + (4 + s), i * 32 + 32, i * 16))
            gdn_act(act, PTILES, 0, None)
            wo_act(act)
            ffn_act(act)

        @block.vector
        def _(dve):
            dve.wait_ge(on["small"], 16 * len(SMALL))
            dve.wait_ge(on["s5_den"], 1)
            dve.reciprocal(trig[:, 9, :], trig[:, 14, :]).then_inc(on["s5_rden"], 1)
            def mod_chunk(c, s, bank):
                dve.wait_ge(on["ada_mm"], count(c + 1))
                dve.tensor_tensor(modrow[:, s, :], ps[bank][0:2, :], bada[:, s, :], ALU.add).then_inc(on["mod_row"], 1)
                dve.wait_ge(on["mod_T"], count(c + 1))
                dve.tensor_copy(modc[:, c, :, :], ps[7][:, 0:8].rearrange("p (q t) -> p q t", t=2)).then_inc(on["mod_cols"], 1)

            for c in range(4):
                mod_chunk(c, c % 2, 4 + c % 2)
            dve.wait_ge(on["mod_cols"], 4)
            dve.tensor_scalar(onep[:, 0, :, :], modc[:, 2:4, :, :].rearrange("p a q t -> p (a q) t"), 1.0, None, ALU.add).then_inc(on["mod_ready"], 1)

            def split_h(s, tile, rows, col):
                dve.wait_ge(on["h_mod"], count(tile + 1))
                dve.tensor_copy(hT_hi[:, :, col], hpre[:, s, :, 0:rows]).then_inc(on["h_hi"], 1)
                dve.wait_ge(on["h_hi"], count(tile + 1))
                dve.tensor_tensor(hT_lo[:, :, col], hpre[:, s, :, 0:rows], hT_hi[:, :, col].bitcast(F32), ALU.subtract).then_inc(on["h_lo"], 1)

            def stats(s, tile, loaded, done, rows):
                dve.wait_ge(on["x"][s], count(loaded))
                dve.wait_ge(on["ln_rs"], count(done))
                for h in range(2):
                    dve.bn_stats(stat[0:rows, s, 6 * h:6 * h + 6], xin[0:rows, s, h * 512:(h + 1) * 512]).then_inc(on["ln_bn"], 1)
                dve.wait_ge(on["ln_bn"], alone(dve, count(tile * 2 + 2)))
                dve.bn_aggr(stat[0:rows, s, 12:14], stat[0:rows, s, 0:12]).then_inc(on["ln_mv"], 1)

            with dve.Fori(0, PTILES // 2) as i:
                for s in range(2):
                    stats(s, i * 2 + s, i * 16 + 16, i * 2, P)
                for s in range(2):
                    split_h(s, i * 2 + s, P, bass.ds(i * 2 * P + s * P, P))
            stats(0, PTILES, 16 * (PTILES // 2 + 1), PTILES, DEC_SEQ)
            split_h(0, PTILES, DEC_SEQ, slice(SEQ, TOK))
            split_lo(dve, 0, 1)
            for n in range(NU):
                split_lo(dve, (n + 1) % 2, n + 2)
            live = SEQ + GAP + DEC_SEQ
            with dve.Fori(0, NB5) as b:
                for j in range(4):
                    n, sl = b * 4 + (NU + j), j % 2
                    split_lo(dve, (j + 1) % 2, n + 2)
                    if j < 3:
                        row = b * 3 + j
                        dve.wait_ge(on["tap0"], count(row))
                        dve.tensor_copy(wtap[:, sl, :], convw[:, bass.ds(b + 4 * j, 1), :].rearrange("p a c -> p (a c)")).then_inc(on["wtap"], 1)
                        dve.wait_ge(on["in_evac"], count(n * 3 + 3))
                        dve.tensor_copy(rawtail[:, bass.ds(b + 4 * j, 1), 0, :].rearrange("p a c -> p (a c)"), rawrow[:, SEQ:SEQ + GAP]).then_inc(on["tail"], 1)
                        dve.tensor_copy(rawtail[:, bass.ds(b + 4 * j, 1), 1, :].rearrange("p a c -> p (a c)"), rawrow[:, RAWW - GAP:RAWW]).then_inc(on["tail"], 1)
                        dve.wait_ge(on["hist"], count(row + 1))
                        dve.wait_ge(on["tap0"], count(row + 1))
                        dve.wait_ge(on["wtap"], count(row + 1))
                        dve.wait_ge(on["tail"], count(row * 2 + 2))
                        for tap in range(1, CONVW):
                            ins = dve.scalar_tensor_tensor(out=convrow[:, sl, 0:live], in0=rawrow[:, tap:tap + live],
                                                           scalar=wtap[:, sl, tap:tap + 1], in1=convrow[:, sl, 0:live],
                                                           op0=ALU.mult, op1=ALU.add)
                            if tap < CONVW - 1:
                                ins.then_inc(on["tap"], 1)
                                dve.wait_ge(on["tap"], count(row * 2 + tap))
                            else:
                                ins.then_inc(on["conv"], 1)
                    else:
                        s5_scan(dve, b)
                        s5_out(dve, b)
            gates_dve(dve)
            glu_dve(dve)
            dve.wait_ge(on["g_init"], 1)
            with dve.Fori(0, PTILES // 2) as i:
                for s in range(2):
                    gdn_dve(dve, i * 2 + s, s, 0, bass.ds(i * 2 * P + s * P, P), P, (i * 2 + (4 + s), i * 32 + 32, i * 16))
            dve.wait_ge(on["s_state"], 16)
            gdn_dve(dve, PTILES, 0, 1, SEQ, DEC_SEQ, None)
            wo_dve(dve)
            ffn_dve(dve)


def kernel(**a):
    import numpy as np
    import concourse.bacc as bacc
    from concourse.bass_utils import run_bass_kernel_spmd

    f = np.ascontiguousarray
    both = lambda x: np.concatenate([x, x], 0)
    pg = lambda x: x[0].T
    pgj = lambda x: x[0].transpose(1, 0, 2)
    gjp = lambda x: x[0].transpose(2, 0, 1)
    c = np.concatenate([a["c_prompt"], a["c_sample"]], 0)
    bre, bim, cre, cim = pgj(a["s5_b_re"]), pgj(a["s5_b_im"]), gjp(a["s5_c_re"]), gjp(a["s5_c_im"])
    arrays = {
        "cT": f(c.reshape(2, KD, P).transpose(2, 1, 0)),
        "s5p": f(np.stack([both(pg(a["s5_a_re"])), both(pg(a["s5_a_im"])),
                           np.broadcast_to(a["s5_log_dt"][0], (P, S5_G))], 1)),
        "s5d": f(np.tile(a["s5_d"][0].reshape(S5_G, S5_J).T, (STEP, 1))),
        "s5h0": f(np.concatenate([pg(a["state_s5_re"][0]), pg(a["state_s5_im"][0])], 0)),
        "s5bc": f(np.stack([np.concatenate(x, 0) for x in ((bre, bim), (bim, bre), (cre, cim), (cim, cre))], 1)),
        "convw": f(a["gdn_conv_w"][0].reshape(CONVW, 12, P).transpose(2, 1, 0)),
        "cache": f(a["cache_gdn_conv"][0, 0].reshape(GAP, 12, P).transpose(2, 1, 0)),
        "balog": f(np.broadcast_to(np.stack([a["gdn_a_log"][0], a["gdn_dt_bias"][0]]), (P, 2, HEADS))),
        "normg": f(a["gdn_norm_g"][0][:, None]),
        "x_prompt": f(a["x_prompt"][0]), "x_sample": f(a["x_sample"][0]),
        "w_ada": f(a["w_ada"][0]), "b_ada": f(np.broadcast_to(a["b_ada"][0], (2, 6 * D_MODEL))),
        "w_in": f(a["w_in"][0]), "w_glu": f(a["w_s5_glu"][0]), "w_out": f(a["w_out"][0]),
        "w_up": f(a["w_ffn_up"][0]), "w_down": f(a["w_ffn_down"][0]), "state_gdn": f(a["state_gdn"][0, 0]),
        "ln_rows": f(np.stack([a["ln1_g"][0], a["ln1_b"][0], a["ln2_g"][0], a["ln2_b"][0]])),
    }
    nc = bacc.Bacc("TRN2", target_bir_lowering=False, num_devices=1)
    I = {k: nc.dram_tensor(k, v.shape, F32, kind="ExternalInput").ap() for k, v in arrays.items()}
    outs = {"y_prompt": (SEQ, D_MODEL), "y_sample": (DEC_SEQ, D_MODEL), "s5_states": (P, S5_G, 2),
            "gdn_states": (2, HEADS, HD, HD), "conv_tails": (P, 12, 2, GAP)}
    O = {k: nc.dram_tensor(k, v, F32, kind="ExternalOutput").ap() for k, v in outs.items()}
    DR = {k: nc.dram_tensor(k, v, F32, kind="Internal").ap() for k, v in {
        "u": (S5_G, S5_J, STEP, W5), "y": (S5_G, S5_J, STEP, W5), "rows": (16, P, ROWW),
        "mod": (2, 6 * D_MODEL), "x1": (TOK, D_MODEL)}.items()}
    stream_step(nc, I, O, DR)
    r = run_bass_kernel_spmd(nc, [arrays], core_ids=[0]).results[0]
    s5 = r["s5_states"].transpose(2, 1, 0)
    conv = r["conv_tails"].transpose(2, 3, 1, 0).reshape(2, GAP, 3 * 4 * HD)
    gdn = r["gdn_states"]
    return (r["y_prompt"][None], r["y_sample"][None],
            f(s5[0:1, :, 0:S5_P])[None], f(s5[0:1, :, S5_P:])[None], f(gdn[0:1])[None], f(conv[0:1])[None],
            f(s5[1:2, :, 0:S5_P])[None], f(s5[1:2, :, S5_P:])[None], f(gdn[1:2])[None], f(conv[1:2])[None])
```

```python
import concourse.bass as bass
from concourse import mybir
from contextlib import ExitStack

F32 = mybir.dt.float32
F32R = mybir.dt.float32r
ALU = mybir.AluOpType
ACT = mybir.ActivationFunctionType

P = 128
D_MODEL, SEQ, DEC_SEQ = 1024, 1024, 64
TOK = SEQ + DEC_SEQ
KD = D_MODEL // P
TILES = -(-TOK // P)
PTILES = SEQ // P
S5_G, S5_J, S5_P = 32, 16, 64
STEP = P // S5_J
NCH = SEQ // STEP
SCH = DEC_SEQ // STEP
W5 = 1 + NCH + 1 + SCH
SAMP5 = 1 + NCH
GB = P // S5_J
NB5 = S5_G // GB
HEADS, HD = 4, 128
CONVW = 4
GAP = CONVW - 1
ROWW = SEQ + GAP + P
SAMP_COL = SEQ + GAP
RAWW = GAP + SEQ + GAP + DEC_SEQ
D_FF = 2816
FB = D_FF // P
CH = [(0, 384), (384, 384), (768, 320)]
ADA_N = 512
ALPHA = 2 ** 0.25
LN_EPS, RMS_EPS = 1e-5, 1e-6
OFF_Z = 2048
OFF_BA = 2560
LEVELS = (2, 4, 8, 16, 32, 64)
LV = len(LEVELS)
TWO_PI = 6.283185307179586
ROUND = 12582912.0


SIGNALS = [
    "a_mm", "acc_in", "ada_mm", "bc", "bl_evac", "bt_T", "bt_ready", "c_in", "c_silu", "ca_ready", "cas_ready", "cleared",
    "conv", "f_add", "f_bn", "f_mv", "f_n", "f_sil", "f_tmp", "f_xg", "g1_row", "g2_row", "g_A", "g_AT", "g_ATs",
    "g_E", "g_EA", "g_EB", "g_KK", "g_L", "g_P", "g_Pb", "g_QK", "g_QKp", "g_R", "g_S", "g_T", "g_U", "g_V", "g_Vb",
    "g_X", "g_X0", "g_XX", "g_Xm", "g_col", "g_dd", "g_init", "g_kS", "g_kv", "g_kv8", "g_mix", "g_mm", "g_oT",
    "g_ob", "g_pool", "g_qd", "g_red", "g_row", "g_sc", "g_sc2", "g_sq", "gate_T", "gate_act", "gate_d", "gate_dve",
    "gate_exp", "gate_g", "gate_ln", "gate_sum", "gate_x", "gates", "glu_mix", "glu_sig", "h2_scale", "h_hi",
    "h_lo", "h_mod", "halfpi", "hist", "in_evac", "k_evac", "ln1_rows", "ln2_rows", "ln_bn", "ln_mv", "ln_r",
    "ln_rs", "masks", "mm", "mod_T", "mod_cols", "mod_ready", "mod_row", "mt", "out", "ph_ready", "pool_step",
    "row_silu", "s5_abs", "s5_arg", "s5_d", "s5_den", "s5_exp_dt", "s5_g", "s5_gelu", "s5_h", "s5_rden", "s5_rot",
    "s5_trig", "s5_x", "s5_x1", "s5_y", "s_state", "small", "state_out", "tail", "tap", "tap0", "u_stored", "ud",
    "w_hi", "w_lo", "wtap", "x_T", "x_norm", "y_hi", "y_lo", "y_mm", "y_out", "y_stored", "z_mm", "z_read",
]
SIGNALS_OF_SLOTS = {"ada": 4, "mod_st": 2, "raw": 2, "row_stored": 2,
                    "stg": 2, "x": 2, "x1_st": 2, "xt": 2, "y": 4}

COUNTED_ON = {
    "o_T": ("g_T", 2 * TILES), "wo_mm": ("g_row", TILES), "f_dn": ("g_kv", TILES * HEADS),
    "ms_hi": ("g_sq", 2 * TILES), "o_n1": ("g_kv8", 2 * TILES), "o_n2": ("g_E", 3 * TILES), "h2_mod": ("g_ATs", TILES),
    "f_hi": ("g_Vb", TILES * HEADS),
    "ms_lo": ("g_red", 2 * TILES), "o_tmp": ("g_dd", TILES), "o_r": ("g_mm", 2 * TILES), "o_bn": ("g_A", TILES * HEADS),
    "o_mv": ("g_QK", TILES), "o_xg": ("g_qd", TILES), "h2_hi": ("g_Xm", 2 * TILES), "h2_lo": ("g_X0", 2 * TILES),
    "f_mul": ("g_R", TILES * HEADS), "f_lo": ("g_ob", TILES),
    "o_rs": ("g_col", TILES), "o_p": ("g_pool", 10 * TILES), "x1_ready": ("g_U", TILES), "f_rs": ("g_EA", 0),
    "f_p": ("g_EB", TILES), "y_ready": ("g_sc2", TILES), "o_g1": ("g_sc", TILES), "f_g2": ("g_L", LV * TILES),
}


def bc(ap, axis, n):
    a = ap.unsqueeze(axis)
    shape = list(a.shape)
    shape[axis] = n
    return a.to_broadcast(shape)


def stream_step(nc, I, O, DR):
    ctx = ExitStack()
    with ctx:
        on = {name: ctx.enter_context(nc.semaphore(name)) for name in SIGNALS}
        for name, slots in SIGNALS_OF_SLOTS.items():
            on[name] = [ctx.enter_context(nc.semaphore(f"{name}{n}")) for n in range(slots)]
        for name, (earlier, _) in COUNTED_ON.items():
            on[name] = on[earlier]

        def at(name, shape, off, dt=F32):
            n = 4
            for d in shape[1:]:
                n *= d
            t = nc.alloc_sbuf_tensor_at(name, shape, dt, offset=off)
            return t, off + (n + 31) // 32 * 32

        base = -(-nc.sbuf_base // 32) * 32 if isinstance(nc.sbuf_base, int) else 1024
        off = base
        LIMIT = nc.sbuf_usable_end if isinstance(nc.sbuf_usable_end, int) else 212000

        def seq(start, *items):
            o, out = start, []
            for it in items:
                name, shape = it[0], it[1]
                t, o = at(name, shape, o, it[2] if len(it) > 2 else F32)
                out.append(t)
            assert o <= LIMIT, (items[0][0], o, LIMIT)
            return out, o

        (ident, triu, ones, lower, mask1, maskT, swapm, cT, csil, modc, onep,
         s5p, trig, sgn, mhalf, dcol_b, dcol, h0c, hout,
         tilecol, convw, cache, rawtail, normg, balog, gcol, stat, rstd), tables_at = seq(
            off,
            ("ident", [P, P]), ("triu", [P, P]), ("ones", [P, P]), ("lower", [P, P]), ("mask1", [P, P]),
            ("maskT", [P, 7, P]), ("swapm", [P, P]),
            ("cT", [P, KD, 2]), ("csil", [P, KD, 2]), ("modc", [P, 12, 4, 2]), ("onep", [P, 2, KD, 2]),
            ("s5p", [P, 3, S5_G]), ("trig", [P, 16, S5_G]),
            ("sgn", [P, 2]), ("mhalf", [P, 8]), ("dcol_b", [P, GB]), ("dcol", [P, S5_G]),
            ("h0c", [P, S5_G]), ("hout", [P, S5_G, 2]),
            ("tilecol", [P, 2, 10, HEADS]), ("convw", [P, 12, CONVW]), ("cache", [P, 12, GAP]), ("rawtail", [P, 12, 2, GAP]),
            ("normg", [P, 1]), ("balog", [P, 2, HEADS]), ("gcol", [P, 10, TILES, HEADS]),
            ("stat", [P, 2, 16]), ("rstd", [P, 2, 2]))
        (pw_r, pw_i, rev_r, rev_i, en1, en2, coef), tables_end = seq(
            tables_at, ("pw_r", [P, S5_G, 9]), ("pw_i", [P, S5_G, 9]), ("rev_r", [P, S5_G, 8]), ("rev_i", [P, S5_G, 8]),
            ("en1", [P, S5_G, 8]), ("en2", [P, S5_G, 8]), ("coef", [P, 4, S5_G, 9]))
        off = tables_end
        R1 = off
        (hT_hi, hT_lo), R2 = seq(R1, ("hT_hi", [P, KD, TOK], F32R), ("hT_lo", [P, KD, TOK], F32R))
        (wraw, whi, wlo), R3 = seq(R2, ("wraw", [P, 2, 1024]), ("whi", [P, 2, 1024], F32R), ("wlo", [P, 2, 1024], F32R))
        (rawrow, convrow, urow, wtap, Ud, CA, CAs, BT, Bl, Bls, Mt, Ksb, phC, phS, rho, X, G, cG, sG,
         bc12, ptmp), endA = seq(
            R3, ("rawrow", [P, RAWW]), ("convrow", [P, 2, ROWW]), ("urow", [P, STEP, W5]), ("wtap", [P, 2, CONVW]),
            ("Ud", [P, GB, W5]), ("CA", [P, GB, 9, S5_J]), ("CAs", [P, GB, STEP, S5_J]), ("BT", [P, GB, STEP, S5_J]),
            ("Bl", [P, GB, P]), ("Bls", [P, GB, P]), ("Mt", [P, GB, P]), ("Ksb", [S5_J, GB, P]),
            ("phC", [P, GB, W5]), ("phS", [P, GB, W5]), ("rho", [P, GB, W5]), ("X", [P, GB, W5]),
            ("G", [P, GB, W5]), ("cG", [P, GB, W5]), ("sG", [P, GB, W5]),
            ("bc12", [P, 4, GB, S5_J]), ("ptmp", [P, GB * 9 * S5_J]))
        (bas,), _ = seq(endA, ("bas", [8, TILES * P]))
        (yraw, y_hi, y_lo, sgb), endG = seq(R3, ("yraw", [P, 4, STEP * W5]), ("y_hi", [P, 4, STEP * W5], F32R),
                                            ("y_lo", [P, 4, STEP * W5], F32R), ("sgb", [P, STEP * W5]))
        (wada2, bada2), _ = seq(endG, ("wada2", [P, 2, KD, ADA_N]), ("bada2", [2, ADA_N]))
        (stg, Lneg, modrow2), _ = seq(R1, ("stg", [P, 2, 16, P]), ("Lneg", [P, 6, HEADS, P]), ("modrow2", [2, 2, ADA_N]))
        hp = [P, HEADS, P]
        (gU, dd, EA, EB, Am, AT, QK, erow, qd, kdec, vp, Pb, Rb, Vb, ob, sq, Sst, Xb, sc), endD = seq(
            R3, ("gU", hp), ("dd", hp), ("EA", hp), ("EB", hp), ("Am", hp), ("AT", hp), ("QK", hp), ("erow", hp),
            ("qd", hp), ("kdec", hp), ("vp", hp), ("Pb", hp), ("Rb", hp), ("Vb", hp), ("ob", hp),
            ("sq", [P, 2 * HEADS, P]), ("Sst", [P, 2, HEADS, P]), ("Xb", [P, HEADS, 2, P]), ("sc", [P, 12, HEADS]))
        assert endD <= endG
        mixT, _ = at("mixT", [P, KD, TOK], R1 + (R2 - R1) // 2)
        (xin, xnorm, hpre, wada, modrow), _ = seq(
            R3, ("xin", [P, 2, D_MODEL]), ("xnorm", [P, 2, D_MODEL]), ("hpre", [P, 2, KD, P]),
            ("wada", [P, 4, KD, ADA_N]), ("modrow", [2, 2, ADA_N]))
        (bada,), _ = seq(R1, ("bada", [2, 4, ADA_N]))
        (wo_hi, wo_lo, xt, xn2, hp2, otmp, g1r), _ = seq(
            R3, ("wo_hi", [P, KD, D_MODEL], F32R), ("wo_lo", [P, KD, D_MODEL], F32R), ("xt", [P, 2, D_MODEL]),
            ("xn2", [P, 2, D_MODEL]), ("hp2", [P, KD, P]), ("otmp", [P, D_MODEL]), ("g1r", [P, D_MODEL]))
        (g1s,), _ = seq(base + 5 * P * 4, ("g1s", [P, D_MODEL]))
        (ln1r,), rows_end = seq(tables_at, ("ln1r", [P, 2, D_MODEL]))
        (g2r,), _ = seq(tables_at, ("g2r", [P, 2, D_MODEL]))
        assert rows_end <= tables_end
        (acc, hid_hi, hid_lo, wd_hi, wd_lo, sil, dtmp), _ = seq(
            R3, ("acc", [P, TILES, D_MODEL]), ("hid_hi", [P, 2, TOK], F32R), ("hid_lo", [P, 2, TOK], F32R),
            ("wd_hi", [P, 2, D_MODEL], F32R), ("wd_lo", [P, 2, D_MODEL], F32R), ("sil", [P, TOK]), ("dtmp", [P, D_MODEL]))
        (ln2r,), _ = seq(R1, ("ln2r", [P, 2, D_MODEL]))
        ps = [ctx.enter_context(nc.psum_tensor(f"bank{n}", [P, 512], F32)) for n in range(8)]

        def count(value):
            return max(0, value) if isinstance(value, int) else value

        def since(name, value):
            return COUNTED_ON[name][1] + count(value)

        def alone(e, value):
            if not isinstance(value, int):
                value = e.to_reg(value)
                e.wait_ge(on["small"], 16 * len(SMALL))
            return value

        class Steps:

            def __init__(self, e, done, base=0):
                self.e, self.done, self.base, self.n = e, done, base, 0

            def __call__(self, ins):
                ins.then_inc(self.done, 1)
                self.n += 1
                self.e.wait_ge(self.done, alone(self.e, self.base + self.n))

        def split_hi(e, slot, loaded, width=1024):
            e.wait_ge(on["raw"][slot], count(loaded))
            nc.scalar.activation(whi[:, slot, 0:width], wraw[:, slot, 0:width], ACT.Copy).then_inc(on["w_hi"], 1)

        def split_lo(e, slot, hi_at, width=1024):
            e.wait_ge(on["w_hi"], count(hi_at))
            nc.vector.tensor_tensor(wlo[:, slot, 0:width], wraw[:, slot, 0:width],
                                         whi[:, slot, 0:width].bitcast(F32), ALU.subtract).then_inc(on["w_lo"], 1)

        def proj_block(e, slot, split_at, banks, bank_free, a_hi, a_lo, kt=KD, chunks=CH):
            e.wait_ge(on["w_lo"], count(split_at))
            for c, (c0, cw) in enumerate(chunks):
                bank_free(c)
                for k in range(kt):
                    for n, (w, a) in enumerate(((whi, a_hi), (whi, a_lo), (wlo, a_hi))):
                        last = nc.tensor.matmul(ps[banks[c]][:, 0:cw], w[:, slot, k * P:(k + 1) * P],
                                                a[:, k, c0:c0 + cw], start=(k == 0 and n == 0),
                                                stop=(k == kt - 1 and n == 2))
                last.then_inc(on["mm"], 1)

        NU, NMAIN = NB5, 4 * NB5
        win = I["w_in"].rearrange("(k p) n -> p k n", p=P)
        wad = I["w_ada"].rearrange("(k p) n -> p k n", p=P)
        SMALL = [(s5p, "s5p"), (dcol, "s5d"), (h0c, "s5h0"), (convw, "convw"), (cache, "cache"),
                 (balog, "balog"), (normg, "normg")]
        ROUNDS5 = [(0, 3), (3, 3), (6, 2)]

        def loads_before(sp):
            def ada(c):
                sp.dma_start(wada[:, c, :, :], wad[:, :, c * ADA_N:(c + 1) * ADA_N]).then_inc(on["ada"][c], 16)
                sp.dma_start(bada[:, c, :], I["b_ada"][:, c * ADA_N:(c + 1) * ADA_N]).then_inc(on["ada"][c], 16)

            sp.dma_start(cT[:], I["cT"]).then_inc(on["c_in"], 16)
            ada(0)
            for t, name in SMALL:
                sp.dma_start(t[:], I[name]).then_inc(on["small"], 16)
            for s in range(2):
                sp.dma_start(xin[:, s, :], I["x_prompt"][s * P:(s + 1) * P, :]).then_inc(on["x"][s], 16)
            for c in range(1, 4):
                ada(c)
            for n in range(2):
                sp.dma_start(wraw[:, n, :].rearrange("p (k n) -> p k n", k=KD), win[:, :, n * P:(n + 1) * P]).then_inc(on["raw"][n], 16)
            with sp.Fori(1, PTILES // 2) as i:
                for s in range(2):
                    sp.wait_ge(on["x_norm"], i * 2 + (s - 1))
                    sp.dma_start(xin[:, s, :], I["x_prompt"][bass.ds(i * 2 * P + s * P, P), :]).then_inc(on["x"][s], 16)
            sp.wait_ge(on["x_norm"], PTILES - 1)
            sp.dma_start(xin[0:DEC_SEQ, 0, :], I["x_sample"]).then_inc(on["x"][0], 16)

        def loads_projection(sp):
            for n in range(2, NU):
                sp.wait_ge(on["w_lo"], n - 1)
                sp.dma_start(wraw[:, n % 2, :].rearrange("p (k n) -> p k n", k=KD), win[:, :, n * P:(n + 1) * P]).then_inc(on["raw"][n % 2], 16)
            def batch(b):
                for j in range(4):
                    sp.wait_ge(on["w_lo"], count(b * 4 + (NU + j - 1)))
                    sp.dma_start(wraw[:, j % 2, :].rearrange("p (k n) -> p k n", k=KD), win[:, :, bass.ds(b * P + (j + 1) * 512, P)]).then_inc(on["raw"][j % 2], 16)
                    if j == 1:
                        sp.wait_ge(on["u_stored"], NU * 16)
                        sp.wait_ge(on["y_mm"], count(b))
                        sp.wait_ge(on["s5_y"], count(b * 3))
                        for s in range(STEP):
                            sp.dma_start(Ud[s * S5_J:(s + 1) * S5_J, :, :], DR["u"][bass.ds(b * GB, GB), :, s, :].rearrange("g j n -> j g n")).then_inc(on["ud"], 16)
                    if j == 3:
                        sp.wait_ge(on["k_evac"], count(b * 2 + 2))
                        for s in range(STEP):
                            sp.dma_start(Mt[s * S5_J:(s + 1) * S5_J, :, s * S5_J:P], Ksb[:, :, 0:P - s * S5_J]).then_inc(on["mt"], 16)

            batch(0)
            with sp.Fori(1, NB5) as b:
                batch(b)
            sp.wait_ge(on["w_lo"], NU + NMAIN - 1)
            sp.dma_start(wraw[:, 0, :].rearrange("p (k n) -> p k n", k=KD), win[:, :, OFF_BA + 8 - P:OFF_BA + 8]).then_inc(on["raw"][0], 16)

        def masks(pool):
            g = Steps(pool, on["pool_step"])
            for t in (ident, lower, mask1, swapm):
                g(pool.memset(t[:], 0.0))
            g(pool.memset(triu[:], 1.0))
            g(pool.memset(ones[:], 1.0))
            g(pool.memset(lower[:], 1.0))
            g(pool.memset(maskT[:], 0.0))
            g(pool.memset(sgn[:], 1.0))
            g(pool.memset(mhalf[:], -0.5))
            g(pool.memset(sgn[0:S5_P, 0:1], -1.0))
            sel = lambda ap, pat, op, fill, base, cm: g(pool.affine_select(
                out=ap, in_=ap, compare_op=op, fill=fill, base=base, pattern=pat, channel_multiplier=cm))
            sel(ident[:], [[-1, P]], ALU.not_equal, 1.0, 0, 1)
            sel(triu[:], [[1, P]], ALU.is_ge, 0.0, 0, -1)
            sel(lower[:], [[-1, P]], ALU.is_gt, 0.0, 0, 1)
            sel(swapm[:], [[-1, P]], ALU.not_equal, -1.0, -S5_P, 1)
            sel(swapm[:], [[-1, P]], ALU.not_equal, 1.0, S5_P, 1)
            for n, b in enumerate((1,) + LEVELS):
                v = maskT[:, n, :].rearrange("p (m h c) -> p m h c", h=2, c=b)[:, :, 1, :]
                g(pool.memset(v, -1.0))
                sel(v, [[-2 * b, P // (2 * b)], [0, b]], ALU.is_ge, 0.0, 0, 1)
                sel(v, [[2 * b, P // (2 * b)], [0, b]], ALU.is_ge, 0.0, b - 1, -1)
            v = mask1[:].rearrange("p (m h) -> p m h", h=2)[:, :, 0]
            g(pool.memset(v, -1.0))
            sel(v, [[-2, P // 2]], ALU.is_equal, 0.0, -1, 1)
            pool.memset(trig[:, 13, :], TWO_PI / 4).then_inc(on["halfpi"], 1)
            pool.memset(sgn[:, 1:2], 1.0).then_inc(on["masks"], 1)
            return g.n

        def unit(pool, g, re, im, t1, t2):
            g(pool.tensor_tensor(t1, re, re, ALU.mult))
            g(pool.tensor_tensor(t2, im, im, ALU.mult))
            g(pool.tensor_tensor(t1, t1, t2, ALU.add))
            g(pool.tensor_scalar(t1, t1, -0.5, 1.5, ALU.mult, ALU.add))
            g(pool.tensor_tensor(re, re, t1, ALU.mult))
            g(pool.tensor_tensor(im, im, t1, ALU.mult))

        def s5_tables(pool, n0):
            g = Steps(pool, on["pool_step"], n0)
            tt = lambda o, a, b, op: g(pool.tensor_tensor(o, a, b, op))
            ts = lambda o, a, s1, s2, op0, op1=None: g(pool.tensor_scalar(o, a, s1, s2, op0, op1) if op1 is not None
                                                       else pool.tensor_scalar(o, a, s1, None, op0))
            T = lambda n: trig[:, n, :]
            are, aim, ldt = (s5p[:, n, :] for n in range(3))
            DT, EXA, TH, KK, MAG, COS, SIN, A1, A2, DEN, FR, FI = range(12)

            def cmul(o_r, o_i, x_r, x_i, y_r, y_i, t1, t2):
                tt(t1, x_r, y_r, ALU.mult)
                tt(t2, x_i, y_i, ALU.mult)
                tt(t1, t1, t2, ALU.subtract)
                tt(t2, x_r, y_i, ALU.mult)
                tt(o_i, x_i, y_r, ALU.mult)
                tt(o_i, o_i, t2, ALU.add)
                g(pool.tensor_copy(o_r, t1))

            pool.wait_ge(on["s5_exp_dt"], 1)
            tt(T(EXA), are, T(DT), ALU.mult)
            pool.tensor_copy(T(A1), T(EXA)).then_inc(on["s5_arg"], 1)
            pool.wait_ge(on["s5_arg"], 1)
            tt(T(TH), aim, T(DT), ALU.mult)
            ts(T(KK), T(TH), 1.0 / TWO_PI, ROUND, ALU.mult, ALU.add)
            ts(T(KK), T(KK), ROUND, None, ALU.subtract)
            for part in (6.28125, 0.0019340515136718750, 1.2556659146e-06):
                ts(T(A2), T(KK), part, None, ALU.mult)
                tt(T(TH), T(TH), T(A2), ALU.subtract)
            g(pool.tensor_scalar(T(TH), T(TH), 3.1415925, -3.1415925, ALU.min, ALU.max))
            pool.tensor_copy(T(A2), T(TH)).then_inc(on["s5_arg"], 1)
            pool.wait_ge(on["s5_arg"], 2)
            pool.wait_ge(on["s5_trig"], 3)
            one = lambda ap: g(pool.memset(ap, 1.0))
            one(pw_r[:, :, 0])
            g(pool.memset(pw_i[:, :, 0], 0.0))
            tt(pw_r[:, :, 1], T(MAG), T(COS), ALU.mult)
            tt(pw_i[:, :, 1], T(MAG), T(SIN), ALU.mult)
            ts(T(FR), pw_r[:, :, 1], 1.0, None, ALU.subtract)
            tt(T(A1), are, are, ALU.mult)
            tt(T(A2), aim, aim, ALU.mult)
            tt(T(A1), T(A1), T(A2), ALU.add)
            pool.tensor_copy(T(14), T(A1)).then_inc(on["s5_den"], 1)
            pool.wait_ge(on["s5_den"], 1)
            tt(T(A1), T(FR), are, ALU.mult)
            tt(T(A2), pw_i[:, :, 1], aim, ALU.mult)
            tt(T(A1), T(A1), T(A2), ALU.add)
            tt(T(A2), T(FR), aim, ALU.mult)
            tt(T(FI), pw_i[:, :, 1], are, ALU.mult)
            tt(T(FI), T(FI), T(A2), ALU.subtract)
            yield
            pool.wait_ge(on["s5_rden"], 1)
            tt(T(FR), T(A1), T(DEN), ALU.mult)
            tt(T(FI), T(FI), T(DEN), ALU.mult)
            t1, t2 = rev_r, rev_i
            for lo, m, y in ((1, 1, 1), (1, 2, 2), (1, 4, 4)):
                cmul(pw_r[:, :, lo + m:lo + 2 * m], pw_i[:, :, lo + m:lo + 2 * m], pw_r[:, :, lo:lo + m], pw_i[:, :, lo:lo + m],
                     pw_r[:, :, y:y + 1].to_broadcast([P, S5_G, m]), pw_i[:, :, y:y + 1].to_broadcast([P, S5_G, m]),
                     t1[:, :, 0:m], t2[:, :, 0:m])
            yield
            ts(coef[:, 1, :, :], pw_i[:], -1.0, None, ALU.mult)
            ts(coef[:, 3, :, :], pw_r[:], -1.0, None, ALU.mult)
            ts(coef[:, 0, :, :], coef[:, 3, :, :], sgn[:, 0:1], None, ALU.mult)
            ts(coef[:, 2, :, :], pw_i[:], sgn[:, 0:1], None, ALU.mult)
            for s in range(STEP):
                g(pool.tensor_copy(rev_r[:, :, s], pw_r[:, :, STEP - 1 - s]))
                g(pool.tensor_copy(rev_i[:, :, s], pw_i[:, :, STEP - 1 - s]))
            fr, fi = bc(T(FR), 2, STEP), bc(T(FI), 2, STEP)
            ptv = ptmp[:, 0:S5_G * STEP].rearrange("p (g s) -> p g s", g=S5_G)
            tt(en1[:], rev_r[:], fr, ALU.mult)
            tt(ptv, rev_i[:], fi, ALU.mult)
            tt(en1[:], en1[:], ptv, ALU.subtract)
            tt(en2[:], rev_r[:], fi, ALU.mult)
            tt(ptv, rev_i[:], fr, ALU.mult)
            tt(en2[:], en2[:], ptv, ALU.add)
            ts(en2[:], en2[:], sgn[:, 0:1], None, ALU.mult)
            for _ in range(3):
                tt(T(A1), T(COS), T(COS), ALU.mult)
                tt(T(A2), T(SIN), T(SIN), ALU.mult)
                tt(T(SIN), T(SIN), T(COS), ALU.mult)
                ts(T(SIN), T(SIN), 2.0, None, ALU.mult)
                tt(T(COS), T(A1), T(A2), ALU.subtract)
                tt(T(MAG), T(MAG), T(MAG), ALU.mult)
            unit(pool, g, T(COS), T(SIN), T(A1), T(A2))
            yield n0 + g.n, (COS, SIN, MAG)

        def s5_batch_tables(pool, b, n0, per, trigs):
            COS, SIN, MAG = trigs
            g = Steps(pool, on["pool_step"], n0 + b * per)
            tt = lambda o, a, c, op: pool.tensor_tensor(o, a, c, op)
            first = isinstance(b, int)
            gs = slice(b * GB, (b + 1) * GB) if first else bass.ds(b * GB, GB)
            pool.dma_start(bc12[:], I["s5bc"][:, :, gs, :]).then_inc(on["bc"], 16)
            pool.wait_ge(on["bc"], alone(pool, count(b * 16 + 16)))

            def combine(out, tmp, m, x, y, c1, c2, name):
                n = out.shape[2]
                g(tt(out, bc(x, 2, n), bc(c1, 3, S5_J), ALU.mult))
                g(tt(tmp, bc(y, 2, n), bc(c2, 3, S5_J), ALU.mult))
                tt(out, out, tmp, ALU.add).then_inc(name, 1)

            B1, B2, C1, C2 = (bc12[:, n, :, :] for n in range(4))
            tmp9 = ptmp[:].rearrange("p (g m j) -> p g m j", g=GB, j=S5_J)
            tmp8 = ptmp[:, 0:GB * STEP * S5_J].rearrange("p (g m j) -> p g m j", g=GB, j=S5_J)
            pool.wait_ge(on["a_mm"], alone(pool, count(b)))
            combine(BT[:], tmp8, STEP, B1, B2, en1[:, gs, :], en2[:, gs, :], on["bt_ready"])
            pool.wait_ge(on["bt_ready"], alone(pool, count(b + 1)))

            def outputs():
                pool.wait_ge(on["y_mm"], alone(pool, count(b)))
                combine(CA[:], tmp9, 9, C1, C2, coef[:, 0, gs, :], coef[:, 1, gs, :], on["ca_ready"])
                pool.wait_ge(on["ca_ready"], alone(pool, count(b + 1)))

            def phases():
                pool.wait_ge(on["s5_rot"], alone(pool, count(b * 2)))
                g(pool.memset(phC[:, :, 0:1], 1.0))
                g(pool.memset(phS[:, :, 0:1], 0.0))
                g(pool.tensor_copy(phC[:, :, 1], trig[:, COS, gs]))
                g(pool.tensor_copy(phS[:, :, 1], trig[:, SIN, gs]))
                m = 1
                while m < NCH:
                    a_r, a_i = phC[:, :, 1:1 + m], phS[:, :, 1:1 + m]
                    y_r, y_i = (x[:, :, m:m + 1].to_broadcast([P, GB, m]) for x in (phC, phS))
                    o_r, o_i = phC[:, :, 1 + m:1 + 2 * m], phS[:, :, 1 + m:1 + 2 * m]
                    t1 = ptmp[:, 0:GB * m].rearrange("p (g m) -> p g m", g=GB)
                    t2 = ptmp[:, GB * m:2 * GB * m].rearrange("p (g m) -> p g m", g=GB)
                    g(tt(o_r, a_r, y_r, ALU.mult))
                    g(tt(t1, a_i, y_i, ALU.mult))
                    g(tt(o_r, o_r, t1, ALU.subtract))
                    g(tt(o_i, a_r, y_i, ALU.mult))
                    g(tt(t1, a_i, y_r, ALU.mult))
                    g(tt(o_i, o_i, t1, ALU.add))
                    m *= 2

            def phase_ends():
                for x in (phC, phS):
                    g(pool.tensor_copy(x[:, :, SAMP5:W5], x[:, :, 0:1 + SCH]))
                g(pool.tensor_copy(rho[:], bc(trig[:, MAG, gs], 2, W5)))
                g(pool.memset(rho[:, :, 0:1], 0.0))
                pool.memset(rho[:, :, SAMP5:SAMP5 + 1], 0.0).then_inc(on["ph_ready"], 1)

            if first:
                outputs()
                phases()
            else:
                phases()
                outputs()
            phase_ends()
            combine(CAs[:], tmp8, STEP, C1, C2, coef[:, 2, gs, 1:9], coef[:, 3, gs, 1:9], on["cas_ready"])
            pool.wait_ge(on["cas_ready"], alone(pool, count(b + 1)))
            return g.n

        def ada_mm(e, c):
            e.wait_ge(on["ada"][c], 32)
            e.wait_ge(on["mod_row"], count(c - 2))
            for k in range(KD):
                last = nc.tensor.matmul(ps[4 + c % 3][0:2, :], csil[:, k, :], wada[:, c, k, :], start=(k == 0), stop=(k == KD - 1))
            last.then_inc(on["ada_mm"], 1)

        def ada_transpose(e, c):
            e.wait_ge(on["mod_row"], c + 1)
            e.wait_ge(on["mod_cols"], count(c))
            for q in range(4):
                last = nc.tensor.transpose(ps[7][:, 2 * q:2 * q + 2], modrow[:, c % 2, q * P:(q + 1) * P], ident[0:2, 0:2])
            last.then_inc(on["mod_T"], 1)

        def ln_steps(eng, step):
            step(0, 0)
            step(1, 1)
            with eng.Fori(1, PTILES // 2 - 1) as i:
                for s in range(2):
                    step(i * 2 + s, s)
            for t in range(PTILES - 2, TILES):
                step(t, t % 2)

        def ln_transpose(e, s, ready, freed, rows):
            e.wait_ge(on["x_norm"], count(ready))
            e.wait_ge(on["h_mod"], count(freed))
            for k in range(KD):
                last = nc.tensor.transpose(ps[4 + 2 * s + k // 4][:, (k % 4) * P:(k % 4) * P + rows],
                                           xnorm[0:rows, s, k * P:(k + 1) * P], ident[0:rows, 0:rows])
            last.then_inc(on["x_T"], 1)

        def s5_A(e, b):
            e.wait_ge(on["bt_ready"], count(b + 1))
            e.wait_ge(on["s5_y"], count(b * 3))
            e.wait_ge(on["s5_h"], count(b))
            for g in range(GB):
                last = nc.tensor.transpose(ps[3 + g // 4][:, (g % 4) * P:(g % 4 + 1) * P],
                                           BT[:, g, :, :].rearrange("p s j -> p (s j)"), ident[:])
            last.then_inc(on["bt_T"], 1)
            e.wait_ge(on["ca_ready"], count(b + 1))
            for g in range(GB):
                last = nc.tensor.matmul(ps[5 + g // 4][0:S5_J, (g % 4) * P:(g % 4 + 1) * P], BT[:, g, STEP - 1, :],
                                        CA[:, g, 0:STEP, :].rearrange("p t i -> p (t i)"), start=True, stop=True)
            last.then_inc(on["a_mm"], 1)

        def s5_Z(e, b):
            e.wait_ge(on["ud"], count(b * (16 * STEP) + 16 * STEP))
            e.wait_ge(on["bl_evac"], count(b * 2 + 2))
            e.wait_ge(on["k_evac"], count(b * 2 + 2))
            for r, (g0, gn) in enumerate(ROUNDS5):
                if r == 2:
                    e.wait_ge(on["z_read"], count(b * 3 + 1))
                for q in range(gn):
                    for B, bank in ((Bl, 3 + r % 2), (Bls, 5 + r % 2)):
                        last = nc.tensor.matmul(ps[bank][:, q * W5:(q + 1) * W5], B[:, g0 + q, :], Ud[:, g0 + q, :],
                                                start=True, stop=True)
                last.then_inc(on["z_mm"], 1)

        def s5_Y(e, b):
            e.wait_ge(on["cas_ready"], count(b + 1))
            e.wait_ge(on["mt"], count(b * (16 * STEP) + 16 * STEP))
            e.wait_ge(on["s5_rot"], count(b * 2 + 2))
            for r, (g0, gn) in enumerate(ROUNDS5):
                for q in range(gn):
                    g, out = g0 + q, ps[3 + r][:, q * W5:q * W5 + W5 - 1]
                    nc.tensor.matmul(out, CA[:, g, 1:9, :].rearrange("p t i -> p (t i)"), cG[:, g, 0:W5 - 1], start=True, stop=False)
                    nc.tensor.matmul(out, CAs[:, g, :, :].rearrange("p t i -> p (t i)"), sG[:, g, 0:W5 - 1], start=False, stop=False)
                    last = nc.tensor.matmul(out, Mt[:, g, :], Ud[:, g, 1:W5], start=False, stop=True)
                last.then_inc(on["y_out"], 1)
            last = nc.tensor.matmul(ps[6][:, 0:GB], swapm[:], sG[:, :, NCH], start=True, stop=True)
            last = nc.tensor.matmul(ps[6][:, GB:2 * GB], swapm[:], sG[:, :, W5 - 1], start=True, stop=True)
            last.then_inc(on["y_mm"], 1)

        def in_block(e, slot, n):
            def bank_free(c):
                if isinstance(n, int) and n == 0:
                    e.wait_ge(on["h_lo"], min(TILES, 3 * (c + 1)))
                if not isinstance(n, int) or n:
                    e.wait_ge(on["in_evac"], count(n * 3 + (c - 2)))
            proj_block(e, slot, n + 1, (0, 1, 2), bank_free, hT_hi, hT_lo)

        def ln_norm(e, s, ready, used, rows):
            e.wait_ge(on["ln_rs"], count(ready))
            e.wait_ge(on["x_T"], count(used))
            nc.scalar.activation(xnorm[0:rows, s, :], xin[0:rows, s, :], ACT.Identity, bias=rstd[0:rows, s, 1:2],
                                      scale=rstd[0:rows, s, 0:1]).then_inc(on["x_norm"], 1)

        def ln_mod(e, s, ready, used, rows, tok, which, sh):
            e.wait_ge(on["x_T"], count(ready))
            e.wait_ge(on["h_lo"], count(used))
            for k in range(KD):
                last = nc.scalar.activation(hpre[:, s, k, 0:rows], ps[4 + 2 * s + k // 4][:, (k % 4) * P:(k % 4) * P + rows], ACT.Identity,
                                            scale=onep[:, which, k, tok:tok + 1],
                                            bias=modc[:, sh + k // 4, k % 4, tok:tok + 1])
            last.then_inc(on["h_mod"], 1)

        def evac_chunks(n, put):
            for c, (c0, cw) in enumerate(CH):
                nc.scalar.wait_ge(on["mm"], count(n * 3 + (c + 1)))
                put(c, c0, cw).then_inc(on["in_evac"], 1)

        def s5_evac_A(act, b):
            act.wait_ge(on["bt_T"], count(b + 1))
            act.wait_ge(on["s5_y"], count(b * 3))
            for h in range(2):
                src = ps[3 + h][:].rearrange("p (g c) -> p g c", c=P)
                dst = slice(4 * h, 4 * h + 4)
                act.activation(Bl[:, dst, :], src, ACT.Copy)
                act.activation(Bls[:, dst, 0:S5_P], src[:, :, S5_P:P], ACT.Copy)
                act.activation(Bls[:, dst, S5_P:P], src[:, :, 0:S5_P], ACT.Copy, scale=-1.0).then_inc(on["bl_evac"], 1)
            act.wait_ge(on["a_mm"], count(b + 1))
            act.wait_ge(on["mt"], count(b * (16 * STEP)))
            for h in range(2):
                act.activation(Ksb[:, 4 * h:4 * h + 4, :], ps[5 + h][0:S5_J, :].rearrange("p (g c) -> p g c", c=P), ACT.Copy).then_inc(on["k_evac"], 1)

        def s5_gelu(act, b):
            act.wait_ge(on["s5_y"], count(b * 3 + 3))
            act.activation(G[:], X[:], ACT.Gelu_apprx_tanh).then_inc(on["s5_gelu"], 1)
            act.wait_ge(on["s5_gelu"], count(b + 1))
            for t in range(STEP):
                act.dma_start(DR["y"][bass.ds(b * GB, GB), :, t, :].rearrange("g i w -> i g w"), G[t * S5_J:(t + 1) * S5_J, :, :]).then_inc(on["y_stored"], 16)

        def s5_rotate(dve, b, r):
            g0, gn = ROUNDS5[r]
            dve.wait_ge(on["z_mm"], count(b * 3 + (r + 1)))
            gsl = slice(g0, g0 + gn)
            v = lambda bank: ps[bank][:, 0:gn * W5].rearrange("p (g w) -> p g w", g=gn)
            dve.tensor_tensor(X[:, gsl, :], phC[:, gsl, :], v(3 + r % 2), ALU.mult).then_inc(on["s5_x1"], 1)
            dve.tensor_tensor(cG[:, gsl, :], phS[:, gsl, :], v(5 + r % 2), ALU.mult).then_inc(on["z_read"], 1)

        def s5_scan_first(dve, b):
            dve.wait_ge(on["ph_ready"], count(b + 1))
            dve.wait_ge(on["y_stored"], count(b * (STEP * 16)))
            dve.wait_ge(on["y_mm"], count(b))
            s5_rotate(dve, b, 0)
            s5_rotate(dve, b, 1)

        def s5_scan(dve, b):
            s5_rotate(dve, b, 2)
            dve.wait_ge(on["s5_x1"], count(b * 3 + 3))
            dve.wait_ge(on["z_read"], count(b * 3 + 3))
            dve.tensor_tensor(X[:], X[:], cG[:], ALU.add).then_inc(on["s5_x"], 1)
            dve.wait_ge(on["s5_x"], count(b * 2 + 1))
            dve.tensor_copy(X[:, :, SAMP5], h0c[:, bass.ds(b * GB, GB)]).then_inc(on["s5_x"], 1)
            dve.wait_ge(on["s5_x"], count(b * 2 + 2))
            dve.tensor_copy(dcol_b[:], dcol[:, bass.ds(b * GB, GB)]).then_inc(on["s5_d"], 1)
            flat = lambda t: t[:].rearrange("p g w -> p (g w)")
            dve.tensor_tensor_scan(flat(G), flat(rho), flat(X), 0.0, ALU.mult, ALU.add).then_inc(on["s5_g"], 1)
            dve.wait_ge(on["s5_g"], count(b + 1))
            dve.tensor_tensor(cG[:], phC[:], G[:], ALU.mult).then_inc(on["s5_rot"], 1)
            dve.tensor_tensor(sG[:], phS[:], G[:], ALU.mult).then_inc(on["s5_rot"], 1)

        def s5_out(dve, b):
            dve.wait_ge(on["s5_d"], count(b + 1))
            for r, (g0, gn) in enumerate(ROUNDS5):
                dve.wait_ge(on["y_out"], count(b * 3 + (r + 1)))
                dve.wait_ge(on["s5_rot"], count(b * 2 + 2))
                for q in range(gn):
                    g = g0 + q
                    last = dve.scalar_tensor_tensor(out=X[:, g, 0:W5 - 1], in0=Ud[:, g, 1:W5], scalar=dcol_b[:, g:g + 1],
                                                    in1=ps[3 + r][:, q * W5:q * W5 + W5 - 1], op0=ALU.mult, op1=ALU.add)
                last.then_inc(on["s5_y"], 1)
            dve.wait_ge(on["y_mm"], count(b + 1))
            for n, col in enumerate((NCH, W5 - 1)):
                last = dve.tensor_tensor(hout[:, bass.ds(b * GB, GB), n], cG[:, :, col], ps[6][:, n * GB:(n + 1) * GB], ALU.add)
            last.then_inc(on["s5_h"], 1)


        (BETA, GATE, DEC, TOT, NEXP, KDEC, GLAST, T0, T1, T2) = range(10)
        gc = lambda n, t: gcol[:, n, t, :] if isinstance(t, int) else gcol[:, n, bass.ds(t, 1), :].rearrange("p a h -> p (a h)")
        R_BA = NU + NMAIN
        R_GLU = R_BA + 1
        MM_BA, MM_GLU = 3 * R_BA, 3 * R_GLU

        def gates_pe(pe):
            pe.wait_ge(on["w_lo"], R_BA + 1)
            for c, (c0, cw) in enumerate(CH):
                pe.wait_ge(on["in_evac"], count(MM_BA - 3 + c + 1))
                for k in range(KD):
                    for n, (w, a) in enumerate(((whi, hT_hi), (whi, hT_lo), (wlo, hT_hi))):
                        last = pe.matmul(ps[c][0:8, 0:cw], w[:, 0, (k + 1) * P - 8:(k + 1) * P], a[:, k, c0:c0 + cw],
                                         start=(k == 0 and n == 0), stop=(k == KD - 1 and n == 2))
                last.then_inc(on["mm"], 1)
            s5_Y(pe, NB5 - 1)
            pe.wait_ge(on["in_evac"], MM_BA + 3)
            for t in range(TILES):
                last = pe.transpose(ps[7][:, 8 * t:8 * t + 8], bas[:, t * P:(t + 1) * P], ident[0:8, 0:8])
            last.then_inc(on["gate_T"], 1)
            pe.wait_ge(on["gate_g"], 1)
            pe.wait_ge(on["s5_h"], NB5)
            flat = gcol[:, GATE, :, :].rearrange("p t h -> p (t h)")
            pe.matmul(ps[6][:, 0:TILES * HEADS], triu[:], flat, start=True, stop=True)
            pe.matmul(ps[6][:, 64:64 + TILES * HEADS], ones[:], flat, start=True, stop=True).then_inc(on["gate_sum"], 1)

        def gates_act(act):
            for c, (c0, cw) in enumerate(CH):
                act.wait_ge(on["mm"], count(MM_BA + c + 1))
                act.activation(bas[:, c0:c0 + cw], ps[c][0:8, 0:cw], ACT.Copy).then_inc(on["in_evac"], 1)
            s5_gelu(act, NB5 - 1)
            g = Steps(act, on["gate_act"])
            act.wait_ge(on["gate_x"], 1)
            raw = ps[7][:, 0:8 * TILES].rearrange("p (t c) -> p t c", c=8)
            g(act.activation(gcol[:, BETA, :, :], raw[:, :, 0:HEADS], ACT.Sigmoid))
            g(act.activation(gcol[:, T1, :, :], gcol[:, T0, :, :], ACT.Abs))
            g(act.activation(gcol[:, T1, :, :], gcol[:, T1, :, :], ACT.Exp, scale=-1.0))
            g(act.activation(gcol[:, T1, :, :], gcol[:, T1, :, :], ACT.Ln, bias=1.0))
            g(act.activation(balog[:, 0, :], balog[:, 0, :], ACT.Exp))
            act.activation(gcol[:, T2, :, :], gcol[:, T0, :, :], ACT.Relu).then_inc(on["gate_ln"], 1)
            act.wait_ge(on["gate_sum"], 1)
            act.wait_ge(on["gate_d"], 2)
            g(act.activation(gcol[:, NEXP, :, :], gcol[:, DEC, :, :], ACT.Exp))
            g(act.activation(gcol[:, GLAST, :, :], gcol[:, TOT, :, :], ACT.Exp))
            act.wait_ge(on["gate_d"], 3)
            act.activation(gcol[:, KDEC, :, :], gcol[:, T0, :, :], ACT.Exp).then_inc(on["gate_exp"], 1)

        def gates_dve(dve):
            dve.wait_ge(on["gate_T"], 1)
            raw = ps[7][:, 0:8 * TILES].rearrange("p (t c) -> p t c", c=8)
            dve.tensor_tensor(gcol[:, T0, :, :], raw[:, :, HEADS:8], bc(balog[:, 1, :], 1, TILES), ALU.add).then_inc(on["gate_x"], 1)
            dve.wait_ge(on["gate_ln"], 1)
            dve.wait_ge(on["gate_act"], 5)
            g = Steps(dve, on["gate_dve"])
            g(dve.tensor_tensor(gcol[:, T1, :, :], gcol[:, T1, :, :], gcol[:, T2, :, :], ALU.add))
            g(dve.tensor_tensor(gcol[:, T1, :, :], gcol[:, T1, :, :], bc(balog[:, 0, :], 1, TILES), ALU.mult))
            g(dve.tensor_scalar(gcol[:, GATE, :, :], gcol[:, T1, :, :], -1.0, None, ALU.mult))
            dve.memset(gcol[DEC_SEQ:P, GATE, TILES - 1, :], 0.0).then_inc(on["gate_g"], 1)
            dve.wait_ge(on["gate_sum"], 1)
            n = TILES * HEADS
            v = lambda a: a.rearrange("p (t h) -> p t h", h=HEADS)
            dve.tensor_copy(gcol[:, DEC, :, :], v(ps[6][:, 0:n])).then_inc(on["gate_d"], 1)
            dve.tensor_copy(gcol[:, TOT, :, :], v(ps[6][:, 64:64 + n])).then_inc(on["gate_d"], 1)
            dve.wait_ge(on["gate_d"], 2)
            dve.tensor_tensor(gcol[:, T0, :, :], gcol[:, TOT, :, :], gcol[:, DEC, :, :], ALU.subtract).then_inc(on["gate_d"], 1)
            dve.wait_ge(on["gate_exp"], 1)
            dve.wait_ge(on["gate_act"], 7)
            dve.tensor_scalar(gcol[:, NEXP, :, :], gcol[:, NEXP, :, :], -1.0, None, ALU.mult).then_inc(on["gates"], 1)

        TCH = [(0, 3), (3, 3), (6, 2)]
        YCH = [(t0 * W5, tn * W5) for t0, tn in TCH]

        def glu_pe(pe):
            pe.wait_ge(on["gate_d"], 2)
            pe.wait_ge(on["y_lo"], 4)
            with pe.Fori(0, 4) as f:
                proj_block(pe, 1, f * 2 + (R_GLU + 1), (3, 4, 5), lambda c: pe.wait_ge(on["glu_sig"], count(f * 3)), y_hi, y_lo, 4, YCH)
                proj_block(pe, 0, f * 2 + (R_GLU + 2), (0, 1, 2), lambda c: pe.wait_ge(on["glu_mix"], count(f * 3)), y_hi, y_lo, 4, YCH)

        def glu_act(act):
            for k in range(4):
                act.wait_ge(on["y"][k], 16)
                act.activation(y_hi[:, k, :], yraw[:, k, :], ACT.Copy).then_inc(on["y_hi"], 1)
            act.wait_ge(on["mm"], MM_BA)
            split_hi(act, 1, 16 * (R_GLU // 2 + 1), 512)
            def pair(f, more):
                act.wait_ge(on["mm"], count(f * 6 + MM_GLU))
                split_hi(act, 0, f * 16 + 16 * ((R_GLU + 1) // 2 + 1), 512)
                act.wait_ge(on["glu_mix"], count(f * 3))
                for c, (c0, cw) in enumerate(YCH):
                    act.wait_ge(on["mm"], count(f * 6 + (MM_GLU + c + 1)))
                    act.activation(sgb[:, c0:c0 + cw], ps[3 + c][:, 0:cw], ACT.Sigmoid).then_inc(on["glu_sig"], 1)
                act.wait_ge(on["mm"], count(f * 6 + (MM_GLU + 3)))
                if more:
                    split_hi(act, 1, f * 16 + 16 * ((R_GLU + 2) // 2 + 1), 512)

            with act.Fori(0, 3) as f:
                pair(f, True)
            pair(3, False)

        def glu_dve(dve):
            for k in range(4):
                dve.wait_ge(on["y_hi"], count(k + 1))
                dve.tensor_tensor(y_lo[:, k, :], yraw[:, k, :], y_hi[:, k, :].bitcast(F32), ALU.subtract).then_inc(on["y_lo"], 1)
            split_lo(dve, 1, R_GLU + 1, 512)
            def pair(f, more):
                split_lo(dve, 0, f * 2 + (R_GLU + 2), 512)
                if more:
                    split_lo(dve, 1, f * 2 + (R_GLU + 3), 512)
                for c, (t0, tn) in enumerate(TCH):
                    dve.wait_ge(on["mm"], count(f * 6 + (MM_GLU + 3 + c + 1)))
                    dve.wait_ge(on["glu_sig"], count(f * 3 + (c + 1)))
                    a = ps[c][:, 0:tn * W5].rearrange("p (t w) -> p t w", w=W5)
                    b = sgb[:, t0 * W5:(t0 + tn) * W5].rearrange("p (t w) -> p t w", w=W5)
                    for w0, wn, first in ((0, NCH, 0), (SAMP5, SCH, SEQ)):
                        out = mixT[:, bass.ds(f, 1), first:first + wn * STEP].rearrange("p a (n t) -> p (a t) n", t=STEP)[:, t0:t0 + tn, :]
                        last = dve.tensor_tensor(out, a[:, :, w0:w0 + wn], b[:, :, w0:w0 + wn], ALU.mult)
                    last.then_inc(on["glu_mix"], 1)

            with dve.Fori(0, 3) as f:
                pair(f, True)
            pair(3, False)

        RQ, RK, DD, C1, C2, SSO, RS = 0, 1, 2, 3, 4, 5, 6
        f4 = lambda ap: ap.rearrange("p h c -> p (h c)")
        h4 = lambda bank: ps[bank][:].rearrange("p (h c) -> p h c", c=P)
        hb = lambda h, part: ps[h][:, part * P:(part + 1) * P]
        q_, k_, v_, z_ = 0, HEADS, 2 * HEADS, 3 * HEADS

        def gdn_pe(pe, t, s, loaded, st, ada, mod_at):
            pe.wait_ge(on["mod_row"], count(mod_at))
            pe.wait_ge(on["g_U"], count(t + 1))
            pe.matmul(ps[7][:], ones[:], f4(gU[:]), start=True, stop=True).then_inc(on["g_row"], 1)
            pe.wait_ge(on["stg"][s], count(loaded))
            pe.wait_ge(on["g_ob"], count(t))
            for h in range(HEADS):
                pe.transpose(h4(4)[:, h, :], stg[:, s, q_ + h, :], ident[:])
            pe.wait_ge(on["g_S"], count(t * HEADS))
            for h in range(HEADS):
                pe.matmul(hb(h, 0), stg[:, s, k_ + h, :], stg[:, s, k_ + h, :], start=True, stop=True).then_inc(on["g_KK"], 1)
            pe.wait_ge(on["g_mix"], count(t))
            for h in range(HEADS):
                last = pe.transpose(h4(5)[:, h, :], stg[:, s, k_ + h, :], ident[:])
            last.then_inc(on["g_T"], 1)
            pe.wait_ge(on["mod_cols"], count(mod_at))
            for h in range(HEADS):
                last = pe.transpose(h4(6)[:, h, :], stg[:, s, v_ + h, :], ident[:])
            last.then_inc(on["g_T"], 1)
            pe.wait_ge(on["g_sq"], count(t * 2 + 1))
            for h in range(HEADS):
                last = pe.matmul(h4(4)[:, h, :], stg[:, s, k_ + h, :], stg[:, s, q_ + h, :], start=True, stop=True)
            last.then_inc(on["g_QKp"], 1)
            pe.wait_ge(on["g_kv8"], count(t * 2 + 1))
            for h in range(HEADS):
                pe.wait_ge(on["g_A"], count(t * HEADS + (h + 1)))
                last = pe.transpose(h4(5)[:, h, :], Am[:, h, :], ident[:])
            last.then_inc(on["g_AT"], 1)
            pe.wait_ge(on["g_X0"], count(t * 2 + 2))
            for l in range(LV):
                pe.wait_ge(on["g_L"], count(t * LV + (l + 1)))
                for h in range(HEADS):
                    if l:
                        pe.wait_ge(on["g_X"], count(t * (HEADS * LV) + ((l - 1) * HEADS + h + 1)))
                    pe.matmul(hb(h, 0), Lneg[:, l, h, :], Xb[:, h, 0, :], start=True, stop=True).then_inc(on["g_P"], 1)
                for h in range(HEADS):
                    pe.wait_ge(on["g_Pb"], count(t * (HEADS * LV) + (l * HEADS + h + 1)))
                    if l < LV - 1:
                        pe.matmul(hb(h, 1), Xb[:, h, 1, :], Pb[:, h, :], start=True, stop=True)
                    pe.matmul(hb(h, 2), Pb[:, h, :], Xb[:, h, 1, :], start=True, stop=True).then_inc(on["g_XX"], 1)
            pe.wait_ge(on["g_QK"], count(t + 1))
            pe.wait_ge(on["g_qd"], count(t + 1))
            for h in range(HEADS):
                pe.wait_ge(on["g_X"], count(t * (HEADS * LV) + ((LV - 1) * HEADS + h + 1)))
                pe.matmul(hb(h, 0), stg[:, s, k_ + h, :], Sst[:, st, h, :], start=True, stop=True).then_inc(on["g_kS"], 1)
            for h in range(HEADS):
                pe.wait_ge(on["g_R"], count(t * HEADS + (h + 1)))
                pe.matmul(hb(h, 3), Xb[:, h, 1, :], Rb[:, h, :], start=True, stop=True).then_inc(on["g_V"], 1)
            pe.wait_ge(on["g_ATs"], count(t + 1))
            pe.wait_ge(on["g_kv8"], count(t * 2 + 2))
            for h in range(HEADS):
                pe.wait_ge(on["g_Vb"], count(t * HEADS + (h + 1)))
                pe.matmul(h4(4)[:, h, :], qd[:, h, :], Sst[:, st, h, :], start=True, stop=False)
                pe.matmul(h4(4)[:, h, :], QK[:, h, :], Vb[:, h, :], start=False, stop=True)
                pe.matmul(hb(h, 0), kdec[:, h, :], Vb[:, h, :], start=True, stop=True).then_inc(on["g_kv"], 1)
            if ada is not None:
                pe.wait_ge(on["g_E"], count(t * 3 + 3))
                ada_chunk_pe(pe, ada[1], s)
            pe.wait_ge(on["g_ob"], count(t + 1))
            for h in range(HEADS):
                last = pe.transpose(h4(5)[:, h, :], ob[:, h, :], ident[:])
            last.then_inc(on["g_oT"], 1)
            if ada is not None:
                pe.wait_ge(on["mod_row"], alone(pe, count(ada[0] + 1)))
                for q in range(4):
                    last = pe.transpose(ps[6][:, 2 * q:2 * q + 2], modrow2[:, s, q * P:(q + 1) * P], ident[0:2, 0:2])
                last.then_inc(on["mod_T"], 1)

        def ada_chunk_pe(pe, loaded, s):
            pe.wait_ge(on["ada"][s], count(loaded))
            for k in range(KD):
                last = pe.matmul(ps[7][0:2, :], csil[:, k, :], wada2[:, s, k, :], start=(k == 0), stop=(k == KD - 1))
            last.then_inc(on["ada_mm"], 1)

        def gdn_act(act, t, s, ada):
            act.wait_ge(on["g_T"], count(t * 2 + 1))
            act.wait_ge(on["g_red"], count(t * 2))
            act.activation(sq[:, 0:HEADS, :], h4(4), ACT.Square)
            act.activation(sq[:, HEADS:, :], h4(5), ACT.Square).then_inc(on["g_sq"], 1)
            act.wait_ge(on["g_mm"], count(t * 2 + 2))
            act.activation(EA[:], EA[:], ACT.Exp, scale=-1.0).then_inc(on["g_E"], 1)
            act.activation(EB[:], EB[:], ACT.Exp).then_inc(on["g_E"], 1)
            act.wait_ge(on["g_dd"], count(t + 1))
            act.activation(f4(erow[:]), ps[7][:], ACT.Exp).then_inc(on["g_E"], 1)
            act.wait_ge(on["g_col"], count(t + 1))
            for h in range(HEADS):
                last = act.activation(kdec[:, h, :], h4(5)[:, h, :], ACT.Copy, scale=tilecol[:, s, KDEC, h:h + 1])
            last.then_inc(on["g_kv8"], 1)
            act.wait_ge(on["g_AT"], count(t + 1))
            act.activation(AT[:], h4(5), ACT.Copy).then_inc(on["g_ATs"], 1)
            act.wait_ge(on["g_sc"], count(t + 1))
            act.wait_ge(on["g_T"], count(t * 2 + 2))
            for h in range(HEADS):
                last = act.activation(vp[:, h, :], h4(6)[:, h, :], ACT.Copy, scale=sc[:, C1, h:h + 1])
            last.then_inc(on["g_kv8"], 1)
            for l in range(LV):
                for h in range(HEADS):
                    act.wait_ge(on["g_P"], count(t * (HEADS * LV) + (l * HEADS + h + 1)))
                    act.activation(Pb[:, h, :], hb(h, 0), ACT.Copy).then_inc(on["g_Pb"], 1)
            for h in range(HEADS):
                act.wait_ge(on["g_V"], count(t * HEADS + (h + 1)))
                act.activation(Vb[:, h, :], hb(h, 3), ACT.Copy).then_inc(on["g_Vb"], 1)
            act.wait_ge(on["g_kv"], count(t * HEADS + HEADS))
            act.activation(sq[:, 0:HEADS, :], h4(4), ACT.Square).then_inc(on["g_sq"], 1)
            if ada is not None:
                act.wait_ge(on["mod_row"], count(ada[0] + 1))
                act.dma_start(DR["mod"][:, bass.ds(ada[0] * ADA_N, ADA_N)], modrow2[:, s, :]).then_inc(on["mod_st"][s], 16)

        def gdn_pool(pool, t, s):
            pool.wait_ge(on["g_row"], alone(pool, count(t)))
            pool.tensor_copy(tilecol[:, s, :, :], gcol[:, :, bass.ds(t, 1), :].rearrange("p n a h -> p n (a h)")).then_inc(on["g_col"], 1)
            pool.wait_ge(on["g_col"], alone(pool, count(t + 1)))
            pool.tensor_tensor(gU[:], bc(triu[:], 1, HEADS), bc(tilecol[:, s, GATE, :], 2, P), ALU.mult).then_inc(on["g_U"], 1)
            g = Steps(pool, on["g_pool"], t * 10)
            pool.wait_ge(on["g_red"], alone(pool, count(t * 2 + 1)))
            g(pool.tensor_scalar(sc[:, 0:2, :], sc[:, 7:9, :], RMS_EPS, None, ALU.add))
            g(pool.tensor_tensor(sc[:, 0:2, :], sc[:, 0:2, :], mhalf[:].rearrange("p (a b) -> p a b", a=2), ALU.pow))
            g(pool.tensor_tensor(sc[:, C1, :], sc[:, RK, :], tilecol[:, s, BETA, :], ALU.mult))
            g(pool.tensor_tensor(sc[:, DD, :], sc[:, C1, :], sc[:, RK, :], ALU.mult))
            g(pool.tensor_tensor(sc[:, C2, :], sc[:, DD, :], tilecol[:, s, NEXP, :], ALU.mult))
            g(pool.tensor_scalar(sc[:, RQ, :], sc[:, RQ, :], HD ** -0.5, None, ALU.mult))
            pool.tensor_tensor(sc[:, 9, :], sc[:, RQ, :], sc[:, RQ, :], ALU.mult).then_inc(on["g_sc"], 1)
            pool.wait_ge(on["g_E"], alone(pool, count(t * 3 + 2)))
            pool.tensor_tensor(EB[:], EB[:], bc(triu[:], 1, HEADS), ALU.mult).then_inc(on["g_EB"], 1)
            pool.wait_ge(on["g_ATs"], alone(pool, count(t + 1)))
            for l in range(LV):
                pool.tensor_tensor(Lneg[:, l, :, :], AT[:], bc(maskT[:, l + 1, :], 1, HEADS), ALU.mult).then_inc(on["g_L"], 1)
            pool.wait_ge(on["g_red"], alone(pool, count(t * 2 + 2)))
            pool.wait_ge(on["g_sc"], alone(pool, count(t + 1)))
            g(pool.tensor_tensor(sc[:, RS, :], sc[:, SSO, :], sc[:, 9, :], ALU.mult))
            g(pool.tensor_scalar(sc[:, RS, :], sc[:, RS, :], 1.0 / HD, RMS_EPS, ALU.mult, ALU.add))
            g(pool.tensor_tensor(sc[:, RS, :], sc[:, RS, :], mhalf[:, 0:HEADS], ALU.pow))
            g(pool.tensor_tensor(sc[:, RS, :], sc[:, RS, :], sc[:, RQ, :], ALU.mult))
            assert g.n == 10
            pool.tensor_copy(sc[:, 10, :], sc[:, RS, :]).then_inc(on["g_sc2"], 1)

        def gdn_dve(dve, t, s, st, first, n, ada):
            dve.wait_ge(on["g_row"], count(t + 1))
            dve.wait_ge(on["g_col"], count(t + 1))
            dve.tensor_tensor(dd[:], h4(7), bc(tilecol[:, s, DEC, :], 2, P), ALU.subtract).then_inc(on["g_dd"], 1)
            dve.wait_ge(on["g_dd"], count(t + 1))
            dve.tensor_scalar(EA[:], dd[:], 0.0, None, ALU.max).then_inc(on["g_mm"], 1)
            dve.tensor_scalar(EB[:], dd[:], 0.0, None, ALU.min).then_inc(on["g_mm"], 1)
            dve.wait_ge(on["g_sq"], count(t * 2 + 1))
            dve.wait_ge(on["g_sc2"], count(t))
            dve.tensor_reduce(sc[:, 7:9, :].rearrange("p a h -> p (a h)"), sq[:], mybir.AxisListType.X, ALU.add).then_inc(on["g_red"], 1)
            dve.wait_ge(on["g_pool"], count(t * 10 + 4))
            dve.wait_ge(on["g_E"], count(t * 3 + 1))
            for h in range(HEADS):
                dve.wait_ge(on["g_KK"], count(t * HEADS + (h + 1)))
                dve.scalar_tensor_tensor(out=Am[:, h, :], in0=hb(h, 0), scalar=sc[:, DD, h:h + 1], in1=EA[:, h, :],
                                              op0=ALU.mult, op1=ALU.mult).then_inc(on["g_A"], 1)
            dve.wait_ge(on["g_A"], count(t * HEADS + HEADS))
            dve.wait_ge(on["g_V"], count(t * HEADS))
            dve.tensor_tensor(Xb[:, :, 0, :], Am[:], bc(mask1[:], 1, HEADS), ALU.mult).then_inc(on["g_Xm"], 1)
            dve.wait_ge(on["g_Xm"], count(t * 2 + 1))
            dve.tensor_tensor(Xb[:, :, 0, :], Xb[:, :, 0, :], bc(ident[:], 1, HEADS), ALU.add).then_inc(on["g_X0"], 1)
            dve.wait_ge(on["g_ATs"], count(t + 1))
            dve.tensor_tensor(Xb[:, :, 1, :], AT[:], bc(maskT[:, 0, :], 1, HEADS), ALU.mult).then_inc(on["g_Xm"], 1)
            dve.wait_ge(on["g_Xm"], count(t * 2 + 2))
            dve.tensor_tensor(Xb[:, :, 1, :], Xb[:, :, 1, :], bc(ident[:], 1, HEADS), ALU.add).then_inc(on["g_X0"], 1)
            dve.wait_ge(on["g_sc"], count(t + 1))
            dve.wait_ge(on["g_E"], count(t * 3 + 3))
            dve.wait_ge(on["g_EB"], count(t + 1))
            dve.wait_ge(on["g_QKp"], count(t + 1))
            dve.tensor_tensor(QK[:], h4(4), EB[:], ALU.mult).then_inc(on["g_QK"], 1)
            dve.tensor_tensor(qd[:], stg[:, s, 0:HEADS, :], erow[:], ALU.mult).then_inc(on["g_qd"], 1)
            dve.wait_ge(on["g_X0"], count(t * 2 + 2))
            for l in range(LV):
                for h in range(HEADS):
                    dve.wait_ge(on["g_XX"], count(t * (HEADS * LV) + (l * HEADS + h + 1)))
                    dve.wait_ge(on["g_X"], count(t * (HEADS * LV) + max(0, l - 1) * HEADS + (h + 1 if l else 0)))
                    lo = 0 if l < LV - 1 else 1
                    src = ps[h][:, P:3 * P].rearrange("p (x c) -> p x c", x=2)
                    dve.tensor_tensor(Xb[:, h, lo:2, :], Xb[:, h, lo:2, :], src[:, lo:2, :], ALU.add).then_inc(on["g_X"], 1)
            dve.wait_ge(on["g_kv8"], count(t * 2 + 2))
            for h in range(HEADS):
                dve.wait_ge(on["g_kS"], count(t * HEADS + (h + 1)))
                dve.scalar_tensor_tensor(out=Rb[:, h, :], in0=hb(h, 0), scalar=sc[:, C2, h:h + 1], in1=vp[:, h, :],
                                              op0=ALU.mult, op1=ALU.add).then_inc(on["g_R"], 1)
            for h in range(HEADS):
                dve.wait_ge(on["g_kv"], count(t * HEADS + (h + 1)))
                dve.wait_ge(on["g_S"], count(t * HEADS))
                dve.scalar_tensor_tensor(out=Sst[:, st, h, :], in0=Sst[:, st, h, :], scalar=tilecol[:, s, GLAST, h:h + 1],
                                              in1=hb(h, 0), op0=ALU.mult, op1=ALU.add).then_inc(on["g_S"], 1)
            dve.wait_ge(on["g_sq"], count(t * 2 + 2))
            dve.tensor_reduce(sc[:, SSO, :], sq[:, 0:HEADS, :], mybir.AxisListType.X, ALU.add).then_inc(on["g_red"], 1)
            dve.wait_ge(on["g_sc2"], count(t + 1))
            dve.wait_ge(on["g_oT"], count(t))
            dve.tensor_tensor(ob[:], h4(4), bc(sc[:, 10, :], 2, P), ALU.mult).then_inc(on["g_ob"], 1)
            if ada is not None:
                dve.wait_ge(on["ada"][s], count(ada[1]))
                dve.wait_ge(on["ada_mm"], count(ada[0] + 1))
                dve.wait_ge(on["mod_st"][s], count(ada[2]))
                dve.tensor_tensor(modrow2[:, s, :], ps[7][0:2, :], bada2[:], ALU.add).then_inc(on["mod_row"], 1)
            dve.wait_ge(on["g_oT"], count(t + 1))
            out = mixT[:, HEADS:, first] if not isinstance(first, int) else mixT[:, HEADS:, first:first + n]
            dve.scalar_tensor_tensor(out=out, in0=h4(5)[:, :, 0:n], scalar=normg[:, 0:1], in1=stg[:, s, z_:, 0:n],
                                          op0=ALU.mult, op1=ALU.mult).then_inc(on["g_mix"], 1)
            if ada is not None:
                dve.wait_ge(on["mod_T"], count(ada[0] + 1))
                dve.tensor_copy(modc[:, bass.ds(ada[0], 1), :, :].rearrange("p c q t -> p (c q) t"),
                                     ps[6][:, 0:8].rearrange("p (q t) -> p q t", t=2)).then_inc(on["mod_cols"], 1)

        R_WO = R_GLU + 8
        R_FF = R_WO + KD
        MM_FF = MM_GLU + 3 * 8
        G1_AT, G2_AT = 2 * D_MODEL, 5 * D_MODEL

        def wo_steps(eng, step):
            step(0, 0)
            step(1, 1)
            with eng.Fori(0, 2) as i:
                for s in range(2):
                    step(i * 2 + (2 + s), s)
            for t in range(6, TILES):
                step(t, t % 2)

        def tile_rows(t):
            return DEC_SEQ if isinstance(t, int) and t == PTILES else P

        def tile_cols(t):
            return bass.ds(t * P, P) if not isinstance(t, int) else slice(t * P, t * P + tile_rows(t))

        slot_of = lambda j: (R_FF + j) % 2
        loaded = lambda i, j: i * 48 + 16 * ((R_FF + j) // 2 + 1)
        FIRST = {(0, 0): 1, (0, 1): 2, (1, 0): 3, (1, 1): 4, (0, 2): 5, (1, 2): 6}

        def mm_of(i, j, c):
            if isinstance(i, int) and (i, j) in ((0, 0), (0, 1)):
                return MM_FF + FIRST[j, c]
            return i * 12 + (MM_FF + 3 * j + c + 1)

        def ffn_block(pe, i, j, chunks=(0, 1, 2)):
            first = isinstance(i, int) and i == 0 and j < 2

            def bank_free(n):
                c = chunks[n]
                if first:
                    pe.wait_ge(on["o_tmp"], since("o_tmp", 2 * TILES))
                    pe.wait_ge(on["h2_lo"], since("h2_lo", min(TILES, 3 * (c + 1))))
                elif j % 2 == 0:
                    pe.wait_ge(on["f_sil"], count(i * 6 + (3 * (j // 2) + c - 2)))
                else:
                    pe.wait_ge(on["f_mul"], since("f_mul", i * 6 + (3 * (j // 2) + c - 2)))
            proj_block(pe, slot_of(j), i * 6 + (R_FF + j + 1), [3 * (j % 2) + c for c in chunks],
                       bank_free, hT_hi, hT_lo, chunks=[CH[c] for c in chunks])

        def ffn_hi(act, i, j):
            act.wait_ge(on["mm"], mm_of(i, j - 2, 2) if j >= 2 else count(i * 12 + (MM_FF + 3 * (j - 1))))
            split_hi(act, slot_of(j), loaded(i, j))

        def ffn_lo(dve, i, j):
            split_lo(dve, slot_of(j), i * 6 + (R_FF + j + 1))

        def wo_pe(pe):
            pe.wait_ge(on["g_mix"], TILES)

            def transposes(u, s):
                n = tile_rows(u)
                pe.wait_ge(on["o_n2"], since("o_n2", u + 1))
                pe.wait_ge(on["h2_mod"], since("h2_mod", u))
                for k in range(KD):
                    last = pe.transpose(ps[6 + k // 4][:, (k % 4) * P:(k % 4) * P + n], xn2[0:n, s, k * P:(k + 1) * P], ident[0:n, 0:n])
                last.then_inc(on["o_T"], 1)

            def step(t, s):
                n = tile_rows(t)
                pe.wait_ge(on["ms_lo"], since("ms_lo", t + 1))
                pe.wait_ge(on["o_tmp"], since("o_tmp", t * 2 - 2))
                for k in range(KD):
                    pe.wait_ge(on["w_lo"], count(R_WO + k + 1))
                    for h in range(2):
                        cols = slice(h * 512, (h + 1) * 512)
                        for m, (a, w) in enumerate(((whi, wo_hi), (whi, wo_lo), (wlo, wo_hi))):
                            last = pe.matmul(ps[2 * s + h][0:n, :], a[:, s, k * P:k * P + n], w[:, k, cols],
                                             start=(k == 0 and m == 0), stop=(k == KD - 1 and m == 2))
                last.then_inc(on["wo_mm"], 1)
                if not (isinstance(t, int) and t < 2):
                    transposes(t - 2, s)

            wo_steps(pe, step)
            for j in range(2):
                ffn_block(pe, 0, j, (0, 1))
                transposes(PTILES - 1 + j, (PTILES - 1 + j) % 2)
            for j in range(2):
                ffn_block(pe, 0, j, (2,))

        def tile_hi(act, t, s):
            n = tile_rows(t)
            act.wait_ge(on["wo_mm"], since("wo_mm", t - 1))
            act.activation(whi[:, s, :].rearrange("p (k c) -> p k c", c=P)[:, :, 0:n], mixT[:, :, tile_cols(t)], ACT.Copy).then_inc(on["ms_hi"], 1)

        def tile_lo(dve, t, s):
            n = tile_rows(t)
            v = lambda x: x[:, s, :].rearrange("p (k c) -> p k c", c=P)[:, :, 0:n]
            dve.wait_ge(on["ms_hi"], since("ms_hi", t + 1))
            dve.tensor_tensor(v(wlo), mixT[:, :, tile_cols(t)], v(whi).bitcast(F32), ALU.subtract).then_inc(on["ms_lo"], 1)

        def normalise(act, out, in_, n, rs, name):
            act.activation(out, in_, ACT.Identity, bias=rstd[0:n, rs, 1:2], scale=rstd[0:n, rs, 0:1]).then_inc(name, 1)

        def wo_act(act):
            act.wait_ge(on["g_mix"], TILES)
            for t in range(2):
                tile_hi(act, t, t)
            for k in range(KD):
                r = R_WO + k
                act.wait_ge(on["raw"][r % 2], count(16 * (r // 2 + 1)))
                act.activation(wo_hi[:, k, :], wraw[:, r % 2, :], ACT.Copy).then_inc(on["w_hi"], 1)

            def modulate(u):
                n, tok = tile_rows(u), 0 if tile_rows(u) == P else 1
                act.wait_ge(on["h2_lo"], since("h2_lo", u))
                act.wait_ge(on["h2_scale"], 1)
                act.wait_ge(on["o_T"], since("o_T", u + 1))
                for k in range(KD):
                    last = act.activation(hp2[:, k, 0:n], ps[6 + k // 4][:, (k % 4) * P:(k % 4) * P + n], ACT.Identity,
                                          scale=onep[:, 1, k, tok:tok + 1], bias=modc[:, 6 + k // 4, k % 4, tok:tok + 1])
                last.then_inc(on["h2_mod"], 1)

            def step(t, s):
                n = tile_rows(t)
                if isinstance(t, int) and t == PTILES:
                    for j in range(2):
                        act.wait_ge(on["wo_mm"], since("wo_mm", PTILES + j))
                        ffn_hi(act, 0, j)
                if not (isinstance(t, int) and t < 2):
                    modulate(t - 2)
                if not (isinstance(t, int) and t > PTILES - 2):
                    tile_hi(act, t + 2, s)
                act.wait_ge(on["o_rs"], since("o_rs", t * 2 + 1))
                act.wait_ge(on["o_bn"], since("o_bn", t * 4 + 2))
                normalise(act, xt[0:n, s, :], xt[0:n, s, :], n, 0, on["o_n1"])
                act.wait_ge(on["o_rs"], since("o_rs", t * 2 + 2))
                act.wait_ge(on["x1_ready"], since("x1_ready", t + 1))
                act.wait_ge(on["o_T"], since("o_T", t - 1))
                normalise(act, xn2[0:n, s, :], xt[0:n, s, :], n, 1, on["o_n2"])

            wo_steps(act, step)
            modulate(PTILES - 1)
            modulate(PTILES)

        def wo_dve(dve):
            dve.wait_ge(on["mod_cols"], 12)
            dve.tensor_scalar(onep[:, 1, :, :], modc[:, 8:10, :, :].rearrange("p a q t -> p (a q) t"), 1.0, None, ALU.add).then_inc(on["h2_scale"], 1)
            for t in range(2):
                tile_lo(dve, t, t)
            dve.wait_ge(on["mod_st"][0], 64)
            dve.wait_ge(on["mod_st"][1], 64)
            dve.wait_ge(on["state_out"], 32)
            for k in range(KD):
                dve.wait_ge(on["w_hi"], count(R_WO + k + 1))
                dve.tensor_tensor(wo_lo[:, k, :], wraw[:, (R_WO + k) % 2, :], wo_hi[:, k, :].bitcast(F32), ALU.subtract).then_inc(on["w_lo"], 1)

            def stats(x, n, slot, bn, name):
                for h in range(2):
                    dve.bn_stats(stat[0:n, slot, 6 * h:6 * h + 6], x[:, h * 512:(h + 1) * 512]).then_inc(on["o_bn"], 1)
                dve.wait_ge(on["o_bn"], alone(dve, since("o_bn", bn)))
                dve.bn_aggr(stat[0:n, slot, 12:14], stat[0:n, slot, 0:12]).then_inc(name, 1)

            def split_h2(u):
                n = tile_rows(u)
                dve.wait_ge(on["h2_mod"], since("h2_mod", u + 1))
                dve.tensor_copy(hT_hi[:, :, tile_cols(u)], hp2[:, :, 0:n]).then_inc(on["h2_hi"], 1)
                dve.wait_ge(on["h2_hi"], since("h2_hi", u + 1))
                dve.tensor_tensor(hT_lo[:, :, tile_cols(u)], hp2[:, :, 0:n], hT_hi[:, :, tile_cols(u)].bitcast(F32), ALU.subtract).then_inc(on["h2_lo"], 1)

            def step(t, s):
                n = tile_rows(t)
                dve.wait_ge(on["wo_mm"], since("wo_mm", t + 1))
                dve.wait_ge(on["o_g1"], since("o_g1", 2 if n < P else 1))
                dve.wait_ge(on["o_r"], since("o_r", t))
                for h in range(2):
                    row = (g1s if n < P else g1r)[0:n, h * 512:(h + 1) * 512]
                    dve.tensor_tensor(otmp[0:n, h * 512:(h + 1) * 512], ps[2 * s + h][0:n, :], row, ALU.mult).then_inc(on["o_tmp"], 1)
                dve.wait_ge(on["o_tmp"], since("o_tmp", t * 2 + 2))
                dve.wait_ge(on["xt"][s], count((t - s) * 8 + 16))
                dve.scalar_tensor_tensor(out=xt[0:n, s, :], in0=xt[0:n, s, :], scalar=ALPHA, in1=otmp[0:n, :],
                                              op0=ALU.mult, op1=ALU.add).then_inc(on["o_r"], 1)
                dve.wait_ge(on["o_r"], since("o_r", t + 1))
                if isinstance(t, int) and t == PTILES:
                    for j in range(2):
                        ffn_lo(dve, 0, j)
                stats(xt[0:n, s, :], n, 0, t * 4 + 2, on["o_mv"])
                if not (isinstance(t, int) and t < 2):
                    split_h2(t - 2)
                dve.wait_ge(on["o_n1"], since("o_n1", t + 1))
                dve.wait_ge(on["ln1_rows"], 32)
                dve.tensor_tensor(xt[0:n, s, :], xt[0:n, s, :], ln1r[0:n, 0, :], ALU.mult).then_inc(on["o_xg"], 1)
                if not (isinstance(t, int) and t > PTILES - 2):
                    tile_lo(dve, t + 2, s)
                dve.wait_ge(on["x1_ready"], since("x1_ready", t + 1))
                stats(xt[0:n, s, :], n, 1, t * 4 + 4, on["o_mv"])

            wo_steps(dve, step)
            split_h2(PTILES - 1)
            split_h2(PTILES)

        def rstd_steps(pool, g, n, slot, eps, name):
            g(pool.tensor_scalar(rstd[0:n, slot, 0:1], stat[0:n, slot, 13:14], eps, None, ALU.add))
            g(pool.tensor_tensor(rstd[0:n, slot, 0:1], rstd[0:n, slot, 0:1], mhalf[0:n, 0:1], ALU.pow))
            pool.tensor_scalar(rstd[0:n, slot, 1:2], stat[0:n, slot, 12:13], rstd[0:n, slot, 0:1], -1.0, ALU.mult, ALU.mult).then_inc(name, 1)

        def wo_pool(pool):
            pool.wait_ge(on["g1_row"], 32)
            pool.tensor_scalar(g1r[:], g1r[:], 1.0, None, ALU.add).then_inc(on["o_g1"], 1)
            pool.tensor_scalar(g1s[0:DEC_SEQ, :], g1s[0:DEC_SEQ, :], 1.0, None, ALU.add).then_inc(on["o_g1"], 1)

            def step(t, s):
                n = tile_rows(t)
                g = Steps(pool, on["o_p"], since("o_p", t * 4))
                pool.wait_ge(on["o_mv"], alone(pool, since("o_mv", t * 2 + 1)))
                pool.wait_ge(on["o_n1"], alone(pool, since("o_n1", t)))
                rstd_steps(pool, g, n, 0, LN_EPS, on["o_rs"])
                pool.wait_ge(on["o_xg"], alone(pool, since("o_xg", t + 1)))
                pool.tensor_tensor(xt[0:n, s, :], xt[0:n, s, :], ln1r[0:n, 1, :], ALU.add).then_inc(on["x1_ready"], 1)
                pool.wait_ge(on["o_mv"], alone(pool, since("o_mv", t * 2 + 2)))
                pool.wait_ge(on["o_n2"], alone(pool, since("o_n2", t)))
                rstd_steps(pool, g, n, 1, LN_EPS, on["o_rs"])

            wo_steps(pool, step)

        def mod_row_of(stream, at_col, n):
            return DR["mod"][stream:stream + 1, at_col:at_col + D_MODEL].to_broadcast([n, D_MODEL])

        def wo_loads(sp):
            sp.wait_ge(on["mod_cols"], 12)
            sp.wait_ge(on["g_mix"], TILES)
            sp.wait_ge(on["mod_st"][0], 16)
            sp.wait_ge(on["mod_st"][1], 16)
            sp.dma_start(g1r[:], mod_row_of(0, G1_AT, P)).then_inc(on["g1_row"], 16)
            for s in range(2):
                sp.dma_start(xt[:, s, :], I["x_prompt"][s * P:(s + 1) * P, :]).then_inc(on["xt"][s], 16)
            sp.dma_start(g1s[0:DEC_SEQ, :], mod_row_of(1, G1_AT, DEC_SEQ)).then_inc(on["g1_row"], 16)
            for n in range(2):
                sp.dma_start(ln1r[:, n, :], I["ln_rows"][n:n + 1, :].to_broadcast([P, D_MODEL])).then_inc(on["ln1_rows"], 16)
            for k in range(2, KD):
                sp.wait_ge(on["w_lo"], count(R_WO + k - 1))
                sp.dma_start(wraw[:, (R_WO + k) % 2, :], I["w_out"][k * P:(k + 1) * P, :]).then_inc(on["raw"][(R_WO + k) % 2], 16)
            for q in range(2):
                up_load(sp, 0, q)

            def step(t, s):
                n = tile_rows(t)
                sp.wait_ge(on["x1_ready"], since("x1_ready", t + 1))
                sp.dma_start(DR["x1"][tile_cols(t), :], xt[0:n, s, :]).then_inc(on["x1_st"][s], 16)
                sp.wait_ge(on["o_n2"], since("o_n2", t + 1))
                sp.wait_ge(on["x1_st"][s], count((t - s) * 8 + 16))
                if isinstance(t, int) and t >= PTILES - 2:
                    if t == PTILES - 2:
                        sp.dma_start(xt[0:DEC_SEQ, 0, :], I["x_sample"]).then_inc(on["xt"][0], 16)
                else:
                    nxt = bass.ds(t * P + 2 * P, P) if not isinstance(t, int) else slice((t + 2) * P, (t + 3) * P)
                    sp.dma_start(xt[:, s, :], I["x_prompt"][nxt, :]).then_inc(on["xt"][s], 16)

            wo_steps(sp, step)

        FI = FB // 2
        wup = I["w_up"].rearrange("(k p) n -> p k n", p=P)

        def up_load(sp, i, j):
            sl = slot_of(j)
            sp.wait_ge(on["w_lo"], alone(sp, count(i * 6 + (R_FF + j - 1))))
            if j < 4:
                col = i * 2 * P + ((j // 2) * P + (j % 2) * D_FF)
                cols = slice(col, col + P) if isinstance(col, int) else bass.ds(col, P)
                sp.dma_start(wraw[:, sl, :].rearrange("p (k n) -> p k n", k=KD), wup[:, :, cols]).then_inc(on["raw"][sl], 16)
            else:
                row = i * 2 * P + (j - 4) * P
                rows = slice(row, row + P) if isinstance(row, int) else bass.ds(row, P)
                sp.dma_start(wraw[:, sl, :], I["w_down"][rows, :]).then_inc(on["raw"][sl], 16)

        def ffn_loads(sp):
            sp.wait_ge(on["wo_mm"], since("wo_mm", TILES))
            for j in range(2, 6):
                up_load(sp, 0, j)
            sp.wait_ge(on["x1_st"][0], 16 * (PTILES // 2 + 1))
            sp.wait_ge(on["x1_st"][1], 16 * (PTILES // 2))
            sp.wait_ge(on["x1_ready"], since("x1_ready", TILES))
            sp.wait_ge(on["mod_st"][0], 64)
            sp.wait_ge(on["mod_st"][1], 64)
            sp.dma_start(acc[:, 0:PTILES, :], DR["x1"][0:SEQ, :].rearrange("(t p) n -> p t n", p=P)).then_inc(on["acc_in"], 16)
            sp.dma_start(acc[0:DEC_SEQ, PTILES, :], DR["x1"][SEQ:TOK, :]).then_inc(on["acc_in"], 16)
            sp.dma_start(g2r[:, 0, :], mod_row_of(0, G2_AT, P)).then_inc(on["g2_row"], 16)
            sp.dma_start(g2r[0:DEC_SEQ, 1, :], mod_row_of(1, G2_AT, DEC_SEQ)).then_inc(on["g2_row"], 16)
            with sp.Fori(1, FI) as i:
                for j in range(6):
                    up_load(sp, i, j)
            sp.wait_ge(on["mm"], MM_FF + 12 * FI)
            for n in range(2):
                sp.dma_start(ln2r[:, n, :], I["ln_rows"][2 + n:3 + n, :].to_broadcast([P, D_MODEL])).then_inc(on["ln2_rows"], 16)
            with sp.Fori(0, PTILES) as t:
                sp.wait_ge(on["y_ready"], since("y_ready", t + 1))
                sp.dma_start(O["y_prompt"][bass.ds(t * P, P), :], acc[:, bass.ds(t, 1), :].rearrange("p a n -> p (a n)")).then_inc(on["out"], 16)
            sp.wait_ge(on["y_ready"], since("y_ready", TILES))
            sp.dma_start(O["y_sample"], acc[0:DEC_SEQ, PTILES, :]).then_inc(on["out"], 16)

        def ffn_pool(pool):
            pool.wait_ge(on["g2_row"], 32)
            pool.tensor_scalar(g2r[:, 0, :], g2r[:, 0, :], 1.0, 1.0 / ALPHA, ALU.add, ALU.mult).then_inc(on["f_g2"], 1)
            pool.tensor_scalar(g2r[0:DEC_SEQ, 1, :], g2r[0:DEC_SEQ, 1, :], 1.0, 1.0 / ALPHA, ALU.add, ALU.mult).then_inc(on["f_g2"], 1)
            pool.wait_ge(on["ln2_rows"], 32)

            def step(t, s, n):
                a = acc_tile(t, n)
                g = Steps(pool, on["f_p"], since("f_p", t * 2))
                pool.wait_ge(on["f_mv"], alone(pool, count(t + 1)))
                pool.wait_ge(on["f_n"], alone(pool, count(t - 1 if isinstance(t, int) else t)))
                rstd_steps(pool, g, n, s, LN_EPS / ALPHA ** 2, on["f_rs"])
                pool.wait_ge(on["f_xg"], alone(pool, count(t + 1)))
                pool.tensor_tensor(a, a, ln2r[0:n, 1, :], ALU.add).then_inc(on["y_ready"], 1)

            final_steps(pool, step)

        def acc_tile(t, n):
            return acc[0:n, t, :] if isinstance(t, int) else acc[0:n, bass.ds(t, 1), :].rearrange("p a n -> p (a n)")

        def final_steps(eng, step):
            with eng.Fori(0, PTILES // 2) as i:
                for s in range(2):
                    step(i * 2 + s, s, P)
            step(PTILES, 0, DEC_SEQ)

        def ffn_down_pe(pe, i):
            pe.wait_ge(on["w_lo"], count(i * 6 + R_FF))
            pe.wait_ge(on["f_lo"], since("f_lo", i * 6))
            for t in range(TILES):
                n = tile_rows(t)
                cols = slice(t * P, t * P + n)
                for h in range(2):
                    pe.wait_ge(on["f_tmp"], count(i * 2 * TILES + (t * 2 + h - 2 * TILES - (1 if t + h else 0))))
                    for b in range(2):
                        for m, (a, w) in enumerate(((hid_hi, wd_hi), (hid_hi, wd_lo), (hid_lo, wd_hi))):
                            last = pe.matmul(ps[6 + h][0:n, :], a[:, b, cols], w[:, b, h * 512:(h + 1) * 512],
                                             start=(b == 0 and m == 0), stop=(b == 1 and m == 2))
                    last.then_inc(on["f_dn"], 1)

        def ffn_pe(pe):
            for j in range(2, 4):
                ffn_block(pe, 0, j)
            with pe.Fori(1, FI) as i:
                ffn_block(pe, i, 0)
                ffn_down_pe(pe, i)
                for j in range(1, 4):
                    ffn_block(pe, i, j)
            ffn_down_pe(pe, FI)

        def ffn_act(act):
            def silu(i, b):
                for c, (c0, cw) in enumerate(CH):
                    act.wait_ge(on["f_lo"], since("f_lo", i * 6 + (3 * b - 3 + c + 1)))
                    act.wait_ge(on["mm"], mm_of(i, 2 * b, c))
                    act.activation(sil[:, c0:c0 + cw], ps[c][:, 0:cw], ACT.Silu).then_inc(on["f_sil"], 1)

            def hidden_hi(i, b):
                act.wait_ge(on["f_dn"], since("f_dn", i * 2 * TILES))
                for c, (c0, cw) in enumerate(CH):
                    act.wait_ge(on["f_mul"], since("f_mul", i * 6 + (3 * b + c + 1)))
                    act.activation(hid_hi[:, b, c0:c0 + cw], sil[:, c0:c0 + cw], ACT.Copy).then_inc(on["f_hi"], 1)

            def turn(i, more):
                if not isinstance(i, int) or i:
                    ffn_hi(act, i, 1)
                silu(i, 0)
                ffn_hi(act, i, 2)
                hidden_hi(i, 0)
                ffn_hi(act, i, 3)
                silu(i, 1)
                for b in range(2):
                    sl = slot_of(4 + b)
                    act.wait_ge(on["raw"][sl], count(loaded(i, 4 + b)))
                    act.wait_ge(on["f_dn"], since("f_dn", i * 2 * TILES))
                    act.activation(wd_hi[:, b, :], wraw[:, sl, :], ACT.Copy).then_inc(on["w_hi"], 1)
                if more:
                    ffn_hi(act, i + 1, 0)
                hidden_hi(i, 1)

            for s in range(2):
                act.wait_ge(on["x1_st"][s], 16 * (PTILES // 2 + 1 - s))
            turn(0, True)
            with act.Fori(1, FI - 1) as i:
                turn(i, True)
            turn(FI - 1, False)

            def step(t, s, n):
                act.wait_ge(on["f_rs"], since("f_rs", t + 1))
                a = acc_tile(t, n)
                normalise(act, a, a, n, s, on["f_n"])

            final_steps(act, step)

        def ffn_dve(dve):
            def down_tile(i, t):
                n = tile_rows(t)
                row = g2r[0:n, 1 if n < P else 0, :]
                for h in range(2):
                    cols, k = slice(h * 512, (h + 1) * 512), t * 2 + h - 2 * TILES
                    dve.wait_ge(on["f_dn"], since("f_dn", i * 2 * TILES + (k + 1)))
                    dve.wait_ge(on["f_add"], count(i * 2 * TILES + (k - (1 if t + h else 0))))
                    dve.tensor_tensor(dtmp[0:n, cols], ps[6 + h][0:n, :], row[:, cols], ALU.mult).then_inc(on["f_tmp"], 1)
                for h in range(2):
                    cols, k = slice(h * 512, (h + 1) * 512), t * 2 + h - 2 * TILES
                    dve.wait_ge(on["f_tmp"], count(i * 2 * TILES + (k + 1)))
                    dve.tensor_tensor(acc[0:n, t, cols], acc[0:n, t, cols], dtmp[0:n, cols], ALU.add).then_inc(on["f_add"], 1)

            def multiply(i, b):
                for c, (c0, cw) in enumerate(CH):
                    dve.wait_ge(on["f_sil"], count(i * 6 + (3 * b + c + 1)))
                    dve.wait_ge(on["mm"], mm_of(i, 2 * b + 1, c))
                    dve.tensor_tensor(sil[:, c0:c0 + cw], sil[:, c0:c0 + cw], ps[3 + c][:, 0:cw], ALU.mult).then_inc(on["f_mul"], 1)

            def hidden_lo(i, b):
                for c, (c0, cw) in enumerate(CH):
                    dve.wait_ge(on["f_hi"], since("f_hi", i * 6 + (3 * b + c + 1)))
                    dve.tensor_tensor(hid_lo[:, b, c0:c0 + cw], sil[:, c0:c0 + cw], hid_hi[:, b, c0:c0 + cw].bitcast(F32),
                                           ALU.subtract).then_inc(on["f_lo"], 1)

            def turn(i, down, more):
                if down:
                    ffn_lo(dve, i, 1)
                if down:
                    for t in range(TILES):
                        down_tile(i, t)
                ffn_lo(dve, i, 2)
                multiply(i, 0)
                hidden_lo(i, 0)
                ffn_lo(dve, i, 3)
                for b in range(2):
                    dve.wait_ge(on["w_hi"], count(i * 6 + (R_FF + 5 + b)))
                    dve.tensor_tensor(wd_lo[:, b, :], wraw[:, slot_of(4 + b), :], wd_hi[:, b, :].bitcast(F32), ALU.subtract).then_inc(on["w_lo"], 1)
                if more:
                    ffn_lo(dve, i + 1, 0)
                multiply(i, 1)
                hidden_lo(i, 1)

            turn(0, False, True)
            dve.wait_ge(on["acc_in"], 32)
            dve.wait_ge(on["f_g2"], since("f_g2", 2))
            with dve.Fori(1, FI - 1) as i:
                turn(i, True, True)
            turn(FI - 1, True, False)
            for t in range(TILES + 1):
                if t < TILES:
                    n, s = tile_rows(t), t % 2
                    down_tile(FI, t)
                    dve.wait_ge(on["f_add"], count(2 * TILES * (FI - 1) + 2 * t + 2))
                    dve.wait_ge(on["f_rs"], since("f_rs", t - 1))
                    for h in range(2):
                        dve.bn_stats(stat[0:n, s, 6 * h:6 * h + 6], acc[0:n, t, h * 512:(h + 1) * 512]).then_inc(on["f_bn"], 1)
                    dve.wait_ge(on["f_bn"], count(t * 2 + 2))
                    dve.bn_aggr(stat[0:n, s, 12:14], stat[0:n, s, 0:12]).then_inc(on["f_mv"], 1)
                if t:
                    u = t - 1
                    n = tile_rows(u)
                    dve.wait_ge(on["ln2_rows"], 32)
                    dve.wait_ge(on["f_n"], count(u + 1))
                    dve.tensor_tensor(acc[0:n, u, :], acc[0:n, u, :], ln2r[0:n, 0, :], ALU.mult).then_inc(on["f_xg"], 1)

        block = ctx.enter_context(nc.Block())

        @block.sync
        def _(sp):
            loads_before(sp)
            loads_projection(sp)
            wglu = I["w_glu"].rearrange("(k p) n -> p k n", p=P)

            def glu_piece(slot, col, free):
                sp.wait_ge(on["w_lo"], alone(sp, count(free)))
                sp.dma_start(wraw[:, slot, 0:512].rearrange("p (k n) -> p k n", k=4), wglu[:, :, col]).then_inc(on["raw"][slot], 16)

            glu_piece(1, slice(512, 640), R_GLU - 1)
            sp.wait_ge(on["y_stored"], NB5 * STEP * 16)
            sp.wait_ge(on["row_stored"][0], 2 * NB5 * 16)
            sp.wait_ge(on["row_stored"][1], 2 * NB5 * 16)
            sp.wait_ge(on["s5_h"], NB5)
            for k in range(4):
                sp.dma_start(yraw[:, k, :].rearrange("p (t w) -> p t w", t=STEP), DR["y"][k * GB:(k + 1) * GB].rearrange("g i t w -> (g i) t w")).then_inc(on["y"][k], 16)
            glu_piece(0, slice(0, P), R_GLU)
            with sp.Fori(1, 4) as f:
                glu_piece(1, bass.ds(f * P + 512, P), f * 2 + (R_GLU - 1))
                glu_piece(0, bass.ds(f * P, P), f * 2 + R_GLU)
            sp.wait_ge(on["gate_T"], 1)
            rows = DR["rows"].rearrange("a p w -> p a w")

            def ada_load(c, s):
                sp.wait_ge(on["ada_mm"], count(c - 1))
                sp.dma_start(wada2[:, s, :, :], wad[:, :, bass.ds(c * ADA_N, ADA_N)]).then_inc(on["ada"][s], 16)
                sp.wait_ge(on["mod_row"], count(c))
                sp.dma_start(bada2[:], I["b_ada"][:, bass.ds(c * ADA_N, ADA_N)]).then_inc(on["ada"][s], 16)

            for s in range(2):
                sp.dma_start(stg[:, s, :, :], rows[:, :, s * P:(s + 1) * P]).then_inc(on["stg"][s], 16)
                ada_load(4 + s, s)
            for k in range(2):
                sp.wait_ge(on["w_lo"], count(R_WO + k - 1))
                sp.dma_start(wraw[:, (R_WO + k) % 2, :], I["w_out"][k * P:(k + 1) * P, :]).then_inc(on["raw"][(R_WO + k) % 2], 16)
            sp.wait_ge(on["glu_mix"], 12)
            sp.dma_start(Sst[:, 1, :, :], I["state_gdn"].rearrange("h k v -> k h v")).then_inc(on["s_state"], 16)
            with sp.Fori(1, PTILES // 2) as i:
                for s in range(2):
                    sp.wait_ge(on["g_mix"], count(i * 2 + (s - 1)))
                    sp.dma_start(stg[:, s, :, :], rows[:, :, bass.ds(i * 2 * P + s * P, P)]).then_inc(on["stg"][s], 16)
                    ada_load(i * 2 + (4 + s), s)
            sp.wait_ge(on["g_mix"], PTILES - 1)
            sp.dma_start(stg[:, 0, :, :], rows[:, :, SAMP_COL:SAMP_COL + P]).then_inc(on["stg"][0], 16)
            sp.wait_ge(on["g_S"], PTILES * HEADS)
            sp.dma_start(O["gdn_states"][0].rearrange("h k v -> k h v"), Sst[:, 0, :, :]).then_inc(on["state_out"], 16)
            sp.wait_ge(on["g_S"], TILES * HEADS)
            sp.dma_start(O["gdn_states"][1].rearrange("h k v -> k h v"), Sst[:, 1, :, :]).then_inc(on["state_out"], 16)
            sp.dma_start(O["s5_states"], hout[:]).then_inc(on["out"], 16)
            sp.dma_start(O["conv_tails"], rawtail[:]).then_inc(on["out"], 16)
            wo_loads(sp)
            ffn_loads(sp)
            sp.wait_ge(on["out"], 16 * (2 + TILES))

        @block.gpsimd
        def _(pool):
            n0 = masks(pool)
            pool.wait_ge(on["small"], 16 * len(SMALL))
            pool.wait_ge(on["halfpi"], 1)

            def reciprocal_std(s, rows, tile, used):
                pool.wait_ge(on["ln_mv"], alone(pool, count(tile + 1)))
                pool.wait_ge(on["x_norm"], alone(pool, count(used)))
                pool.tensor_scalar(rstd[0:rows, s, 0:1], stat[0:rows, s, 13:14], LN_EPS, None, ALU.add).then_inc(on["ln_r"], 1)
                pool.wait_ge(on["ln_r"], alone(pool, count(tile * 2 + 1)))
                pool.tensor_tensor(rstd[0:rows, s, 0:1], rstd[0:rows, s, 0:1], mhalf[0:rows, 0:1], ALU.pow).then_inc(on["ln_r"], 1)
                pool.wait_ge(on["ln_r"], alone(pool, count(tile * 2 + 2)))
                pool.tensor_scalar(rstd[0:rows, s, 1:2], stat[0:rows, s, 12:13], rstd[0:rows, s, 0:1], -1.0,
                                        ALU.mult, ALU.mult).then_inc(on["ln_rs"], 1)

            tables = s5_tables(pool, n0)
            next(tables)

            def ln_step(t, s):
                reciprocal_std(s, tile_rows(t), t, t - 1)
                if isinstance(t, int) and t == 1:
                    next(tables)

            ln_steps(pool, ln_step)
            pool.wait_ge(on["h_lo"], TILES)
            pool.wait_ge(on["mod_cols"], 4)
            for t in (urow, convrow, Mt, bas):
                pool.memset(t[:], 0.0).then_inc(on["cleared"], 1)
            pool.memset(rawrow[:, 0:GAP], 0.0).then_inc(on["cleared"], 1)
            n0, trigs = next(tables)
            assert s5_batch_tables(pool, 0, n0, 56, trigs) == 56
            with pool.Fori(1, NB5) as b:
                s5_batch_tables(pool, b, n0, 56, trigs)
            pool.wait_ge(on["glu_mix"], 12)
            pool.wait_ge(on["gates"], 1)
            pool.memset(Sst[:, 0, :, :], 0.0).then_inc(on["g_init"], 1)
            with pool.Fori(0, PTILES // 2) as i:
                for s in range(2):
                    gdn_pool(pool, i * 2 + s, s)
            gdn_pool(pool, PTILES, 0)
            wo_pool(pool)
            ffn_pool(pool)

        @block.tensor
        def _(pe):
            pe.wait_ge(on["c_silu"], 1)
            ada_mm(pe, 0)
            pe.wait_ge(on["masks"], 1)
            for c in range(1, 4):
                ada_mm(pe, c)
                ada_transpose(pe, c - 1)
            ada_transpose(pe, 3)
            pe.wait_ge(on["mod_cols"], 4)
            ln_steps(pe, lambda t, s: ln_transpose(pe, s, t + 1, t - 1, tile_rows(t)))
            for n in range(NU):
                in_block(pe, n % 2, n)
            pe.wait_ge(on["h_mod"], TILES)
            def batch(b):
                for j in range(4):
                    in_block(pe, j % 2, b * 4 + (NU + j))
                    if j == 0 and not isinstance(b, int):
                        s5_Y(pe, b - 1)
                    if j == 1:
                        s5_A(pe, b)
                    if j == 2:
                        s5_Z(pe, b)

            batch(0)
            with pe.Fori(1, NB5) as b:
                batch(b)
            gates_pe(pe)
            glu_pe(pe)
            pe.wait_ge(on["g_init"], 1)
            with pe.Fori(0, PTILES // 2) as i:
                for s in range(2):
                    gdn_pe(pe, i * 2 + s, s, i * 16 + 16, 0, (i * 2 + (4 + s), i * 32 + 64, i * 16), i * 2 + (4 + s))
            pe.wait_ge(on["s_state"], 16)
            gdn_pe(pe, PTILES, 0, 16 * (PTILES // 2 + 1), 1, None, 12)
            wo_pe(pe)
            ffn_pe(pe)

        @block.scalar
        def _(act):
            act.wait_ge(on["c_in"], 16)
            act.activation(csil[:], cT[:], ACT.Silu).then_inc(on["c_silu"], 1)
            act.wait_ge(on["small"], 16 * len(SMALL))
            act.activation(trig[:, 0, :], s5p[:, 2, :], ACT.Exp).then_inc(on["s5_exp_dt"], 1)
            act.wait_ge(on["s5_arg"], 1)
            act.activation(trig[:, 4, :], trig[:, 1, :], ACT.Exp).then_inc(on["s5_trig"], 1)
            act.wait_ge(on["s5_arg"], 2)
            act.activation(trig[:, 6, :], trig[:, 2, :], ACT.Sin).then_inc(on["s5_trig"], 1)
            act.activation(trig[:, 12, :], trig[:, 2, :], ACT.Abs).then_inc(on["s5_abs"], 1)
            act.wait_ge(on["s5_abs"], 1)
            act.activation(trig[:, 5, :], trig[:, 12, :], ACT.Sin, scale=-1.0, bias=trig[:, 13, 0:1]).then_inc(on["s5_trig"], 1)
            for t in range(2):
                ln_norm(act, t, t + 1, 0, P)
            for n in range(2):
                split_hi(act, n, 16)
            act.wait_ge(on["mod_ready"], 1)

            def ln_step(t, s):
                rows, nxt = tile_rows(t), tile_rows(t + 2) if isinstance(t, int) else P
                ln_mod(act, s, t + 1, t - 1, rows, 0 if rows == P else 1, 0, 0)
                if not isinstance(t, int) or t + 2 < TILES:
                    ln_norm(act, s, t + 3, t + 1, nxt)

            ln_steps(act, ln_step)
            act.wait_ge(on["cleared"], 5)

            def put_u(c, c0, cw):
                p0 = min(cw, SEQ - c0)
                ins = act.activation(urow[:, :, 1 + c0 // STEP:1 + (c0 + p0) // STEP].rearrange("p s n -> p n s"),
                                     ps[c][:, 0:p0].rearrange("p (n s) -> p n s", s=STEP), ACT.Copy)
                if p0 < cw:
                    ins = act.activation(urow[:, :, SAMP5 + 1:W5].rearrange("p s n -> p n s"),
                                         ps[c][:, p0:cw].rearrange("p (n s) -> p n s", s=STEP), ACT.Copy)
                return ins

            def put_row(row, first, func):
                def put(c, c0, cw):
                    p0 = min(cw, SEQ - c0)
                    ins = act.activation(row[:, first + c0:first + c0 + p0], ps[c][:, 0:p0], func)
                    if p0 < cw:
                        ins = act.activation(row[:, first + SAMP_COL:first + SAMP_COL + DEC_SEQ], ps[c][:, p0:cw], func)
                    return ins
                return put

            for n in range(NU):
                if n:
                    act.wait_ge(on["mm"], 3 * n)
                    split_hi(act, (n + 1) % 2, 16 * ((n + 1) // 2 + 1))
                if n:
                    act.wait_ge(on["u_stored"], count(16 * n))
                evac_chunks(n, put_u)
                act.wait_ge(on["in_evac"], count(3 * n + 3))
                act.dma_start(DR["u"][n * GB:(n + 1) * GB].rearrange("g j s w -> (g j) s w"), urow[:]).then_inc(on["u_stored"], 16)
            live = SEQ + GAP + DEC_SEQ
            def batch(b):
                for j in range(4):
                    n, sl = b * 4 + (NU + j), j % 2
                    act.wait_ge(on["mm"], count(n * 3))
                    split_hi(act, (j + 1) % 2, b * 32 + 16 * ((NU + j + 1) // 2 + 1))
                    if j == 2:
                        s5_evac_A(act, b)
                    if j < 3:
                        act.wait_ge(on["conv"], count(b * 3 + j))
                        act.activation(rawrow[:, GAP + SEQ:SAMP_COL + GAP], cache[:, bass.ds(b + 4 * j, 1), :].rearrange("p a c -> p (a c)"),
                                            ACT.Copy).then_inc(on["hist"], 1)
                        evac_chunks(n, put_row(rawrow, GAP, ACT.Copy))
                        act.wait_ge(on["hist"], count(b * 3 + (j + 1)))
                        act.wait_ge(on["in_evac"], count(n * 3 + 3))
                        act.wait_ge(on["wtap"], count(b * 3 + (j + 1)))
                        act.wait_ge(on["row_stored"][sl], count(b * 32 + 16 * (j // 2)))
                        act.activation(convrow[:, sl, 0:live], rawrow[:, 0:live], ACT.Copy, scale=wtap[:, sl, 0:1]).then_inc(on["tap0"], 1)
                        act.wait_ge(on["conv"], count(b * 3 + (j + 1)))
                        act.activation(convrow[:, sl, 0:live], convrow[:, sl, 0:live], ACT.Silu).then_inc(on["row_silu"], 1)
                        act.wait_ge(on["row_silu"], count(b * 3 + (j + 1)))
                    else:
                        act.wait_ge(on["row_stored"][sl], count(b * 32 + 16))
                        evac_chunks(n, put_row(convrow[:, sl, :], 0, ACT.Silu))
                        act.wait_ge(on["in_evac"], count(n * 3 + 3))
                    act.dma_start(DR["rows"][bass.ds(b + 4 * j, 1)].rearrange("a p w -> (a p) w"), convrow[:, sl, :]).then_inc(on["row_stored"][sl], 16)
                    if j == 0 and not isinstance(b, int):
                        s5_gelu(act, b - 1)

            batch(0)
            with act.Fori(1, NB5) as b:
                batch(b)
            gates_act(act)
            glu_act(act)
            act.wait_ge(on["glu_mix"], 12)
            act.wait_ge(on["gates"], 1)
            with act.Fori(0, PTILES // 2) as i:
                for s in range(2):
                    gdn_act(act, i * 2 + s, s, (i * 2 + (4 + s), i * 32 + 64, i * 16))
            gdn_act(act, PTILES, 0, None)
            wo_act(act)
            ffn_act(act)

        @block.vector
        def _(dve):
            dve.wait_ge(on["small"], 16 * len(SMALL))
            def mod_add(c):
                dve.wait_ge(on["ada_mm"], c + 1)
                dve.wait_ge(on["mod_T"], count(c - 1))
                dve.tensor_tensor(modrow[:, c % 2, :], ps[4 + c % 3][0:2, :], bada[:, c, :], ALU.add).then_inc(on["mod_row"], 1)

            def mod_keep(c):
                dve.wait_ge(on["mod_T"], c + 1)
                dve.tensor_copy(modc[:, c, :, :], ps[7][:, 0:8].rearrange("p (q t) -> p q t", t=2)).then_inc(on["mod_cols"], 1)

            def split_h(s, tile, rows, col):
                dve.wait_ge(on["h_mod"], count(tile + 1))
                dve.tensor_copy(hT_hi[:, :, col], hpre[:, s, :, 0:rows]).then_inc(on["h_hi"], 1)
                dve.wait_ge(on["h_hi"], count(tile + 1))
                dve.tensor_tensor(hT_lo[:, :, col], hpre[:, s, :, 0:rows], hT_hi[:, :, col].bitcast(F32), ALU.subtract).then_inc(on["h_lo"], 1)

            def stats(s, tile, loaded, done, rows):
                dve.wait_ge(on["x"][s], count(loaded))
                dve.wait_ge(on["ln_rs"], count(done))
                for h in range(2):
                    dve.bn_stats(stat[0:rows, s, 6 * h:6 * h + 6], xin[0:rows, s, h * 512:(h + 1) * 512]).then_inc(on["ln_bn"], 1)
                dve.wait_ge(on["ln_bn"], alone(dve, count(tile * 2 + 2)))
                dve.bn_aggr(stat[0:rows, s, 12:14], stat[0:rows, s, 0:12]).then_inc(on["ln_mv"], 1)

            mod_add(0)
            for t in range(2):
                stats(t, t, 16, 0, P)
            dve.wait_ge(on["s5_den"], 1)
            dve.reciprocal(trig[:, 9, :], trig[:, 14, :]).then_inc(on["s5_rden"], 1)
            for c in range(1, 4):
                mod_add(c)
                mod_keep(c - 1)
            mod_keep(3)
            dve.wait_ge(on["mod_cols"], 4)
            dve.tensor_scalar(onep[:, 0, :, :], modc[:, 2:4, :, :].rearrange("p a q t -> p (a q) t"), 1.0, None, ALU.add).then_inc(on["mod_ready"], 1)

            def ln_step(t, s):
                nxt = tile_rows(t + 2) if isinstance(t, int) else P
                if not isinstance(t, int) or t + 2 < TILES:
                    stats(s, t + 2, t * 8 + (32 - 8 * s), t + 1, nxt)
                split_h(s, t, tile_rows(t), tile_cols(t))

            for n in range(2):
                split_lo(dve, n, n + 1)
            ln_steps(dve, ln_step)
            for n in range(NU):
                if n:
                    split_lo(dve, (n + 1) % 2, n + 2)
            live = SEQ + GAP + DEC_SEQ
            def batch(b):
                for j in range(4):
                    n, sl = b * 4 + (NU + j), j % 2
                    split_lo(dve, (j + 1) % 2, n + 2)
                    if j < 3:
                        row = b * 3 + j
                        dve.wait_ge(on["tap0"], count(row))
                        dve.tensor_copy(wtap[:, sl, :], convw[:, bass.ds(b + 4 * j, 1), :].rearrange("p a c -> p (a c)")).then_inc(on["wtap"], 1)
                        dve.wait_ge(on["in_evac"], count(n * 3 + 3))
                        dve.tensor_copy(rawtail[:, bass.ds(b + 4 * j, 1), 0, :].rearrange("p a c -> p (a c)"), rawrow[:, SEQ:SEQ + GAP]).then_inc(on["tail"], 1)
                        dve.tensor_copy(rawtail[:, bass.ds(b + 4 * j, 1), 1, :].rearrange("p a c -> p (a c)"), rawrow[:, RAWW - GAP:RAWW]).then_inc(on["tail"], 1)
                        dve.wait_ge(on["hist"], count(row + 1))
                        dve.wait_ge(on["tap0"], count(row + 1))
                        dve.wait_ge(on["wtap"], count(row + 1))
                        dve.wait_ge(on["tail"], count(row * 2 + 2))
                        if j == 2:
                            s5_scan_first(dve, b)
                        for tap in range(1, CONVW):
                            ins = dve.scalar_tensor_tensor(out=convrow[:, sl, 0:live], in0=rawrow[:, tap:tap + live],
                                                           scalar=wtap[:, sl, tap:tap + 1], in1=convrow[:, sl, 0:live],
                                                           op0=ALU.mult, op1=ALU.add)
                            if tap < CONVW - 1:
                                ins.then_inc(on["tap"], 1)
                                dve.wait_ge(on["tap"], count(row * 2 + tap))
                            else:
                                ins.then_inc(on["conv"], 1)
                    else:
                        s5_scan(dve, b)
                    if j == 0 and not isinstance(b, int):
                        s5_out(dve, b - 1)

            batch(0)
            with dve.Fori(1, NB5) as b:
                batch(b)
            s5_out(dve, NB5 - 1)
            gates_dve(dve)
            glu_dve(dve)
            dve.wait_ge(on["g_init"], 1)
            with dve.Fori(0, PTILES // 2) as i:
                for s in range(2):
                    gdn_dve(dve, i * 2 + s, s, 0, bass.ds(i * 2 * P + s * P, P), P, (i * 2 + (4 + s), i * 32 + 64, i * 16))
            dve.wait_ge(on["s_state"], 16)
            gdn_dve(dve, PTILES, 0, 1, SEQ, DEC_SEQ, None)
            wo_dve(dve)
            ffn_dve(dve)


def kernel(**a):
    import numpy as np
    import concourse.bacc as bacc
    from concourse.bass_utils import run_bass_kernel_spmd

    f = np.ascontiguousarray
    both = lambda x: np.concatenate([x, x], 0)
    pg = lambda x: x[0].T
    pgj = lambda x: x[0].transpose(1, 0, 2)
    gjp = lambda x: x[0].transpose(2, 0, 1)
    c = np.concatenate([a["c_prompt"], a["c_sample"]], 0)
    bre, bim, cre, cim = pgj(a["s5_b_re"]), pgj(a["s5_b_im"]), gjp(a["s5_c_re"]), gjp(a["s5_c_im"])
    arrays = {
        "cT": f(c.reshape(2, KD, P).transpose(2, 1, 0)),
        "s5p": f(np.stack([both(pg(a["s5_a_re"])), both(pg(a["s5_a_im"])),
                           np.broadcast_to(a["s5_log_dt"][0], (P, S5_G))], 1)),
        "s5d": f(np.tile(a["s5_d"][0].reshape(S5_G, S5_J).T, (STEP, 1))),
        "s5h0": f(np.concatenate([pg(a["state_s5_re"][0]), pg(a["state_s5_im"][0])], 0)),
        "s5bc": f(np.stack([np.concatenate(x, 0) for x in ((bre, bim), (bim, bre), (cre, cim), (cim, cre))], 1)),
        "convw": f(a["gdn_conv_w"][0].reshape(CONVW, 12, P).transpose(2, 1, 0)),
        "cache": f(a["cache_gdn_conv"][0, 0].reshape(GAP, 12, P).transpose(2, 1, 0)),
        "balog": f(np.broadcast_to(np.stack([a["gdn_a_log"][0], a["gdn_dt_bias"][0]]), (P, 2, HEADS))),
        "normg": f(a["gdn_norm_g"][0][:, None]),
        "x_prompt": f(a["x_prompt"][0]), "x_sample": f(a["x_sample"][0]),
        "w_ada": f(a["w_ada"][0]), "b_ada": f(np.broadcast_to(a["b_ada"][0], (2, 6 * D_MODEL))),
        "w_in": f(a["w_in"][0]), "w_glu": f(a["w_s5_glu"][0]), "w_out": f(a["w_out"][0]),
        "w_up": f(a["w_ffn_up"][0]), "w_down": f(a["w_ffn_down"][0]), "state_gdn": f(a["state_gdn"][0, 0]),
        "ln_rows": f(np.stack([a["ln1_g"][0], a["ln1_b"][0], a["ln2_g"][0], a["ln2_b"][0]])),
    }
    nc = bacc.Bacc("TRN2", target_bir_lowering=False, num_devices=1)
    I = {k: nc.dram_tensor(k, v.shape, F32, kind="ExternalInput").ap() for k, v in arrays.items()}
    outs = {"y_prompt": (SEQ, D_MODEL), "y_sample": (DEC_SEQ, D_MODEL), "s5_states": (P, S5_G, 2),
            "gdn_states": (2, HEADS, HD, HD), "conv_tails": (P, 12, 2, GAP)}
    O = {k: nc.dram_tensor(k, v, F32, kind="ExternalOutput").ap() for k, v in outs.items()}
    DR = {k: nc.dram_tensor(k, v, F32, kind="Internal").ap() for k, v in {
        "u": (S5_G, S5_J, STEP, W5), "y": (S5_G, S5_J, STEP, W5), "rows": (16, P, ROWW),
        "mod": (2, 6 * D_MODEL), "x1": (TOK, D_MODEL)}.items()}
    stream_step(nc, I, O, DR)
    r = run_bass_kernel_spmd(nc, [arrays], core_ids=[0]).results[0]
    s5 = r["s5_states"].transpose(2, 1, 0)
    conv = r["conv_tails"].transpose(2, 3, 1, 0).reshape(2, GAP, 3 * 4 * HD)
    gdn = r["gdn_states"]
    return (r["y_prompt"][None], r["y_sample"][None],
            f(s5[0:1, :, 0:S5_P])[None], f(s5[0:1, :, S5_P:])[None], f(gdn[0:1])[None], f(conv[0:1])[None],
            f(s5[1:2, :, 0:S5_P])[None], f(s5[1:2, :, S5_P:])[None], f(gdn[1:2])[None], f(conv[1:2])[None])
```
